# Optimizing a Trainium2 kernel written in Bass

```python
import jax
import jax.numpy as jnp
from jax import lax
import numpy as np
import jax, jax.numpy as jnp

D_MODEL = 1024
BATCH = 1
SEQ = 256
DEPTH = 2

GRID_W = 64
CTX_LEN = 256
N_EVEN = (DEPTH + 1) // 2
N_ODD = DEPTH // 2

HEAD_DIM = 64
ATTN_HEADS = (D_MODEL // 2) // HEAD_DIM
ATTN_KV_HEADS = ATTN_HEADS // 4
ATTN_GROUP = ATTN_HEADS // ATTN_KV_HEADS
WINDOW = 128
ATTN_BLOCK = 128
ROPE_BASE = 10000.0

HGRN_EXPAND = 128
HGRN_WIDTH = D_MODEL // 2
HGRN_HEADS = HGRN_WIDTH // HGRN_EXPAND
HGRN_DK = HGRN_EXPAND
HGRN_DV = HGRN_EXPAND
CHUNK = 64

RET_HEADS = 4
RET_DK = D_MODEL // RET_HEADS
RET_DV = 2 * RET_DK
RET_BASE = 10000.0

FFN_HIDDEN = -(-8 * D_MODEL // (3 * 256)) * 256

A_Q = ATTN_HEADS * HEAD_DIM
A_KV = ATTN_KV_HEADS * HEAD_DIM
EVEN_PARTS = (('a_q', A_Q), ('a_k', A_KV), ('a_v', A_KV), ('b_q', HGRN_WIDTH), ('b_ff', HGRN_WIDTH),
              ('b_fb', HGRN_WIDTH), ('b_i', HGRN_WIDTH), ('b_g', HGRN_WIDTH))
EVEN_IN = A_Q + 2 * A_KV + 5 * HGRN_WIDTH
EVEN_OUT = A_Q + HGRN_HEADS * HGRN_DV
ODD_PARTS = (('q', RET_HEADS * RET_DK), ('k', RET_HEADS * RET_DK), ('v', RET_HEADS * RET_DV),
             ('g', RET_HEADS * RET_DV))
ODD_IN = 2 * RET_HEADS * RET_DK + 2 * RET_HEADS * RET_DV
ODD_OUT = RET_HEADS * RET_DV
EPS = 1e-6
F32 = jnp.float32


def _offsets(parts):
    out, start = {}, 0
    for name, width in parts:
        out[name] = (start, start + width)
        start += width
    return out

def split_parts(u, parts):
    return {n: u[..., s:e] for n, (s, e) in _offsets(parts).items()}

def project_parts(h, w, parts, names):
    off = _offsets(parts)
    return {n: h @ w[:, off[n][0]:off[n][1]] for n in names}

def rms_norm(x, g=None):
    xf = x.astype(F32)
    y = xf * lax.rsqrt(jnp.mean(xf * xf, axis=-1, keepdims=True) + EPS)
    if g is not None:
        y = y * g.astype(F32)
    return y.astype(x.dtype)

def modulate(h, shift, scale):
    return h * (1.0 + scale) + shift

def to_heads(u, n_heads):
    b, l, _ = u.shape
    return u.reshape(b, l, n_heads, -1).transpose(0, 2, 1, 3)

def from_heads(o):
    return o.transpose(0, 2, 1, 3)

def flip(a):
    return jnp.flip(a, axis=2)

def axial_rope_tables(n_tok):
    t = jnp.arange(n_tok)
    row = (t // GRID_W).astype(F32)
    col = (t % GRID_W).astype(F32)
    n_freq = HEAD_DIM // 4
    inv = ROPE_BASE ** (-jnp.arange(n_freq, dtype=F32) / n_freq)
    ang = jnp.concatenate([row[:, None] * inv, col[:, None] * inv], axis=-1)
    return jnp.cos(ang), jnp.sin(ang)

def retention_rope_tables(n_tok):
    theta = 1.0 / (RET_BASE ** jnp.linspace(0.0, 1.0, RET_DK // 2, dtype=F32))
    ang = jnp.arange(n_tok, dtype=F32)[:, None] * theta
    return jnp.cos(ang), jnp.sin(ang)

def apply_rope(x, cos, sin):
    half = x.shape[-1] // 2
    xf = x.astype(F32)
    x1, x2 = xf[..., :half], xf[..., half:]
    return jnp.concatenate([x1 * cos - x2 * sin, x2 * cos + x1 * sin], axis=-1).astype(x.dtype)

def attn_q_heads(u, g):
    b, l, _ = u.shape
    q = rms_norm(u.reshape(b, l, ATTN_KV_HEADS, ATTN_GROUP, HEAD_DIM), g)
    return q.transpose(0, 2, 3, 1, 4)

def kv_heads(u, g=None):
    b, l, _ = u.shape
    h = u.reshape(b, l, ATTN_KV_HEADS, HEAD_DIM)
    if g is not None:
        h = rms_norm(h, g)
    return h.transpose(0, 2, 1, 3)

def window_attention(q, k, v, k_ctx, v_ctx, sink):
    b, kv, g, l, d = q.shape
    n_blocks = l // ATTN_BLOCK
    span = ATTN_BLOCK + 2 * WINDOW
    pad = ((0, 0), (0, 0), (WINDOW, WINDOW), (0, 0))
    kp, vp = jnp.pad(k, pad), jnp.pad(v, pad)
    scale = d ** -0.5
    sink_col = jnp.broadcast_to(sink[None, :, :, None, None], (b, kv, g, ATTN_BLOCK, 1))

    def block(i):
        start = i * ATTN_BLOCK
        qb = lax.dynamic_slice_in_dim(q, start, ATTN_BLOCK, axis=3)
        kb = lax.dynamic_slice_in_dim(kp, start, span, axis=2)
        vb = lax.dynamic_slice_in_dim(vp, start, span, axis=2)
        q_pos = start + jnp.arange(ATTN_BLOCK)
        k_pos = start - WINDOW + jnp.arange(span)
        valid = ((jnp.abs(k_pos[None, :] - q_pos[:, None]) <= WINDOW)
                 & (k_pos >= 0)[None, :] & (k_pos < l)[None, :])
        s_lat = jnp.einsum('bkgqd,bksd->bkgqs', qb, kb, preferred_element_type=F32) * scale
        s_lat = jnp.where(valid, s_lat, -jnp.inf)
        s_ctx = jnp.einsum('bkgqd,bkcd->bkgqc', qb, k_ctx, preferred_element_type=F32) * scale
        p = jax.nn.softmax(jnp.concatenate([sink_col, s_lat, s_ctx], axis=-1), axis=-1)
        p_lat = p[..., 1:1 + span].astype(v.dtype)
        p_ctx = p[..., 1 + span:].astype(v.dtype)
        return (jnp.einsum('bkgqs,bksd->bkgqd', p_lat, vb)
                + jnp.einsum('bkgqc,bkcd->bkgqd', p_ctx, v_ctx))

    o = lax.map(block, jnp.arange(n_blocks))
    return o.transpose(1, 0, 4, 2, 3, 5).reshape(b, l, kv * g * d)

def context_attention(q, k, v, sink):
    b, kv, g, lc, d = q.shape
    s = jnp.einsum('bkgqd,bkcd->bkgqc', q, k, preferred_element_type=F32) * d ** -0.5
    sink_col = jnp.broadcast_to(sink[None, :, :, None, None], (b, kv, g, lc, 1))
    p = jax.nn.softmax(jnp.concatenate([sink_col, s], axis=-1), axis=-1)[..., 1:].astype(v.dtype)
    o = jnp.einsum('bkgqc,bkcd->bkgqd', p, v)
    return o.transpose(0, 3, 1, 2, 4).reshape(b, lc, kv * g * d)

def chunk_scan(q_in, k_in, v, decay, s0):
    xs = (jnp.moveaxis(q_in, 2, 0), jnp.moveaxis(k_in, 2, 0), jnp.moveaxis(v, 2, 0), decay)

    def step(s, inp):
        q_n, k_n, v_n, a_n = inp
        o_n = jnp.einsum('bhcd,bhde->bhce', q_n, s)
        s = a_n * s + jnp.einsum('bhcd,bhce->bhde', k_n, v_n)
        return s, o_n

    s, o = lax.scan(step, s0, xs)
    return jnp.moveaxis(o, 0, 2), s

def gla_chunked(q, k, v, log_f, s0):
    b, h, l, dk = q.shape
    dv = v.shape[-1]
    n = l // CHUNK
    qc, kc, lc = (a.reshape(b, h, n, CHUNK, dk) for a in (q, k, log_f))
    vc = v.reshape(b, h, n, CHUNK, dv)
    cum = jnp.cumsum(lc, axis=3)
    ref = cum[:, :, :, CHUNK // 2:CHUNK // 2 + 1]
    scores = jnp.einsum('bhntd,bhnsd->bhnts', qc * jnp.exp(cum - ref), kc * jnp.exp(ref - cum))
    lower = jnp.tril(jnp.ones((CHUNK, CHUNK), dtype=bool))
    o_intra = jnp.einsum('bhnts,bhnse->bhnte', jnp.where(lower, scores, 0.0), vc)
    cum_last = cum[:, :, :, -1:]
    decay = jnp.moveaxis(jnp.exp(cum_last[:, :, :, 0]), 2, 0)[..., None]
    o_inter, s = chunk_scan(qc * jnp.exp(cum), kc * jnp.exp(cum_last - cum), vc, decay, s0)
    return (o_intra + o_inter).reshape(b, h, l, dv), s

def gla_final_state(k, v, log_f):
    cum = jnp.cumsum(log_f, axis=2)
    return jnp.einsum('bhld,bhle->bhde', k * jnp.exp(cum[:, :, -1:] - cum), v)

def retention_chunked(q, k, v, log_gamma, s0):
    b, h, l, dk = q.shape
    dv = v.shape[-1]
    n = l // CHUNK
    qc = q.reshape(b, h, n, CHUNK, dk)
    kc = k.reshape(b, h, n, CHUNK, dk)
    vc = v.reshape(b, h, n, CHUNK, dv)
    pos = jnp.arange(CHUNK, dtype=F32)
    rel = pos[:, None] - pos[None, :]
    dmat = jnp.where(rel >= 0, jnp.exp(log_gamma[:, None, None] * jnp.maximum(rel, 0.0)), 0.0)
    scores = jnp.einsum('bhntd,bhnsd->bhnts', qc, kc) * dmat[None, :, None]
    o_intra = jnp.einsum('bhnts,bhnse->bhnte', scores, vc)
    lg = log_gamma[:, None]
    q_in = qc * jnp.exp(lg * (pos + 1.0))[None, :, None, :, None]
    k_in = kc * jnp.exp(lg * (CHUNK - 1.0 - pos))[None, :, None, :, None]
    decay = jnp.broadcast_to(jnp.exp(log_gamma * CHUNK)[None, None, :, None, None], (n, 1, h, 1, 1))
    o_inter, s = chunk_scan(q_in, k_in, vc, decay, s0)
    return (o_intra + o_inter).reshape(b, h, l, dv), s

def retention_final_state(k, v, log_gamma):
    lc = k.shape[2]
    w = jnp.exp(log_gamma[:, None] * (lc - 1.0 - jnp.arange(lc, dtype=F32)))
    return jnp.einsum('bhld,bhle->bhde', k * w[None, :, :, None], v)

def gated_head_norm(o, g_raw, gain=None):
    b, h, l, dv = o.shape
    y = rms_norm(from_heads(o), gain) * jax.nn.silu(g_raw.reshape(b, l, h, dv).astype(F32))
    return y.reshape(b, l, h * dv)

def even_mixer(h_ctx, h_lat, w_in, w_out, qk_g, sink, out_g, lb, cos, sin, need_ctx):
    dt = h_lat.dtype
    n_b = h_ctx.shape[0]
    sink = sink.astype(F32).reshape(ATTN_KV_HEADS, ATTN_GROUP)
    lb = lb.reshape(HGRN_HEADS, 1, HGRN_DK)
    p = split_parts(h_lat @ w_in, EVEN_PARTS)
    names = [n for n, _ in EVEN_PARTS] if need_ctx else ['a_k', 'a_v', 'b_ff', 'b_fb', 'b_i']
    pc = project_parts(h_ctx, w_in, EVEN_PARTS, names)

    def gates(f_raw):
        f = lb + (1.0 - lb) * jax.nn.sigmoid(to_heads(f_raw, HGRN_HEADS).astype(F32))
        return 1.0 - f, jnp.log(f)

    k_ctx = kv_heads(pc['a_k'], qk_g[1])
    v_ctx = kv_heads(pc['a_v'])
    q_lat = apply_rope(attn_q_heads(p['a_q'], qk_g[0]), cos, sin)
    k_lat = apply_rope(kv_heads(p['a_k'], qk_g[1]), cos, sin)
    a_lat = window_attention(q_lat, k_lat, kv_heads(p['a_v']), k_ctx, v_ctx, sink)

    k_fw_c, lf_fw_c = gates(pc['b_ff'])
    k_bw_c, lf_bw_c = gates(pc['b_fb'])
    i_c = to_heads(pc['b_i'], HGRN_HEADS).astype(F32)
    if need_ctx:
        zeros = jnp.zeros((n_b, HGRN_HEADS, HGRN_DK, HGRN_DV), F32)
        q_c = jax.nn.silu(to_heads(pc['b_q'], HGRN_HEADS).astype(F32))
        o_fw_c, s_fw = gla_chunked(q_c, k_fw_c, i_c, lf_fw_c, zeros)
        o_bw_c, s_bw = gla_chunked(flip(q_c), flip(k_bw_c), flip(i_c), flip(lf_bw_c), zeros)
    else:
        s_fw = gla_final_state(k_fw_c, i_c, lf_fw_c)
        s_bw = gla_final_state(flip(k_bw_c), flip(i_c), flip(lf_bw_c))
    k_fw, lf_fw = gates(p['b_ff'])
    k_bw, lf_bw = gates(p['b_fb'])
    q_l = jax.nn.silu(to_heads(p['b_q'], HGRN_HEADS).astype(F32))
    i_l = to_heads(p['b_i'], HGRN_HEADS).astype(F32)
    o_fw, _ = gla_chunked(q_l, k_fw, i_l, lf_fw, s_fw)
    o_bw, _ = gla_chunked(flip(q_l), flip(k_bw), flip(i_l), flip(lf_bw), s_bw)
    b_lat = gated_head_norm(o_fw + flip(o_bw), p['b_g'], out_g)

    y_lat = jnp.concatenate([a_lat.astype(dt), b_lat.astype(dt)], axis=-1) @ w_out
    if not need_ctx:
        return None, y_lat
    a_ctx = context_attention(attn_q_heads(pc['a_q'], qk_g[0]), k_ctx, v_ctx, sink)
    b_ctx = gated_head_norm(o_fw_c + flip(o_bw_c), pc['b_g'], out_g)
    y_ctx = jnp.concatenate([a_ctx.astype(dt), b_ctx.astype(dt)], axis=-1) @ w_out
    return y_ctx, y_lat

def odd_mixer(h_ctx, h_lat, w_in, w_out, cos, sin, need_ctx):
    dt = h_lat.dtype
    n_b = h_ctx.shape[0]
    log_g_fw = jnp.log(1.0 - 2.0 ** (-5.0 - jnp.arange(RET_HEADS, dtype=F32)))
    log_g_bw = log_g_fw[::-1]
    k_scale = RET_DK ** -0.5
    p = split_parts(h_lat @ w_in, ODD_PARTS)
    names = [n for n, _ in ODD_PARTS] if need_ctx else ['k', 'v']
    pc = project_parts(h_ctx, w_in, ODD_PARTS, names)

    k_c = to_heads(pc['k'], RET_HEADS).astype(F32) * k_scale
    v_c = to_heads(pc['v'], RET_HEADS).astype(F32)
    if need_ctx:
        zeros = jnp.zeros((n_b, RET_HEADS, RET_DK, RET_DV), F32)
        q_c = to_heads(pc['q'], RET_HEADS).astype(F32)
        o_fw_c, s_fw = retention_chunked(q_c, k_c, v_c, log_g_fw, zeros)
        o_bw_c, s_bw = retention_chunked(flip(q_c), flip(k_c), flip(v_c), log_g_bw, zeros)
    else:
        s_fw = retention_final_state(k_c, v_c, log_g_fw)
        s_bw = retention_final_state(flip(k_c), flip(v_c), log_g_bw)

    q_l = apply_rope(to_heads(p['q'], RET_HEADS).astype(F32), cos, sin)
    k_l = apply_rope(to_heads(p['k'], RET_HEADS).astype(F32), cos, sin) * k_scale
    v_l = to_heads(p['v'], RET_HEADS).astype(F32)
    o_fw, _ = retention_chunked(q_l, k_l, v_l, log_g_fw, s_fw)
    o_bw, _ = retention_chunked(flip(q_l), flip(k_l), flip(v_l), log_g_bw, s_bw)
    y_lat = gated_head_norm(o_fw + flip(o_bw), p['g']).astype(dt) @ w_out
    if not need_ctx:
        return None, y_lat
    y_ctx = gated_head_norm(o_fw_c + flip(o_bw_c), pc['g']).astype(dt) @ w_out
    return y_ctx, y_lat

def swiglu(h, w_in, w_out):
    gate, up = jnp.split(h @ w_in, 2, axis=-1)
    return (jax.nn.silu(gate) * up) @ w_out

def first_inputs(seed: int = 0) -> dict:
    key = jax.random.key(seed)
    ks = jax.random.split(key, 17)
    d = D_MODEL

    def nrm(k, shape, scale):
        return jax.random.normal(k, shape, F32) * scale

    return {
        'x': nrm(ks[0], (BATCH, SEQ, d), 1.0),
        'c': nrm(ks[1], (BATCH, d), 1.0),
        'ctx': nrm(ks[2], (BATCH, CTX_LEN, d), 1.0),
        'c_ctx': nrm(ks[3], (d,), 1.0),
        'mod_w': nrm(ks[4], (DEPTH, d, 6 * d), 0.5 * d ** -0.5),
        'mod_b': nrm(ks[5], (DEPTH, 6 * d), 0.02),
        'norm_g': 1.0 + nrm(ks[6], (DEPTH, 2, d), 0.02),
        'ffn_w_in': nrm(ks[7], (DEPTH, d, 2 * FFN_HIDDEN), d ** -0.5),
        'ffn_w_out': nrm(ks[8], (DEPTH, FFN_HIDDEN, d), FFN_HIDDEN ** -0.5),
        'even_w_in': nrm(ks[9], (N_EVEN, d, EVEN_IN), d ** -0.5),
        'even_w_out': nrm(ks[10], (N_EVEN, EVEN_OUT, d), EVEN_OUT ** -0.5),
        'attn_qk_norm_g': 1.0 + nrm(ks[11], (N_EVEN, 2, HEAD_DIM), 0.02),
        'attn_sink': nrm(ks[12], (N_EVEN, ATTN_HEADS), 0.5),
        'hgrn_out_norm_g': 1.0 + nrm(ks[13], (N_EVEN, HGRN_DV), 0.02),
        'hgrn_lb': nrm(ks[14], (N_EVEN + 1, HGRN_WIDTH), 0.1),
        'odd_w_in': nrm(ks[15], (N_ODD, d, ODD_IN), d ** -0.5),
        'odd_w_out': nrm(ks[16], (N_ODD, ODD_OUT, d), ODD_OUT ** -0.5),
    }

def first_block(x, c, ctx, c_ctx, mod_w, mod_b, norm_g, ffn_w_in, ffn_w_out, even_w_in, even_w_out,
              attn_qk_norm_g, attn_sink, hgrn_out_norm_g, hgrn_lb, odd_w_in, odd_w_out):
    n_tok = x.shape[1]
    rope_cos, rope_sin = axial_rope_tables(n_tok)
    ret_cos, ret_sin = retention_rope_tables(n_tok)
    lower_bounds = jnp.cumsum(jax.nn.softmax(hgrn_lb.astype(F32), axis=0), axis=0)
    cond_lat = jax.nn.silu(c)
    cond_ctx = jax.nn.silu(c_ctx)
    for layer in range(DEPTH):
        last = layer == DEPTH - 1
        j = layer // 2
        m_lat = jnp.split((cond_lat @ mod_w[layer] + mod_b[layer])[:, None, :], 6, axis=-1)
        m_ctx = jnp.split((cond_ctx @ mod_w[layer] + mod_b[layer])[None, None, :], 6, axis=-1)
        h_lat = modulate(rms_norm(x, norm_g[layer, 0]), m_lat[0], m_lat[1])
        h_ctx = modulate(rms_norm(ctx, norm_g[layer, 0]), m_ctx[0], m_ctx[1])
        if layer % 2 == 0:
            y_ctx, y_lat = even_mixer(h_ctx, h_lat, even_w_in[j], even_w_out[j], attn_qk_norm_g[j],
                                      attn_sink[j], hgrn_out_norm_g[j], lower_bounds[j],
                                      rope_cos, rope_sin, not last)
        else:
            y_ctx, y_lat = odd_mixer(h_ctx, h_lat, odd_w_in[j], odd_w_out[j], ret_cos, ret_sin, not last)
        x = x + m_lat[2] * y_lat
        x = x + m_lat[5] * swiglu(modulate(rms_norm(x, norm_g[layer, 1]), m_lat[3], m_lat[4]),
                                  ffn_w_in[layer], ffn_w_out[layer])
        if not last:
            ctx = ctx + m_ctx[2] * y_ctx
            ctx = ctx + m_ctx[5] * swiglu(modulate(rms_norm(ctx, norm_g[layer, 1]), m_ctx[3], m_ctx[4]),
                                          ffn_w_in[layer], ffn_w_out[layer])
    return x


DN_HEADS = 8
DN_HEAD_DIM = 128
DN_WIDTH = DN_HEADS * DN_HEAD_DIM
DN_CONV = 4
DN_CHUNK = 64
SWA_Q_HEADS = 16
SWA_KV_HEADS = 2
SWA_HEAD_DIM = 64
SWA_GROUP = SWA_Q_HEADS // SWA_KV_HEADS
SWA_WIDTH = SWA_Q_HEADS * SWA_HEAD_DIM
SWA_KV_WIDTH = SWA_KV_HEADS * SWA_HEAD_DIM
SWA_BLOCK = 128
ROPE_THETA = 500000.0
ROPE_DIM = SWA_HEAD_DIM // 4
D_FF = 2816
FFN_CONV = 3
IN_SIZES = (3 * DN_WIDTH, DN_WIDTH, DN_HEADS, DN_HEADS, SWA_WIDTH, SWA_KV_WIDTH, SWA_KV_WIDTH, D_MODEL, D_MODEL)
IN_TOTAL = 4 * DN_WIDTH + 2 * DN_HEADS + SWA_WIDTH + 2 * SWA_KV_WIDTH + 2 * D_MODEL


def _split_columns(t, sizes):
    idx, acc = [], 0
    for s in sizes[:-1]:
        acc += s
        idx.append(acc)
    return jnp.split(t, idx, axis=-1)

def rms_norm_2(x, w):
    xf = x.astype(jnp.float32)
    y = xf * lax.rsqrt(jnp.mean(xf * xf, axis=-1, keepdims=True) + EPS)
    return (y * w.astype(jnp.float32)).astype(x.dtype)

def l2_norm(x):
    xf = x.astype(jnp.float32)
    return (xf * lax.rsqrt(jnp.sum(xf * xf, axis=-1, keepdims=True) + EPS)).astype(x.dtype)

def causal_dwconv(x, w):
    K, C = w.shape
    return lax.conv_general_dilated(
        x, w[:, None, :].astype(x.dtype), window_strides=(1,), padding=[(K - 1, 0)],
        dimension_numbers=('NWC', 'WIO', 'NWC'), feature_group_count=C)

def partial_rope(x, pos):
    half = ROPE_DIM // 2
    inv = jnp.power(ROPE_THETA, -jnp.arange(half, dtype=jnp.float32) / half)
    ang = pos.astype(jnp.float32)[..., None] * inv
    cos, sin = jnp.cos(ang)[:, :, None, :], jnp.sin(ang)[:, :, None, :]
    xr = x[..., :ROPE_DIM].astype(jnp.float32)
    x1, x2 = xr[..., :half], xr[..., half:]
    rot = jnp.concatenate([x1 * cos - x2 * sin, x2 * cos + x1 * sin], axis=-1).astype(x.dtype)
    return jnp.concatenate([rot, x[..., ROPE_DIM:]], axis=-1)

def gated_delta_rule_chunked(q, k, v, g, beta):
    B, T, H, Dk = q.shape
    Dv = v.shape[-1]
    C = DN_CHUNK
    N = T // C
    f32 = jnp.float32

    def chunks(t):
        return t.astype(f32).reshape(B, N, C, H, -1).transpose(0, 3, 1, 2, 4)

    qc = chunks(q) * (Dk ** -0.5)
    kc, vc = chunks(k), chunks(v)
    gc = jnp.cumsum(g.astype(f32).reshape(B, N, C, H).transpose(0, 3, 1, 2), axis=-1)
    bc = beta.astype(f32).reshape(B, N, C, H).transpose(0, 3, 1, 2)
    tri_incl = jnp.tril(jnp.ones((C, C), dtype=bool))
    tri_strict = jnp.tril(jnp.ones((C, C), dtype=bool), -1)
    decay = jnp.exp(jnp.where(tri_incl, gc[..., :, None] - gc[..., None, :], -jnp.inf))
    k_beta = kc * bc[..., None]
    L = jnp.where(tri_strict, jnp.einsum('bhnid,bhnjd->bhnij', k_beta, kc) * decay, 0.0)
    A = L + jnp.eye(C, dtype=f32)
    rhs = jnp.concatenate([vc * bc[..., None], k_beta * jnp.exp(gc)[..., None]], axis=-1)
    sol = lax.linalg.triangular_solve(A, rhs, left_side=True, lower=True, unit_diagonal=True)
    u, w = sol[..., :Dv], sol[..., Dv:]
    qk = jnp.einsum('bhnid,bhnjd->bhnij', qc, kc) * decay
    q_dec = qc * jnp.exp(gc)[..., None]
    g_last = gc[..., -1]
    k_dec = kc * jnp.exp(g_last[..., None] - gc)[..., None]

    def step(S, xs):
        qd, kd, u_i, w_i, qk_i, gl = xs
        v_new = u_i - jnp.einsum('bhcd,bhde->bhce', w_i, S)
        o = jnp.einsum('bhcd,bhde->bhce', qd, S) + jnp.einsum('bhij,bhje->bhie', qk_i, v_new)
        S = S * jnp.exp(gl)[..., None, None] + jnp.einsum('bhcd,bhce->bhde', kd, v_new)
        return S, o

    xs = tuple(jnp.moveaxis(t, 2, 0) for t in (q_dec, k_dec, u, w, qk, g_last))
    S0 = jnp.zeros((B, H, Dk, Dv), f32)
    _, o = lax.scan(step, S0, xs)
    return o.transpose(1, 0, 3, 2, 4).reshape(B, T, H, Dv).astype(v.dtype)

def swa_sink_attention(q, k, v, sinks):
    B, T, Hq, D = q.shape
    nb = T // SWA_BLOCK
    f32 = jnp.float32
    qb = q.astype(f32).reshape(B, nb, SWA_BLOCK, SWA_KV_HEADS, SWA_GROUP, D)

    def band(t):
        tb = t.astype(f32).reshape(B, nb, SWA_BLOCK, SWA_KV_HEADS, D)
        prev = jnp.pad(tb, ((0, 0), (1, 0), (0, 0), (0, 0), (0, 0)))[:, :-1]
        return jnp.concatenate([prev, tb], axis=2)

    kb, vb = band(k), band(v)
    s = jnp.einsum('bnqhgd,bnkhd->bnhgqk', qb, kb) * (D ** -0.5)
    qi = jnp.arange(SWA_BLOCK)[:, None]
    kj = jnp.arange(2 * SWA_BLOCK)[None, :]
    rel = qi + SWA_BLOCK - kj
    blk = jnp.arange(nb)[:, None, None]
    mask = (rel >= 0) & (rel < WINDOW) & (blk * SWA_BLOCK + kj >= SWA_BLOCK)
    s = jnp.where(mask[None, :, None, None], s, -jnp.inf)
    sink = sinks.astype(f32).reshape(1, 1, SWA_KV_HEADS, SWA_GROUP, 1, 1)
    m = jnp.maximum(jnp.max(s, axis=-1, keepdims=True), sink)
    p = jnp.exp(s - m)
    denom = jnp.sum(p, axis=-1, keepdims=True) + jnp.exp(sink - m)
    o = jnp.einsum('bnhgqk,bnkhd->bnqhgd', p / denom, vb)
    return o.reshape(B, T, Hq * D).astype(q.dtype)

def second_inputs(seed: int = 0) -> dict:
    key = jax.random.key(seed)
    ks = jax.random.split(key, 24)
    nrm = jax.random.normal
    f32 = jnp.float32
    Lr = DEPTH
    x = nrm(ks[0], (BATCH, SEQ, D_MODEL), f32)
    c = nrm(ks[1], (BATCH, D_MODEL), f32)
    positions = (jax.random.randint(ks[2], (BATCH, 1), 0, 2048, dtype=jnp.int32)
                 + jnp.arange(SEQ, dtype=jnp.int32)[None, :])
    w_ada = nrm(ks[3], (Lr, D_MODEL, 6 * D_MODEL), f32) * D_MODEL ** -0.5
    b_ada = nrm(ks[4], (Lr, 6 * D_MODEL), f32) * 0.02
    norm_mix = 1.0 + 0.02 * nrm(ks[5], (Lr, D_MODEL), f32)
    w_in = nrm(ks[6], (Lr, D_MODEL, IN_TOTAL), f32) * D_MODEL ** -0.5
    dn_conv = nrm(ks[7], (Lr, DN_CONV, 3 * DN_WIDTH), f32) * DN_CONV ** -0.5
    dn_a_log = jnp.log(jax.random.uniform(ks[8], (Lr, DN_HEADS), f32, 1.0, 16.0))
    dt = jnp.exp(jax.random.uniform(ks[9], (Lr, DN_HEADS), f32, np.log(1e-3), np.log(1e-1)))
    dn_dt_bias = jnp.log(jnp.expm1(dt))
    dn_norm = 1.0 + 0.02 * nrm(ks[10], (Lr, DN_HEAD_DIM), f32)
    w_dn_out = nrm(ks[11], (Lr, DN_WIDTH, D_MODEL), f32) * DN_WIDTH ** -0.5
    swa_q_norm = 1.0 + 0.02 * nrm(ks[12], (Lr, SWA_HEAD_DIM), f32)
    swa_k_norm = 1.0 + 0.02 * nrm(ks[13], (Lr, SWA_HEAD_DIM), f32)
    swa_sinks = nrm(ks[14], (Lr, SWA_Q_HEADS), f32)
    w_swa_out = nrm(ks[15], (Lr, SWA_WIDTH, D_MODEL), f32) * SWA_WIDTH ** -0.5
    w_o = nrm(ks[16], (Lr, D_MODEL, D_MODEL), f32) * D_MODEL ** -0.5
    norm_ffn = 1.0 + 0.02 * nrm(ks[17], (Lr, D_MODEL), f32)
    w_up = nrm(ks[18], (Lr, D_MODEL, 2 * D_FF), f32) * D_MODEL ** -0.5
    ffn_conv = nrm(ks[19], (Lr, FFN_CONV, D_FF), f32) * FFN_CONV ** -0.5
    ffn_conv_b = nrm(ks[20], (Lr, D_FF), f32) * 0.02
    w_down = nrm(ks[21], (Lr, D_FF, D_MODEL), f32) * D_FF ** -0.5
    return {"x": x, "c": c, "positions": positions, "w_ada": w_ada, "b_ada": b_ada,
            "norm_mix": norm_mix, "w_in": w_in, "dn_conv": dn_conv, "dn_a_log": dn_a_log,
            "dn_dt_bias": dn_dt_bias, "dn_norm": dn_norm, "w_dn_out": w_dn_out,
            "swa_q_norm": swa_q_norm, "swa_k_norm": swa_k_norm, "swa_sinks": swa_sinks,
            "w_swa_out": w_swa_out, "w_o": w_o, "norm_ffn": norm_ffn, "w_up": w_up,
            "ffn_conv": ffn_conv, "ffn_conv_b": ffn_conv_b, "w_down": w_down}

def second_block(x, c, positions, w_ada, b_ada, norm_mix, w_in, dn_conv, dn_a_log, dn_dt_bias,
              dn_norm, w_dn_out, swa_q_norm, swa_k_norm, swa_sinks, w_swa_out, w_o,
              norm_ffn, w_up, ffn_conv, ffn_conv_b, w_down):
    B, T, _ = x.shape
    c_act = jax.nn.silu(c)
    for l in range(DEPTH):
        mod = c_act @ w_ada[l] + b_ada[l]
        sh1, sc1, gt1, sh2, sc2, gt2 = [m[:, None, :] for m in jnp.split(mod, 6, axis=-1)]

        h = rms_norm_2(x, norm_mix[l]) * (1.0 + sc1) + sh1
        proj = h @ w_in[l]
        dn_qkv, dn_z, dn_a, dn_b, sw_q, sw_k, sw_v, gate_a, gate_b = _split_columns(proj, IN_SIZES)

        dn_qkv = jax.nn.silu(causal_dwconv(dn_qkv, dn_conv[l]))
        dq, dk, dv = [t.reshape(B, T, DN_HEADS, DN_HEAD_DIM) for t in jnp.split(dn_qkv, 3, axis=-1)]
        dq, dk = l2_norm(dq), l2_norm(dk)
        g = -jnp.exp(dn_a_log[l].astype(jnp.float32)) * jax.nn.softplus(
            dn_a.astype(jnp.float32) + dn_dt_bias[l].astype(jnp.float32))
        beta = jax.nn.sigmoid(dn_b.astype(jnp.float32))
        o_dn = gated_delta_rule_chunked(dq, dk, dv, g, beta)
        o_dn = rms_norm_2(o_dn, dn_norm[l]) * jax.nn.silu(dn_z.reshape(B, T, DN_HEADS, DN_HEAD_DIM))
        y_a = o_dn.reshape(B, T, DN_WIDTH) @ w_dn_out[l]

        sq = partial_rope(rms_norm_2(sw_q.reshape(B, T, SWA_Q_HEADS, SWA_HEAD_DIM), swa_q_norm[l]), positions)
        sk = partial_rope(rms_norm_2(sw_k.reshape(B, T, SWA_KV_HEADS, SWA_HEAD_DIM), swa_k_norm[l]), positions)
        sv = sw_v.reshape(B, T, SWA_KV_HEADS, SWA_HEAD_DIM)
        y_b = swa_sink_attention(sq, sk, sv, swa_sinks[l]) @ w_swa_out[l]

        merged = jax.nn.sigmoid(gate_a) * y_a + jax.nn.sigmoid(gate_b) * y_b
        x = x + gt1 * (merged @ w_o[l])

        h = rms_norm_2(x, norm_ffn[l]) * (1.0 + sc2) + sh2
        up_act, up_lin = jnp.split(h @ w_up[l], 2, axis=-1)
        up_act = causal_dwconv(up_act, ffn_conv[l]) + ffn_conv_b[l]
        x = x + gt2 * ((jax.nn.silu(up_act) * up_lin) @ w_down[l])
    return x


def setup_inputs(seed=0):
    out = dict(first_inputs(seed))
    for name, value in second_inputs(seed + 1).items():
        if name != "x":
            out[name + "_2"] = value
    return out


def reference(
    x, c, ctx, c_ctx, mod_w, mod_b, norm_g, ffn_w_in, ffn_w_out, even_w_in, even_w_out,
    attn_qk_norm_g, attn_sink, hgrn_out_norm_g, hgrn_lb, odd_w_in, odd_w_out, c_2, positions_2,
    w_ada_2, b_ada_2, norm_mix_2, w_in_2, dn_conv_2, dn_a_log_2, dn_dt_bias_2, dn_norm_2,
    w_dn_out_2, swa_q_norm_2, swa_k_norm_2, swa_sinks_2, w_swa_out_2, w_o_2, norm_ffn_2, w_up_2,
    ffn_conv_2, ffn_conv_b_2, w_down_2,
):
    x = first_block(
        x, c, ctx, c_ctx, mod_w, mod_b, norm_g, ffn_w_in, ffn_w_out, even_w_in, even_w_out,
        attn_qk_norm_g, attn_sink, hgrn_out_norm_g, hgrn_lb, odd_w_in, odd_w_out,
    )
    return second_block(
        x, c_2, positions_2, w_ada_2, b_ada_2, norm_mix_2, w_in_2, dn_conv_2, dn_a_log_2,
        dn_dt_bias_2, dn_norm_2, w_dn_out_2, swa_q_norm_2, swa_k_norm_2, swa_sinks_2,
        w_swa_out_2, w_o_2, norm_ffn_2, w_up_2, ffn_conv_2, ffn_conv_b_2, w_down_2,
    )


_drawn_inputs = setup_inputs


def setup_inputs(seed=0):
    import zlib

    import numpy as np

    out = dict(_drawn_inputs(seed))
    spreads = {}
    factors = {'norm_g': 4.031,
     'attn_qk_norm_g': 8.0,
     'attn_sink': 8.0,
     'hgrn_out_norm_g': 8.0,
     'hgrn_lb': 8.0,
     'norm_mix_2': 4.818,
     'dn_norm_2': 7.643,
     'swa_q_norm_2': 8.0,
     'swa_k_norm_2': 8.0,
     'swa_sinks_2': 3.885,
     'norm_ffn_2': 3.041,
     'ffn_conv_b_2': 5.245}
    for name, (base, spread) in spreads.items():
        noise = np.random.default_rng([zlib.crc32(name.encode()), seed]).standard_normal(out[name].shape)
        drawn = base * np.exp(spread * noise) if base else spread * noise
        out[name] = jnp.asarray(drawn.astype(out[name].dtype))
    for name, factor in factors.items():
        out[name] = (out[name] * factor).astype(out[name].dtype)
    return out
```

```python
from contextlib import ExitStack

import numpy as np

import concourse.bass as bass
from concourse import mybir

F32 = mybir.dt.float32
I32 = mybir.dt.int32
U8 = mybir.dt.uint8
ALU = mybir.AluOpType
ACT = mybir.ActivationFunctionType
AXX = mybir.AxisListType.X

P = 128
D = 1024
KD = D // P
NT = 4
CTX, LAT, BOTH = (0, 1), (2, 3), (0, 1, 2, 3)
EPS = 1e-6
MOD_CHUNKS = 12
FF = 2816
KF = FF // P
FF_SPLIT = (8, 8, 6)
EVEN_HEADS, HD = 8, 64
HG = 4
RET = 4
DN = 8
SWA = 16
RING = 2
WT = KD * 512
EXP_LN = "natural_log_exp_and_others"
SILU_TANH = "silu_and_others"
NEG = -1e30


def shape_constants():
    f = np.float32
    t = np.arange(256)
    p, q = np.arange(P)[:, None], np.arange(P)[None, :]
    same64 = (p // 64) == (q // 64)
    inv = (10000.0 ** (-np.arange(16, dtype=f) / 16)).astype(f)
    ang = np.concatenate([(t // 64).astype(f)[:, None] * inv, (t % 64).astype(f)[:, None] * inv], axis=-1)
    rope = np.concatenate([np.cos(ang), np.sin(ang)], axis=-1).reshape(2, P, 64).transpose(1, 0, 2)
    theta = (1.0 / (10000.0 ** np.linspace(0.0, 1.0, 128, dtype=f))).astype(f)
    rang = theta[:, None] * t.astype(f)[None, :]
    ret_rope = np.concatenate([np.cos(rang), np.sin(rang)], axis=1)
    win = np.zeros((P, 2, 512), f)
    swa = np.zeros((P, 384), f)
    swa[:, 0:128] = np.where(q <= p, 0.0, NEG)
    for i in range(2):
        qt = (i * P + np.arange(P))[:, None]
        win[:, i, 256:] = np.where(np.abs(t[None, :] - qt) <= 128, 0.0, NEG)
        if i == 1:
            swa[:, 128:384] = np.where((t[None, :] <= qt) & (qt - t[None, :] < 128), 0.0, NEG)
    u = np.arange(512)
    scan = np.stack([(u % 64 != 0), (u % 64 != 63)]).astype(f)
    f_const = np.concatenate(
        [
            np.eye(P), np.ones((P, P)), (p <= q), np.where(p <= q, 0.0, NEG), np.where(q < p, 0.0, NEG),
            rope.reshape(P, 128), ret_rope, win.reshape(P, 1024), swa,
            np.broadcast_to(scan.reshape(1, 1024), (P, 1024)),
            np.broadcast_to((500000.0 ** (-np.arange(8, dtype=f) / 8)).astype(f)[None, :], (P, 8)),
        ],
        axis=1,
    ).astype(f)
    masks = [same64 & (p <= q), same64 & (p >= q)]
    for level in range(7):
        b = 1 << level
        fill = (p // (2 * b) == q // (2 * b)) & (p // b % 2 == 1) & (q // b % 2 == 0)
        masks += [fill, fill.T]
    b_const = np.concatenate(masks, axis=1).astype(f)
    gamma = np.log(1.0 - 2.0 ** (-5.0 - np.arange(RET)))
    s, tt = np.arange(512)[:, None], t[None, :]
    ret = []
    for h in range(RET):
        a, b = gamma[h], gamma[RET - 1 - h]
        context = np.exp(a * (tt + 256.0 - s)) + np.exp(b * (256.0 - tt + s))
        d = tt - (s - 256.0)
        latent = np.where(d >= 0, np.exp(a * np.maximum(d, 0)), 0) + np.where(d <= 0, np.exp(b * np.maximum(-d, 0)), 0)
        ret.append(np.where(s < 256, context, latent) / 16.0)
    ret = np.stack(ret).reshape(RET, 4, P, 256).transpose(0, 2, 1, 3)
    return f_const, np.ascontiguousarray(b_const), np.ascontiguousarray(ret.astype(f))


F_COLS = {}
_at = 0
for _name, _n in (("ident", P), ("ones", P), ("tri", P), ("incl", P), ("strict", P), ("rope", 128),
                  ("ret_rope", 512), ("win", 1024), ("swa", 384), ("scan", 1024), ("inv", 8)):
    F_COLS[_name] = (_at, _at + _n)
    _at += _n
F_WIDTH = _at


class Plan:

    def __init__(self):
        self.jobs, self.tiles, self.parts = 0, 0, 0
        self.job, self.tile, self.part = {}, {}, {}
        self.done = []

    def start(self, stage):
        self.job[stage], self.tile[stage], self.part[stage] = self.jobs, self.tiles, self.parts

    def free_jobs(self, stage, n):
        self.start(stage)
        self.jobs += n

    def weights(self, stage, jobs_per_tile):
        self.start(stage)
        for n in jobs_per_tile:
            self.jobs += n
            self.tiles += 1
            self.done.append(("job", self.jobs))

    def down(self, stage, halves, groups, tok):
        self.start(stage)
        for _ in range(halves):
            for g in range(groups):
                self.tiles += 1
                if g < groups - 1:
                    self.parts += 1
                    self.done.append(("part", self.parts))
                else:
                    self.jobs += tok
                    self.done.append(("job", self.jobs))


MOD_START = [("A", 0), ("A", 1), ("B", 0), ("A", 2), ("B", 1), ("A", 3), ("B", 2), ("B", 3)]
MOD_FILL = [[("A", 4)]] + [[("A", n), ("B", n - 1)] for n in range(5, 48)] + [[("B", 47)]]
MOD_GROUPS = [MOD_START] + MOD_FILL
FILL_ATT, FILL_HG, FILL_RET = 16, 16, 13


def make_plans():
    a = Plan()
    where = {}

    def mod(g):
        for kind, n in MOD_GROUPS[g]:
            name = f"mod{kind}{n}"
            if kind == "A":
                a.weights(name, [1])
            else:
                a.free_jobs(name, 1)

    mod(0)
    a.free_jobs("norm0", KD)
    a.weights("even_q", [4])
    a.weights("even_k", [4])
    a.weights("even_v", [4])
    a.weights("even_bq", [HG])
    a.weights("even_bf", [HG, HG])
    a.weights("even_bi", [4])
    a.weights("even_bg", [4])
    a.free_jobs("even_qkT", 2 * NT)
    for g in range(FILL_ATT):
        mod(1 + g)
    for w in range(2 * HG):
        for g in range(FILL_HG // (2 * HG)):
            mod(1 + FILL_ATT + 2 * w + g)
        if w % 2:
            a.free_jobs(f"hg_o{w // 2}", 1)
    a.free_jobs("even_catT", KD)
    a.free_jobs("gate0", 4)
    a.weights("even_out", [4, 4])
    a.free_jobs("norm1", KD)
    a.weights("ffn0", [4] * 11)
    a.free_jobs("gate1", 4)
    a.down("down0", 2, 3, 4)
    a.free_jobs("norm2", KD)
    a.weights("ret_q", [4, 4])
    a.weights("ret_k", [4, 4])
    a.weights("ret_v", [4] * 4)
    a.weights("ret_g", [2] * 4)
    for g in range(FILL_RET):
        mod(1 + FILL_ATT + FILL_HG + g)
    a.free_jobs("ret_oT", KD)
    a.free_jobs("gate2", 2)
    a.down("ret_out", 2, 2, 2)
    a.free_jobs("norm3", KD)
    a.weights("ffn1", [4] * 11)
    a.free_jobs("gate3", 2)
    a.down("down1", 2, 3, 2)

    b = Plan()
    b.free_jobs("param", 2)
    b.free_jobs("norm", KD)
    b.weights("swa_q", [2, 2])
    b.weights("swa_k", [2])
    b.weights("swa_v", [2])
    b.weights("dn_in", [4] * 6)
    b.weights("dn_ab", [2])
    b.free_jobs("swa_qkT", 6)
    b.weights("gate_b", [2, 2])
    b.free_jobs("swa_oT", KD)
    b.weights("swa_out", [2, 2])
    b.weights("dn_z", [2, 2])
    b.weights("gate_a", [2, 2])
    b.free_jobs("dn_oT", KD)
    b.weights("dn_out", [2, 2])
    b.free_jobs("mergeT", KD)
    b.free_jobs("gate_mix", 2)
    b.weights("w_o", [2, 2])
    b.free_jobs("norm_ffn", KD)
    b.weights("up", [4] * 11)
    b.free_jobs("gate_ffn", 2)
    b.down("down", 2, 3, 2)
    return a, b


def need(eng, sem, value):
    if isinstance(value, int) and value <= 0:
        return
    eng.wait_ge(sem, value)


def since(eng, sem, before, n):
    if n > 0:
        eng.wait_ge(sem, before + n)


class Chain:

    def __init__(self, eng, sem):
        self.eng, self.sem, self.n, self.base = eng, sem, 0, 0

    def link(self, ins):
        self.n += 1
        ins.then_inc(self.sem, 1)
        self.eng.wait_ge(self.sem, self.base + self.n)

    def enter(self, layer, per_layer):
        self.base, self.n, self.per = self.n + layer * per_layer, 0, per_layer

    def leave(self, name):
        assert self.n == self.per, f"{name}: {self.n} links in a layer"


class Cursor:

    def __init__(self):
        self.n, self.base = 0, 0

    def next(self):
        self.n += 1
        return self.n - 1

    def enter(self, base):
        self.n, self.base = 0, base


DVE_LINKS, ACT_LINKS = 294, 22


def first_then_second_block(nc, a, out):
    pre, per = make_plans()
    DEPTH2 = a["w_in_2"].shape[0]

    with ExitStack() as ctx:
        def sb(name, shape, dt=F32):
            return ctx.enter_context(nc.sbuf_tensor(name, shape, dt))

        def sem(name):
            return ctx.enter_context(nc.semaphore(name))

        x = sb("x", [P, NT, D])
        hT = sb("hT", [P, KD, NT * P])
        ring = sb("ring", [P, RING, WT])
        gate = sb("gate", [P, 2, D])
        ybuf = sb("ybuf", [P, 2, 512])
        conv_in = sb("conv_in", [P, 2, 260])
        fconst = sb("fconst", [P, F_WIDTH])
        bconst = sb("bconst", [P, 2048], U8)
        vcols = sb("vcols", [P, 256])
        modc = sb("modc", [P, 4, 2, 48])
        mb = sb("mb", [P, 2, 48])
        ab = sb("ab", [P, 2, KD])
        rows = sb("rows", [2, 2, 512])
        cond = sb("cond", [P, 2, KD, 2])
        st = sb("st", [P, 512])
        pcols = sb("pcols", [P, 216])
        brow = sb("brow", [P, 288])
        erow = sb("erow", [P, 264])
        dg = sb("dg", [P, 2, 512])
        eps = sb("eps", [P, 1])
        ARENA = 24576
        arena = sb("arena", [P, ARENA])

        def view(at, *shape):
            n = int(np.prod(shape))
            assert at + n <= ARENA, (at, shape)
            v = arena[:, at:at + n]
            if len(shape) == 1:
                return v
            names = "abcd"[:len(shape)]
            return v.rearrange(f"p ({' '.join(names)}) -> p {' '.join(names)}", **dict(zip(names, shape)))

        def const(name):
            lo, hi = F_COLS[name]
            return fconst[:, lo:hi]

        ident, ones, tri = const("ident"), const("ones"), const("tri")

        def over(v, shape):
            return v.to_broadcast(shape)

        acc = ctx.enter_context(nc.psum_tensor("acc", [P, 4, 512], F32))
        mx = ctx.enter_context(nc.psum_tensor("mx", [P, 4, 512], F32))

        hv, hg_, hq = view(0, 4, 512), view(2048, 4, 512), view(4096, 4, 512)
        masks = view(0, 2048)
        hf = [view(6144, 4, 512), view(8192, 4, 512)]
        cat = view(10240, 4, 1024)
        A0 = 14336
        qk_raw, v_raw = view(A0, 4, 640), view(A0 + 2560, 4, 128)
        qk_t0, qk_t1 = view(A0 + 3072, 640), view(A0 + 3712, 640)
        qk_p = view(A0 + 4352, 2, 640)
        ekT, eqT = view(A0 + 5632, 512), view(A0 + 6144, 4, 512)
        eS, ePT = view(A0 + 8192, 2, 512), view(A0 + 9216, 2, 512)
        e_set = [[view(A0 + 2048 * d + 512 * j, 512) for j in range(4)] for d in range(2)]
        h_kk = [view(A0 + 4096 + 512 * d, 512) for d in range(2)]
        h_cum = view(A0 + 5120, 512)
        h_kd = view(A0 + 5632, 2, 4, 128)
        h_sc = [view(A0 + 6656 + 512 * d, 4, 128) for d in range(2)]
        h_S = [view(A0 + 7680 + 1024 * d, 8, 128) for d in range(2)]
        h_kz = view(A0 + 9728, 512)
        o_sq = view(A0, 4, 512)
        ffT4, ffT2 = view(0, KF, 512), view(0, KF, 256)
        f_xs4, f_xs2 = view(11264, 4, 1024), view(5632, 2, 1024)
        g_buf, u_buf, c_buf = view(16384, 2, 512), view(17408, 3, 512), view(18944, 2, 256)
        rv, rg, rk, rq = view(0, 4, 2048), view(8192, 2, 2048), view(12288, 8, 512), view(16384, 8, 256)
        r_t = view(18432, 2, 2, 256)
        r_P, r_D, r_junk = view(19456, 2, 4, 256), view(21504, 2, 4, 256), view(23552, 512)
        r_xs = view(0, 4, 1024)
        d_xs, dnf = view(0, 2, 1024), view(0, 24, 256)
        sqk, s_v = view(6144, 2, 1152), view(8448, 2, 128)
        s_t0, s_t1, s_p = view(8704, 1152), view(9856, 1152), view(11008, 2, 1152)
        sqT, skT = view(13312, 8, 256), view(15360, 256)
        sS, sPT, oswa = view(15616, 2, 256), view(16128, 2, 256), view(16640, 2, 1024)
        sgb, yb = view(18688, 2, 1024), view(20736, 2, 1024)
        dz, sga = view(6144, 2, 1024), view(18688, 2, 1024)
        B0 = 8192
        dL, dT, dTT, dQ, dY = ([view(B0 + 1024 * j + 512 * c, 4, 128) for c in range(2)] for j in range(5))
        t_in, t_st = view(B0 + 5120, 4, 128), view(B0 + 5632, 4, 128)
        t_g, kdec, kbe = view(B0 + 6144, 4, 128), view(B0 + 6656, 4, 128), view(B0 + 7168, 4, 128)
        dS, nwT, qdec, o_t = (view(B0 + 7680 + 512 * j, 4, 128) for j in range(4))
        vb = [view(17920, 4, 128), view(22784, 4, 128)]
        vn = [view(23296 + 512 * c, 4, 128) for c in range(2)]
        l2_sq, l2_rs = view(B0, 2, 512), view(B0 + 1024, 2, 512)
        srope = sb("srope", [P, 2, 16])
        prow = dg[:, :, 0:P]
        dab = sb("dab", [P, 2, 16])
        pos_i = sb("pos_i", [P, 2], I32)

        const_in, rows_in, x_in, even_in = sem("const_in"), sem("rows_in"), sem("x_in"), sem("even_in")
        lrow_in, lbc_in, pos_in = sem("layer_rows_in"), sem("layer_bcast_in"), sem("positions_in")
        dtab_in = [sem("dtab0_in"), sem("dtab1_in")]
        out_stored = sem("out_stored")
        w_in = [sem(f"weights{s}_in") for s in range(RING)]
        w_part = sem("weights_partly_used")
        acc_full, acc_done = sem("acc_full"), sem("acc_done")
        vcol_ps, vcol_sb, cond_e, cond_ready = sem("vcol_ps"), sem("vcol_sb"), sem("cond_e"), sem("cond_ready")
        dve_chain, act_chain = sem("dve_chain"), sem("act_chain")
        setup_done = sem("setup_done")
        ang_ready, rope_ready = sem("ang_ready"), sem("rope_ready")
        norm_rs, norm_xs, norm_ab = sem("norm_rs"), sem("norm_xs"), sem("norm_ab")
        dg_ready, y_used = sem("dg_ready"), sem("y_used")
        qk_ss, qk_rs, qk_ready = sem("qk_ss"), sem("qk_rs"), sem("qk_ready")
        att_s, att_m, att_p, att_t, att_pt, att_o, att_d = (sem(f"att_{n}") for n in (
            "scores", "shifted", "probs", "transposed", "pt_copied", "out_ps", "out_done"))
        lb_x, lb_e = sem("lb_x"), sem("lb_e")
        hg_f, hg_lf, hg_cum, hg_e, hg_prod = (sem(f"hg_{n}") for n in ("f", "logf", "cum", "exps", "products"))
        hg_kt, hg_kts, hg_s, hg_ss, hg_u, hg_st = (sem(f"hg_{n}") for n in (
            "kd_ps", "kd_sb", "scores_ps", "scores_sb", "updates", "states"))
        hg_osq, hg_ors, cat_ready = sem("hg_out_ss"), sem("hg_out_rs"), sem("cat_ready")
        ff_conv, ff_silu, ff_mul = sem("ff_conv"), sem("ff_silu"), sem("ff_mul")
        ret_rope, ret_s, ret_p, ret_o, ret_rs, ret_n = (sem(f"ret_{n}") for n in (
            "roped", "scores", "weighted", "out_ps", "rstd", "normed"))
        lcol_ps, lcol_sb = sem("layer_cols_ps"), sem("layer_cols_sb")
        dc_conv, dc_silu = sem("dn_conv"), sem("dn_silu")
        l2_sqd, l2_ps, l2_rsd, l2_done = sem("l2_sq"), sem("l2_ps"), sem("l2_rs"), sem("l2_done")
        gb_x, gb_e, gc_in, gc_ps, gc_sb, gc_e = (sem(f"dn_{n}") for n in (
            "gate_x", "gate_e", "g", "cum_ps", "cum_sb", "cum_e"))
        tg_in, tg_ps, dec_in, dec_e = sem("dn_tri_g"), sem("dn_cum_rows"), sem("dn_decay_in"), sem("dn_decay")
        kq_ps, l_ready, kv_ps, kv_sb = sem("dn_kk_qk"), sem("dn_triangle"), sem("dn_kv_ps"), sem("dn_kv_sb")
        inv_y, inv_ys, inv_t, inv_d = (sem(f"inv_{n}") for n in ("y_ps", "y_sb", "t_ps", "t_sb"))
        fin_ps, fin_sb, dn_rs, dn_o = sem("dn_fin_ps"), sem("dn_fin_sb"), sem("dn_out_rs"), sem("dn_out_done")

        def wcols(w, lo, hi):
            return w.rearrange("(k p) n -> p k n", p=P)[:, :, lo:hi]

        block = ctx.enter_context(nc.Block())

        @block.sync
        def _(sp):
            tile = Cursor()

            def load(*parts, in_loop=None):
                t = tile.next()
                if in_loop is None:
                    slot = t % RING
                    if t >= RING:
                        kind, n = pre.done[t - RING]
                        sp.wait_ge(acc_full if kind == "job" else w_part, n)
                else:
                    slot = (pre.tiles + t) % RING
                    if t >= RING:
                        kind, n = per.done[t - RING]
                        if kind == "job":
                            sp.wait_ge(acc_full, in_loop * per.jobs + (pre.jobs + n))
                        else:
                            sp.wait_ge(w_part, in_loop * per.parts + (pre.parts + n))
                width = at = sum(q.shape[2] for q in parts)
                for p in reversed(parts):
                    k, n = p.shape[1], p.shape[2]
                    at -= n
                    dst = ring[:, slot, 0:k * width].rearrange("p (k n) -> p k n", k=k)[:, :, at:at + n]
                    sp.dma_start(dst, p).then_inc(w_in[slot], 16 if len(parts) == 2 else 32)

            def mod(g):
                for kind, n in MOD_GROUPS[g]:
                    if kind == "A":
                        layer, c = n // MOD_CHUNKS, n % MOD_CHUNKS
                        w = a["mod_w"][layer] if layer < 2 else a["w_ada_2"][layer - 2]
                        load(wcols(w, 512 * c, 512 * c + 512))

            mod(0)
            ew = a["even_w_in"][0]
            for lo, hi in ((0, 512), (512, 640), (640, 768), (768, 1280), (1280, 1792), (1792, 2304),
                           (2304, 2816), (2816, 3328)):
                load(wcols(ew, lo, hi))
            for g in range(FILL_ATT + FILL_HG):
                mod(1 + g)
            for h in range(2):
                load(wcols(a["even_w_out"][0], 512 * h, 512 * h + 512))

            def feed_forward(w_up, w_down, in_loop=None):
                for b in range(11):
                    load(wcols(w_up, 256 * b, 256 * b + 256), wcols(w_up, FF + 256 * b, FF + 256 * b + 256),
                         in_loop=in_loop)
                for h in range(2):
                    at = 0
                    for n in FF_SPLIT:
                        load(wcols(w_down[P * at:P * (at + n), :], 512 * h, 512 * h + 512), in_loop=in_loop)
                        at += n

            feed_forward(a["ffn_w_in"][0], a["ffn_w_out"][0])
            for c in range(12):
                load(wcols(a["odd_w_in"][0], 512 * c, 512 * c + 512))
            for g in range(FILL_RET):
                mod(1 + FILL_ATT + FILL_HG + g)
            for h in range(2):
                for g in range(2):
                    load(wcols(a["odd_w_out"][0][D * g:D * (g + 1), :], 512 * h, 512 * h + 512))
            feed_forward(a["ffn_w_in"][1], a["ffn_w_out"][1])
            assert tile.n == pre.tiles

            with sp.Fori(0, DEPTH2) as l:
                def of(name):
                    w = a[name]
                    rest = "abc"[:len(w.shape) - 1]
                    return w[bass.ds(l, 1)].rearrange(f"o {' '.join(rest)} -> (o {rest[0]}) {' '.join(rest[1:])}")

                tile.enter(0)
                sp.wait_ge(acc_full, l * per.jobs + pre.jobs)
                sp.wait_ge(y_used, l * 16 + 24)
                for dst, src in (
                    (prow[0:96, 0, :], of("dn_conv_2").rearrange("k (b p) -> (k b) p", p=P)),
                    (prow[96:104, 0, :], a["norm_mix_2"][bass.ds(l, 1)].rearrange("o (b p) -> (o b) p", p=P)),
                    (prow[104:112, 0, :], a["norm_ffn_2"][bass.ds(l, 1)].rearrange("o (b p) -> (o b) p", p=P)),
                    (prow[0:66, 1, :], of("ffn_conv_2").rearrange("k (b p) -> (k b) p", p=P)),
                    (prow[66:88, 1, :], a["ffn_conv_b_2"][bass.ds(l, 1)].rearrange("o (b p) -> (o b) p", p=P)),
                ):
                    sp.dma_start(dst, src).then_inc(lrow_in, 16)
                at = 0
                for name in ("dn_dt_bias_2", "dn_a_log_2", "swa_q_norm_2", "swa_k_norm_2", "swa_sinks_2", "dn_norm_2"):
                    n = a[name].shape[1]
                    sp.dma_start(brow[:, at:at + n], a[name][bass.ds(l, 1)].to_broadcast([P, n])).then_inc(lbc_in, 16)
                    at += n
                w = of("w_in_2")
                for lo, n in ((4112, 512), (4624, 512), (5136, 128), (5264, 128), (0, 512), (512, 512), (1024, 512),
                              (1536, 512), (2048, 512), (2560, 512), (4096, 16), (6416, 512), (6928, 512)):
                    if lo:
                        load(wcols(w, lo, lo + n), in_loop=l)
                    else:
                        load(wcols(w, 0, n // 2), wcols(w, n // 2, n), in_loop=l)
                for h in range(2):
                    load(wcols(of("w_swa_out_2"), 512 * h, 512 * h + 512), in_loop=l)
                for lo in (3072, 3584, 5392, 5904):
                    load(wcols(w, lo, lo + 512), in_loop=l)
                for name in ("w_dn_out_2", "w_o_2"):
                    for h in range(2):
                        load(wcols(of(name), 512 * h, 512 * h + 512), in_loop=l)
                feed_forward(of("w_up_2"), of("w_down_2"), in_loop=l)
                assert tile.n == per.tiles

            sp.wait_ge(y_used, 24 + 16 * DEPTH2)
            sp.dma_start(out[0].rearrange("(t p) d -> p t d", p=P), x[:, 2:4, :]).then_inc(out_stored, 16)
            sp.wait_ge(out_stored, 16)

        @block.gpsimd
        def _(pool):
            for h in range(RET):
                if h >= 2:
                    pool.wait_ge(ret_p, 2 * (h - 1))
                else:
                    pool.wait_ge(acc_full, pre.job["ret_q"])
                    pool.wait_ge(y_used, 16)
                nc.gpsimd.dma_start(r_D[:, h % 2], a["const_ret"][h]).then_inc(dtab_in[h % 2], 16)

        @block.tensor
        def _(pe):
            job, tile, part = Cursor(), Cursor(), Cursor()
            loop = [None]

            def weights(width, k=KD):
                t = tile.next()
                if loop[0] is None:
                    slot = t % RING
                    pe.wait_ge(w_in[slot], 32 * (t // RING + 1))
                else:
                    slot = (pre.tiles + t) % RING
                    pe.wait_ge(w_in[slot], loop[0] * (32 * per.tiles // RING) + 32 * ((pre.tiles + t) // RING + 1))
                return ring[:, slot, 0:k * width].rearrange("p (k n) -> p k n", k=k)

            def bank():
                n = job.next()
                if loop[0] is None:
                    need(pe, acc_done, n - 3)
                else:
                    pe.wait_ge(acc_done, job.base + (n - 3 if n >= 4 else 0))
                return acc[:, n % 4, :]

            def done(n):
                need(pe, acc_done, job.base + n)

            def stage(name):
                p = pre if loop[0] is None else per
                assert (job.n, tile.n) == (p.job[name], p.tile[name]), (name, job.n, tile.n, p.job[name], p.tile[name])

            def by_token(tiles, width, src=hT):
                w = weights(width)
                for i in tiles:
                    b = bank()
                    for k in range(KD):
                        ins = nc.tensor.matmul(b[:, 0:width], src[:, k, P * i:P * (i + 1)], w[:, k, :],
                                               start=k == 0, stop=k == KD - 1)
                    ins.then_inc(acc_full, 1)

            def by_feature(blocks, lo, hi):
                w = weights(P * blocks)
                for f in range(blocks):
                    b = bank()
                    for k in range(KD):
                        ins = nc.tensor.matmul(b[:, 0:hi - lo], w[:, k, P * f:P * (f + 1)], hT[:, k, lo:hi],
                                               start=k == 0, stop=k == KD - 1)
                    ins.then_inc(acc_full, 1)

            def down(src, groups, tiles, ready):
                for h in range(2):
                    banks = [bank() for _ in tiles]
                    at = 0
                    for g, n in enumerate(groups):
                        ready(at + n)
                        w = weights(512, n)
                        for b, i in zip(banks, tiles):
                            for k in range(n):
                                ins = nc.tensor.matmul(b, src[:, at + k, P * i:P * (i + 1)], w[:, k, :],
                                                       start=at + k == 0, stop=at + k == sum(groups) - 1)
                            if g == len(groups) - 1:
                                ins.then_inc(acc_full, 1)
                        if g < len(groups) - 1:
                            ins.then_inc(w_part, 1)
                        at += n

            def transposed(src, tiles, blocks=1):
                for k in range(0, KD * blocks, blocks):
                    b = bank()
                    for q in range(blocks):
                        for j, i in enumerate(tiles):
                            at = P * (q * len(tiles) + j)
                            ins = nc.tensor.transpose(b[:, at:at + P], src[:, i, P * (k + q):P * (k + q + 1)], ident)
                    ins.then_inc(acc_full, 1)

            def mod(g):
                for kind, n in MOD_GROUPS[g]:
                    stage(f"mod{kind}{n}")
                    if kind == "A":
                        w = weights(512)
                        b = bank()
                        for k in range(KD):
                            ins = nc.tensor.matmul(b[0:2, :], cond[:, n // 24, k, :], w[:, k, :],
                                                   start=k == 0, stop=k == KD - 1)
                    else:
                        b = bank()
                        done(pre.job[f"modA{n}"] + 1)
                        for q in range(4):
                            ins = nc.tensor.matmul(b[:, 2 * q:2 * q + 2], rows[:, n % 2, P * q:P * (q + 1)],
                                                   ident[0:2, 0:2], start=True, stop=True)
                    ins.then_inc(acc_full, 1)

            def norm(use, tiles, name):
                stage(name)
                pe.wait_ge(norm_xs, use + 1)
                xs = {0: cat, 1: f_xs4, 2: r_xs, 3: f_xs2}[use] if isinstance(use, int) else None
                return xs

            def gates(jobs, base):
                for s in range(jobs):
                    b = bank()
                    pe.wait_ge(dg_ready, base + s + 1)
                    nc.tensor.matmul(b, ones, dg[:, s % 2, :], start=True, stop=True).then_inc(acc_full, 1)

            def attention(base, units, fill):
                n = len(units)
                for u in range(n + 2):
                    if u < n:
                        q, k, blocks, v = units[u]
                        since(pe, att_m, base, u - 1)
                        nc.tensor.matmul(mx[:, u % 2, 0:P * blocks], q, k, start=True, stop=True).then_inc(att_s, 1)
                    if 1 <= u <= n:
                        blocks = units[u - 1][2]
                        pe.wait_ge(att_p, base + u)
                        since(pe, att_pt, base, u - 1)
                        for j in range(blocks):
                            ins = nc.tensor.transpose(mx[:, 2, P * j:P * (j + 1)], att_S[(u - 1) % 2][:, P * j:P * (j + 1)],
                                                      ident)
                        ins.then_inc(att_t, 1)
                    if u >= 2:
                        o, (_, _, blocks, v) = u - 2, units[u - 2]
                        pe.wait_ge(att_pt, base + o + 1)
                        since(pe, att_d, base, o)
                        for j in range(blocks):
                            ins = nc.tensor.matmul(mx[:, 3, HD * (o % 8):HD * (o % 8 + 1)],
                                                   att_PT[o % 2][:, P * j:P * (j + 1)], v[j],
                                                   start=j == 0, stop=j == blocks - 1)
                        ins.then_inc(att_o, 1)
                    fill(u)

            pe.wait_ge(const_in, 32)
            pe.wait_ge(rows_in, 16 * 7)
            for j in range(2):
                ins = nc.tensor.transpose(mx[:, 0, P * j:P * (j + 1)], dg[:, j, 0:P], ident)
            ins.then_inc(vcol_ps, 1)
            pe.wait_ge(cond_ready, 1)
            mod(0)
            transposed(norm(0, BOTH, "norm0"), BOTH)
            stage("even_q")
            done(pre.job["norm0"] + KD)
            by_token(BOTH, 512)
            by_token(BOTH, P)
            by_token(BOTH, P)
            for _ in range(3):
                by_feature(HG, 0, 512)
            by_token(BOTH, 512)
            by_token(BOTH, 512)
            stage("even_qkT")
            for i in BOTH:
                pe.wait_ge(qk_ready, i + 1)
                b = bank()
                for j in range(4):
                    ins = nc.tensor.transpose(b[:, P * j:P * (j + 1)], qk_p[:, i % 2, P * j:P * (j + 1)], ident)
                ins.then_inc(acc_full, 1)
                b = bank()
                nc.tensor.transpose(b[:, 0:P], qk_p[:, i % 2, 512:640], ident).then_inc(acc_full, 1)
            done(pre.job["even_qkT"] + 2 * NT)
            units = []
            att_S, att_PT = [eS[:, j, :] for j in range(2)], [ePT[:, j, :] for j in range(2)]
            for i in BOTH:
                for kv in range(2):
                    for j in range(4):
                        half = slice(HD * kv, HD * kv + HD)
                        blocks = 2 if i in CTX else 4
                        units.append((eqT[half, j, P * i:P * (i + 1)], ekT[half, 0:P * blocks], blocks,
                                      [v_raw[:, t, HD * kv:HD * kv + HD] for t in range(blocks)]))
            attention(0, units, lambda u: mod(1 + u // 2) if u % 2 == 0 and u // 2 < FILL_ATT else None)
            for w in range(2 * HG):
                h, d = w // 2, w % 2
                pe.wait_ge(hg_prod, w + 1)
                kd = e_set[d][3]
                for t in range(NT):
                    ins = nc.tensor.transpose(mx[:, 0, P * t:P * (t + 1)], kd[:, P * t:P * (t + 1)], ident)
                ins.then_inc(hg_kt, 1)
                need(pe, hg_ss, w)
                for t in range(NT):
                    s = slice(P * t, P * (t + 1))
                    for early in (True, False):
                        at = 32 * (early == (d == 1))
                        q = e_set[d][0][:, s].rearrange("p (n t) -> p n t", t=64)[:, :, at:at + 32]
                        o = mx[:, 1, s].rearrange("p (n t) -> p n t", t=64)[:, :, at:at + 32]
                        ins = nc.tensor.matmul(o, (h_kz if early else e_set[d][1])[:, s], q, start=True, stop=True)
                ins.then_inc(hg_s, 1)
                for g in range(FILL_HG // (2 * HG)):
                    mod(1 + FILL_ATT + 2 * w + g)
                pe.wait_ge(hg_kts, w + 1)
                need(pe, hg_st, w)
                for c in range(8):
                    half = slice(64 * (c % 2), 64 * (c % 2) + 64)
                    ins = nc.tensor.matmul(mx[:, 2 + c % 2, P * (c // 2):P * (c // 2 + 1)], h_kd[half, w % 2, c // 2, :],
                                           hv[half, c // 2, P * h:P * (h + 1)], start=True, stop=True)
                ins.then_inc(hg_u, 1)
                if d == 1:
                    stage(f"hg_o{h}")
                    b = bank()
                    pe.wait_ge(hg_ss, w + 1)
                    pe.wait_ge(hg_st, w + 1)
                    for t in range(NT):
                        v = hv[:, t, P * h:P * (h + 1)]
                        nc.tensor.matmul(b[:, P * t:P * (t + 1)], h_sc[0][:, t, :], v, start=True, stop=False)
                        nc.tensor.matmul(b[:, P * t:P * (t + 1)], h_sc[1][:, t, :], v, start=False, stop=False)
                        for c in (2 * t, 2 * t + 1):
                            half = slice(64 * (c % 2), 64 * (c % 2) + 64)
                            for dd, first in ((0, c == 0), (1, c == 3)):
                                if not first:
                                    ins = nc.tensor.matmul(b[half, P * t:P * (t + 1)], e_set[dd][2][:, 64 * c:64 * c + 64],
                                                           h_S[dd][:, c, :], start=False, stop=dd == (c != 3))
                    ins.then_inc(acc_full, 1)
            pe.wait_ge(cat_ready, 1)
            stage("even_catT")
            transposed(cat, BOTH)
            gates(4, 0)
            stage("even_out")
            done(pre.job["even_catT"] + KD)
            by_token(BOTH, 512)
            by_token(BOTH, 512)

            def feed_forward(names, use, ffT, lo, hi, tiles, gate_base):
                stage(names[0])
                for _ in range(11):
                    by_feature(4, lo, hi)
                gates(4 if len(tiles) == 4 else 2, gate_base)
                down(ffT, FF_SPLIT, tiles, lambda n: pe.wait_ge(ff_mul, use * KF + n))

            transposed(norm(1, BOTH, "norm1"), BOTH)
            done(pre.job["norm1"] + KD)
            feed_forward(["ffn0"], 0, ffT4, 0, 512, BOTH, 4)
            transposed(norm(2, BOTH, "norm2"), BOTH)
            done(pre.job["norm2"] + KD)
            for _ in range(2):
                by_feature(4, 256, 512)
            for _ in range(2):
                by_feature(4, 0, 512)
            for _ in range(4):
                by_token(BOTH, 512)
            for _ in range(4):
                by_token(LAT, 512)
            fills = iter(range(FILL_RET))
            done(pre.job["ret_v"] + 16)
            for h in range(RET):
                pe.wait_ge(ret_rope, h + 1)
                for s2 in range(2):
                    need(pe, ret_p, 2 * h - 1 + s2)
                    for s in (2 * s2, 2 * s2 + 1):
                        for k in range(2):
                            ins = nc.tensor.matmul(mx[:, s2, 256 * (s % 2):256 * (s % 2) + 256],
                                                   rk[:, 2 * h + k, P * s:P * (s + 1)], rq[:, 2 * h + k, :],
                                                   start=k == 0, stop=k == 1)
                    ins.then_inc(ret_s, 1)
                for _ in range(3 if h < 3 else 4):
                    mod(1 + FILL_ATT + FILL_HG + next(fills))
                pe.wait_ge(ret_p, 2 * h + 2)
                for t in range(2):
                    need(pe, ret_n, 2 * h - 1 + t)
                    for s in range(4):
                        ins = nc.tensor.matmul(mx[:, 2 + t, :], r_P[:, h % 2, s, P * t:P * (t + 1)],
                                               rv[:, s, 512 * h:512 * (h + 1)], start=s == 0, stop=s == 3)
                    ins.then_inc(ret_o, 1)
            pe.wait_ge(ret_n, 2 * RET)
            stage("ret_oT")
            transposed(rg, (0, 1), 2)
            gates(2, 8)
            stage("ret_out")
            roT = hT[:, :, :].rearrange("p a b -> p (a b)").rearrange("p (k t) -> p k t", k=16)
            done(pre.job["ret_oT"] + KD)
            down(roT, (8, 8), (0, 1), lambda n: None)
            transposed(norm(3, LAT, "norm3"), (0, 1))
            done(pre.job["norm3"] + KD)
            feed_forward(["ffn1"], 1, ffT2, 256, 512, (0, 1), 10)
            assert job.n == pre.jobs and tile.n == pre.tiles

            with pe.Fori(0, DEPTH2) as l:
                loop[0] = l
                job.enter(l * per.jobs + pre.jobs)
                tile.enter(0)
                oT = hT[:, :, 0:256]
                stage("param")
                pe.wait_ge(lrow_in, l * 80 + 80)
                for j, n in enumerate((112, 88)):
                    b = bank()
                    nc.tensor.transpose(b[:, 0:n], prow[0:n, j, :], ident[0:n, 0:n]).then_inc(acc_full, 1)
                stage("norm")
                pe.wait_ge(norm_xs, l * 2 + 5)
                transposed(d_xs, (0, 1))
                done(per.job["norm"] + KD)
                for _ in range(2):
                    by_token(LAT, 512)
                for _ in range(2):
                    by_token(LAT, P)
                for _ in range(6):
                    by_feature(4, 256, 512)
                by_token(LAT, 16)
                stage("swa_qkT")
                for i in range(2):
                    pe.wait_ge(qk_ready, l * 2 + (NT + i + 1))
                    for j2 in range(2):
                        b = bank()
                        for j in range(4):
                            at = 512 * j2 + P * j
                            ins = nc.tensor.transpose(b[:, P * j:P * (j + 1)], s_p[:, i, at:at + P], ident)
                        ins.then_inc(acc_full, 1)
                    b = bank()
                    nc.tensor.transpose(b[:, 0:P], s_p[:, i, 1024:1152], ident).then_inc(acc_full, 1)
                done(per.job["swa_qkT"] + 6)
                att_S, att_PT = [sS[:, j, :] for j in range(2)], [sPT[:, j, :] for j in range(2)]
                units = []
                for i in range(2):
                    for kv in range(2):
                        for j in range(8):
                            half = slice(HD * kv, HD * kv + HD)
                            units.append((sqT[half, j, P * i:P * (i + 1)], skT[half, 0:P * (i + 1)], i + 1,
                                          [s_v[:, t, HD * kv:HD * kv + HD] for t in range(i + 1)]))
                attention(l * 32 + 32, units, lambda u: None)
                stage("gate_b")
                for _ in range(2):
                    by_token(LAT, 512)
                stage("swa_oT")
                pe.wait_ge(att_d, l * 32 + 64)
                transposed(oswa, (0, 1))
                done(per.job["swa_oT"] + KD)
                for _ in range(2):
                    by_token((0, 1), 512, oT)
                stage("dn_z")
                for _ in range(4):
                    by_token(LAT, 512)
                for s in range(8):
                    pe.wait_ge(l2_sqd, l * 8 + s + 1)
                    since(pe, l2_rsd, l * 8, s - 1)
                    nc.tensor.matmul(mx[:, s % 2, :], ones, l2_sq[:, s % 2, :], start=True, stop=True).then_inc(l2_ps, 1)
                pe.wait_ge(gc_in, l + 1)
                dg_ = st[:, 64:80].rearrange("p (c h) -> p c h", c=2)
                for c in range(2):
                    nc.tensor.matmul(mx[:, 2, 8 * c:8 * c + 8], tri, dg_[:, c, :], start=True, stop=True)
                nc.tensor.matmul(mx[:, 2, 16:24], ones, dg_[:, 0, :], start=True, stop=True).then_inc(gc_ps, 1)
                pe.wait_ge(l2_done, l * 8 + 8)
                for hg in range(2):
                    if hg:
                        pe.wait_ge(dn_o, l * 4 + 2)
                    for c in range(2):
                        g = 2 * hg + c
                        tok = slice(P * c, P * (c + 1))
                        pe.wait_ge(tg_in, l * 4 + g + 1)
                        nc.tensor.matmul(mx[:, 3, :], ones, t_in.rearrange("p a b -> p (a b)"),
                                         start=True, stop=True).then_inc(tg_ps, 1)
                        since(pe, l_ready, l * 4, g)
                        for h in range(4):
                            kT, qT = dnf[:, 8 + 4 * hg + h, tok], dnf[:, 4 * hg + h, tok]
                            nc.tensor.matmul(mx[:, 0, P * h:P * (h + 1)], kT, kT, start=True, stop=True)
                            ins = nc.tensor.matmul(mx[:, 1, P * h:P * (h + 1)], kT, qT, start=True, stop=True)
                        ins.then_inc(kq_ps, 1)
                        for j, f in enumerate((16, 8)):
                            since(pe, kv_sb, l * 8, 2 * g + j)
                            for h in range(4):
                                ins = nc.tensor.transpose(mx[:, 2, P * h:P * (h + 1)], dnf[:, f + 4 * hg + h, tok], ident)
                            ins.then_inc(kv_ps, 1)
                        if c == 1:
                            pe.wait_ge(l_ready, l * 4 + g + 1)
                    for level in range(7):
                        n = (hg * 7 + level) * 2
                        for c in range(2):
                            if level:
                                pe.wait_ge(inv_d, l * 28 + n - 1 + c)
                            for h in range(4):
                                ins = nc.tensor.matmul(mx[:, c, P * h:P * (h + 1)], dL[c][:, h, :], dTT[c][:, h, :],
                                                       start=True, stop=True)
                            ins.then_inc(inv_y, 1)
                        for c in range(2):
                            pe.wait_ge(inv_ys, l * 28 + n + c + 1)
                            if level == 0 and c == 0:
                                pe.wait_ge(kv_sb, l * 8 + 4 * hg + 4)
                            since(pe, inv_d, l * 28, n + c)
                            for h in range(4):
                                nc.tensor.matmul(mx[:, 2, P * h:P * (h + 1)], dT[c][:, h, :], dY[c][:, h, :],
                                                 start=True, stop=True)
                                ins = nc.tensor.matmul(mx[:, 3, P * h:P * (h + 1)], dY[c][:, h, :], dT[c][:, h, :],
                                                       start=True, stop=True)
                            ins.then_inc(inv_t, 1)
                    pe.wait_ge(inv_d, l * 28 + 14 * hg + 14)
                    heads = [(h, slice(P * h, P * (h + 1))) for h in range(4)]
                    for h, s in heads:
                        ins = nc.tensor.matmul(mx[:, 0, s], dTT[0][:, h, :], vb[0][:, h, :], start=True, stop=True)
                    ins.then_inc(fin_ps, 1)
                    for h, s in heads:
                        ins = nc.tensor.matmul(mx[:, 2, s], kbe[:, h, :], dTT[1][:, h, :], start=True, stop=True)
                    ins.then_inc(fin_ps, 1)
                    pe.wait_ge(fin_sb, l * 8 + 4 * hg + 1)
                    for h, s in heads:
                        ins = nc.tensor.matmul(mx[:, 1, s], kdec[:, h, :], vn[0][:, h, :], start=True, stop=True)
                    ins.then_inc(fin_ps, 1)
                    pe.wait_ge(fin_sb, l * 8 + 4 * hg + 3)
                    for h, s in heads:
                        nc.tensor.matmul(mx[:, 3, s], dTT[1][:, h, :], vb[1][:, h, :], start=True, stop=False)
                        ins = nc.tensor.matmul(mx[:, 3, s], nwT[:, h, :], dS[:, h, :], start=False, stop=True)
                    ins.then_inc(fin_ps, 1)
                    for h, s in heads:
                        ins = nc.tensor.matmul(mx[:, 0, s], dQ[0][:, h, :], vn[0][:, h, :], start=True, stop=True)
                    ins.then_inc(fin_ps, 1)
                    pe.wait_ge(fin_sb, l * 8 + 4 * hg + 4)
                    for h, s in heads:
                        nc.tensor.matmul(mx[:, 1, s], qdec[:, h, :], dS[:, h, :], start=True, stop=False)
                        ins = nc.tensor.matmul(mx[:, 1, s], dQ[1][:, h, :], vn[1][:, h, :], start=False, stop=True)
                    ins.then_inc(fin_ps, 1)
                stage("dn_oT")
                pe.wait_ge(dn_o, l * 4 + 4)
                transposed(dz, (0, 1))
                done(per.job["dn_oT"] + KD)
                for _ in range(2):
                    by_token((0, 1), 512, oT)
                stage("mergeT")
                pe.wait_ge(y_used, l * 16 + 32)
                transposed(yb, (0, 1))
                gates(2, l * 4 + 12)
                done(per.job["mergeT"] + KD)
                for _ in range(2):
                    by_token((0, 1), 512, oT)
                stage("norm_ffn")
                pe.wait_ge(norm_xs, l * 2 + 6)
                transposed(f_xs2, (0, 1))
                done(per.job["norm_ffn"] + KD)
                feed_forward(["up"], l + 2, ffT2, 256, 512, (0, 1), l * 4 + 14)
                assert job.n == per.jobs and tile.n == per.tiles

        @block.scalar
        def _(act):
            job, uses = Cursor(), Cursor()
            chain = Chain(act, act_chain)
            loop = [None]

            for dst, src in ((fconst[:], a["const_f"]), (masks, a["const_b"])):
                act.dma_start(dst, src).then_inc(const_in, 16)
            for dst, src in (
                (dg[0:96, 0, 0:P], a["mod_b"].rearrange("l (b p) -> (l b) p", p=P)),
                (dg[96:128, 0, 0:P], a["norm_g"].rearrange("l h (k p) -> (l h k) p", p=P)),
                (dg[0:96, 1, 0:P], a["b_ada_2"].rearrange("l (b p) -> (l b) p", p=P)),
                (dg[96:104, 1, 0:P], a["c"].rearrange("o (k p) -> (o k) p", p=P)),
                (dg[104:112, 1, 0:P], a["c_ctx"].rearrange("(k p) -> k p", p=P)),
                (dg[112:120, 1, 0:P], a["c_2"].rearrange("o (k p) -> (o k) p", p=P)),
                (dg[120:128, 1, 0:P], a["hgrn_lb"].rearrange("l (k p) -> (l k) p", p=P)),
            ):
                act.dma_start(dst, src).then_inc(rows_in, 16)
            for j, name in enumerate(("ctx", "x")):
                act.dma_start(x[:, 2 * j:2 * j + 2, :], a[name][0].rearrange("(t p) d -> p t d", p=P)).then_inc(x_in, 16)
            for lo, src in ((0, a["attn_qk_norm_g"][0, 0:1, :]), (64, a["attn_qk_norm_g"][0, 1:2, :]),
                            (128, a["hgrn_out_norm_g"]), (256, a["attn_sink"])):
                n = src.shape[1]
                act.dma_start(erow[:, lo:lo + n], src.to_broadcast([P, n])).then_inc(even_in, 16)
            act.dma_start(pos_i[:, :], a["positions_2"][0].rearrange("(t p) -> p t", p=P),
                          allow_slow_non_contiguous=True).then_inc(pos_in, 16)

            def evac(dst, width, func=ACT.Copy, rows_=P, shape=None, first=0, signal=True, **kw):
                if first == 0:
                    job.now = job.next()
                    act.wait_ge(acc_full, job.base + job.now + 1)
                src = acc[0:rows_, job.now % 4, first:first + width]
                if shape:
                    src = src.rearrange(shape[0], **shape[1])
                ins = nc.scalar.activation(dst, src, func, **kw)
                if signal:
                    ins.then_inc(acc_done, 1)

            def stage(name):
                p = pre if loop[0] is None else per
                assert job.n == p.job[name], name

            def mod(g):
                for kind, n in MOD_GROUPS[g]:
                    stage(f"mod{kind}{n}")
                    if kind == "A":
                        evac(rows[:, n % 2, :], 512, rows_=2)
                    else:
                        c = 4 * (n % MOD_CHUNKS)
                        evac(modc[:, n // MOD_CHUNKS, :, c:c + 4], 8, shape=("p (b c) -> p c b", dict(c=2)))

            def exp_ln():
                nc.scalar.preload_act_table_set(EXP_LN)

            def silu_tanh():
                nc.scalar.preload_act_table_set(SILU_TANH)

            def rsqrt(dst, src, tmp, scale, signal):
                chain.link(nc.scalar.activation(tmp, src, ACT.Ln, bias=eps[:, 0:1], scale=scale))
                nc.scalar.activation(dst, tmp, ACT.Exp, scale=-0.5).then_inc(signal, 1)

            def norm(tiles, xs, name, sums_before=None):
                exp_ln()
                if sums_before is not None:
                    act.wait_ge(y_used, sums_before)
                for j, i in enumerate(tiles):
                    ins = nc.scalar.activation(xs[:, j, :], x[:, i, :], ACT.Square, accum_out=st[:, j:j + 1])
                n = len(tiles)
                chain.link(ins)
                rsqrt(st[:, 4:4 + n], st[:, 0:n], st[:, 416:416 + n], 1.0 / D, norm_rs)
                stage(name)

            def modulated(shift, n, use):
                act.wait_ge(norm_ab, use + 1)
                for k in range(KD):
                    if n == 4:
                        evac(hT[:, k, 0:256], 256, ACT.Identity, signal=False,
                             scale=ab[:, 1, k:k + 1], bias=mb[:, 1, shift + k:shift + k + 1])
                        evac(hT[:, k, 256:512], 256, ACT.Identity, first=256,
                             scale=ab[:, 0, k:k + 1], bias=mb[:, 0, shift + k:shift + k + 1])
                    else:
                        evac(hT[:, k, 256:512], 256, ACT.Identity,
                             scale=ab[:, 0, k:k + 1], bias=mb[:, 0, shift + k:shift + k + 1])

            def gates(conds):
                for g in conds:
                    for h in range(2):
                        evac(gate[:, g, 512 * h:512 * h + 512], 512)

            def sums(n, base=0):
                for _ in range(n):
                    u = uses.next()
                    need(act, y_used, uses.base + u - 1 if loop[0] is not None else u - 1)
                    evac(ybuf[:, u % 2, :], 512)

            def attention(base, n, blocks, sink, S, PT, fill):
                for u in range(n + 1):
                    if u < n:
                        act.wait_ge(att_m, base + u + 1)
                        c = u % 8
                        nc.scalar.activation(S[u % 2][:, 0:P * blocks(u)], S[u % 2][:, 0:P * blocks(u)], ACT.Exp,
                                             bias=st[:, 8 + c:9 + c], accum_out=st[:, 16 + c:17 + c])
                        nc.scalar.activation(st[:, 24 + c:25 + c], sink(u), ACT.Exp,
                                             bias=st[:, 8 + c:9 + c]).then_inc(att_p, 1)
                    if u >= 1:
                        act.wait_ge(att_t, base + u)
                        since(act, att_o, base, u - 2)
                        w = P * blocks(u - 1)
                        nc.scalar.activation(PT[(u - 1) % 2][:, 0:w], mx[:, 2, 0:w], ACT.Copy).then_inc(att_pt, 1)
                    fill(u)

            silu_tanh()
            act.wait_ge(vcol_sb, 1)
            for blk, j, lo in ((0, 0, 224), (0, 1, 232), (1, 0, 240), (1, 1, 240)):
                ins = nc.scalar.activation(cond[:, blk, :, j], vcols[:, lo:lo + KD], ACT.Silu)
            ins.then_inc(cond_ready, 1)
            act.wait_ge(ang_ready, 1)
            nc.scalar.activation(srope[:, :, :], st[:, 464:496].rearrange("p (t f) -> p t f", t=2),
                                 ACT.Sin).then_inc(rope_ready, 1)
            exp_ln()
            act.wait_ge(lb_x, 1)
            nc.scalar.activation(st[:, 336:344], st[:, 328:336], ACT.Exp).then_inc(lb_e, 1)
            act.wait_ge(x_in, 32)
            norm(BOTH, cat, "modA0")
            mod(0)
            stage("norm0")
            modulated(0, 4, 0)
            silu_tanh()
            for i in BOTH:
                evac(qk_raw[:, i, 0:512], 512)
            for i in BOTH:
                evac(qk_raw[:, i, 512:640], P)
            for i in BOTH:
                evac(v_raw[:, i, :], P)
            for h in range(HG):
                evac(hq[:, h, :], 512, ACT.Silu)
            for d in range(2):
                for h in range(HG):
                    evac(hf[d][:, h, :], 512, ACT.Tanh, scale=0.5)
            for i in BOTH:
                evac(hv[:, i, :], 512)
            for i in BOTH:
                evac(hg_[:, i, :], 512, ACT.Silu)
            exp_ln()
            act.wait_ge(qk_ss, 1)
            rsqrt(st[:, 120:160], st[:, 80:120], st[:, 120:160], 1.0 / HD, qk_rs)
            for i in BOTH:
                evac(eqT[:, :, P * i:P * (i + 1)], 512, shape=("p (j t) -> p j t", dict(j=4)))
                evac(ekT[:, P * i:P * (i + 1)], P)
            act.wait_ge(even_in, 64)
            attention(0, 32, lambda u: 2 if u < 16 else 4, lambda u: erow[:, 256 + u % 8:257 + u % 8],
                      [eS[:, j, :] for j in range(2)], [ePT[:, j, :] for j in range(2)],
                      lambda u: mod(1 + u // 2) if u % 2 == 0 and u // 2 < FILL_ATT else None)
            for w in range(2 * HG):
                h, d = w // 2, w % 2
                act.wait_ge(hg_f, w + 1)
                nc.scalar.activation(e_set[d][1], hf[d][:, h, :], ACT.Ln).then_inc(hg_lf, 1)
                act.wait_ge(hg_cum, w + 1)
                nc.scalar.activation(e_set[d][1], e_set[d][0], ACT.Exp, scale=-1.0)
                nc.scalar.activation(e_set[d][2], h_cum, ACT.Exp)
                chain.link(nc.scalar.activation(e_set[d][3], e_set[d][3], ACT.Exp))
                nc.scalar.activation(e_set[d][0], e_set[d][0], ACT.Exp).then_inc(hg_e, 1)
                act.wait_ge(hg_kt, w + 1)
                need(act, hg_u, w - 1)
                nc.scalar.activation(h_kd[:, w % 2, :, :], mx[:, 0, :].rearrange("p (t k) -> p t k", t=4),
                                     ACT.Copy).then_inc(hg_kts, 1)
                for g in range(FILL_HG // (2 * HG)):
                    mod(1 + FILL_ATT + 2 * w + g)
                if d == 1:
                    stage(f"hg_o{h}")
                    evac(cat[:, :, 512 + P * h:512 + P * (h + 1)], 512, shape=("p (t e) -> p t e", dict(t=4)))
            act.wait_ge(hg_osq, 1)
            rsqrt(st[:, 384:400], st[:, 368:384], st[:, 384:400], 1.0 / P, hg_ors)
            stage("even_catT")
            for k in range(KD):
                evac(hT[:, k, :], 512)
            gates((0, 1))
            stage("even_out")
            sums(8)

            def feed_forward(use, n, tiles, gated, shift, xs, norm_job, conv=False):
                norm(tiles, xs, norm_job, gated)
                modulated(shift, len(tiles), use_norm[0])
                silu_tanh()
                for t in range(11):
                    for j in range(2):
                        b = 2 * t + j
                        if conv:
                            since(act, ff_conv, l_ff[0] * KF, b - 1)
                            evac(conv_in[:, j, 3:259], n)
                        else:
                            need(act, ff_mul, use * KF + b - 1)
                            evac(g_buf[:, j, 0:n], n, ACT.Silu)
                    for j in range(2):
                        b = 2 * t + j
                        if conv:
                            since(act, ff_mul, use * KF, b - 1)
                        evac(u_buf[:, j, 0:n], n)
                    if conv:
                        for j in range(2):
                            act.wait_ge(ff_conv, l_ff[0] * KF + 2 * t + j + 1)
                            nc.scalar.activation(g_buf[:, j, 0:n], c_buf[:, j, :], ACT.Silu).then_inc(ff_silu, 1)

            use_norm, l_ff = [1], [0]
            feed_forward(0, 512, BOTH, 8, 24, f_xs4, "norm1")
            gates((0, 1))
            sums(8)
            norm(BOTH, r_xs, "norm2", 16)
            modulated(0, 4, 2)
            silu_tanh()
            for f in range(8):
                evac(rq[:, f, :], 256)
            for f in range(8):
                evac(rk[:, f, :], 512)
            for c in range(4):
                for i in BOTH:
                    evac(rv[:, i, 512 * c:512 * (c + 1)], 512)
            for c in range(4):
                for t in range(2):
                    evac(rg[:, t, 512 * c:512 * (c + 1)], 512, ACT.Silu)
            exp_ln()
            fills = iter(range(FILL_RET))
            for h in range(RET):
                for _ in range(3 if h < 3 else 4):
                    mod(1 + FILL_ATT + FILL_HG + next(fills))
                for t in range(2):
                    n = 2 * h + t
                    act.wait_ge(ret_o, n + 1)
                    chain.link(nc.scalar.activation(r_junk, mx[:, 2 + t, :], ACT.Square,
                                                    accum_out=st[:, 400 + n:401 + n]))
                    rsqrt(st[:, 408 + n:409 + n], st[:, 400 + n:401 + n], st[:, 416 + n:417 + n], 1.0 / 512, ret_rs)
            stage("ret_oT")
            roT = hT[:, :, :].rearrange("p a b -> p (a b)").rearrange("p (k t) -> p k t", k=16)
            for k in range(KD):
                evac(roT[:, 2 * k:2 * k + 2, :], 512, shape=("p (q t) -> p q t", dict(q=2)))
            gates((1,))
            stage("ret_out")
            sums(4)
            use_norm[0] = 3
            feed_forward(1, 256, LAT, 20, 24, f_xs2, "norm3")
            gates((1,))
            sums(4)
            assert job.n == pre.jobs

            with act.Fori(0, DEPTH2) as l:
                loop[0] = l
                job.enter(l * per.jobs + pre.jobs)
                uses.enter(l * 16 + 24)
                chain.enter(l, ACT_LINKS)
                for j, n in enumerate((112, 88)):
                    evac(pcols[:, P * j:P * j + n], n)
                norm(LAT, d_xs, "norm", l * 16 + 24)
                modulated(0, 2, l * 2 + 4)
                silu_tanh()
                for c in range(2):
                    for t in range(2):
                        evac(sqk[:, t, 512 * c:512 * (c + 1)], 512)
                for t in range(2):
                    evac(sqk[:, t, 1024:1152], P)
                for t in range(2):
                    evac(s_v[:, t, :], P)
                for b in range(25):
                    if b < 24:
                        since(act, dc_conv, l * 24, b - 1)
                        evac(conv_in[:, b % 2, 3:259], 256)
                    if b:
                        act.wait_ge(dc_conv, l * 24 + b)
                        nc.scalar.activation(dnf[:, b - 1, :], dnf[:, b - 1, :], ACT.Silu).then_inc(dc_silu, 1)
                for t in range(2):
                    evac(dab[:, t, :], 16)
                exp_ln()
                act.wait_ge(qk_ss, l + 2)
                rsqrt(st[:, 120:156], st[:, 80:116], st[:, 120:156], 1.0 / HD, qk_rs)
                for i in range(2):
                    for j2 in range(2):
                        evac(sqT[:, 4 * j2:4 * j2 + 4, P * i:P * (i + 1)], 512, shape=("p (j t) -> p j t", dict(j=4)))
                    evac(skT[:, P * i:P * (i + 1)], P)
                attention(l * 32 + 32, 32, lambda u: 1 if u < 16 else 2, lambda u: brow[:, 144 + u % 16:145 + u % 16],
                          [sS[:, j, :] for j in range(2)], [sPT[:, j, :] for j in range(2)], lambda u: None)
                silu_tanh()
                for c in range(2):
                    for t in range(2):
                        evac(sgb[:, t, 512 * c:512 * (c + 1)], 512, ACT.Tanh, scale=0.5)
                for k in range(KD):
                    evac(hT[:, k, 0:256], 256)
                stage("swa_out")
                sums(4)
                for c in range(2):
                    for t in range(2):
                        evac(dz[:, t, 512 * c:512 * (c + 1)], 512, ACT.Silu)
                act.wait_ge(y_used, l * 16 + 28)
                for c in range(2):
                    for t in range(2):
                        evac(sga[:, t, 512 * c:512 * (c + 1)], 512, ACT.Tanh, scale=0.5)
                exp_ln()
                for s in range(8):
                    act.wait_ge(l2_ps, l * 8 + s + 1)
                    since(act, l2_done, l * 8, s - 1)
                    chain.link(nc.scalar.activation(l2_rs[:, s % 2, :], mx[:, s % 2, :], ACT.Ln, bias=eps[:, 0:1]))
                    nc.scalar.activation(l2_rs[:, s % 2, :], l2_rs[:, s % 2, :], ACT.Exp, scale=-0.5).then_inc(l2_rsd, 1)
                act.wait_ge(gb_x, l + 1)
                chain.link(nc.scalar.activation(st[:, 280:296], st[:, 264:280], ACT.Exp, scale=-1.0))
                nc.scalar.activation(st[:, 280:296], st[:, 280:296], ACT.Ln, bias=1.0)
                nc.scalar.activation(st[:, 296:304], brow[:, 8:16], ACT.Exp)
                nc.scalar.activation(st[:, 216:232].rearrange("p (t h) -> p t h", t=2), dab[:, :, 8:16], ACT.Exp,
                                     scale=-1.0).then_inc(gb_e, 1)
                act.wait_ge(gc_sb, l + 1)
                nc.scalar.activation(st[:, 184:200], st[:, 160:176], ACT.Exp)
                nc.scalar.activation(st[:, 200:208], st[:, 208:216], ACT.Exp).then_inc(gc_e, 1)
                for hg in range(2):
                    for c in range(2):
                        g = 2 * hg + c
                        act.wait_ge(dec_in, l * 4 + g + 1)
                        if c == 1:
                            nc.scalar.activation(qdec, mx[:, 3, :].rearrange("p (h t) -> p h t", h=4), ACT.Exp)
                        nc.scalar.activation(t_g, t_g, ACT.Exp)
                        nc.scalar.activation(t_st, t_st, ACT.Exp).then_inc(dec_e, 1)
                    for level in range(7):
                        n = (hg * 7 + level) * 2
                        for c in range(2):
                            act.wait_ge(inv_y, l * 28 + n + c + 1)
                            if level:
                                act.wait_ge(inv_t, l * 28 + n - 1 + c)
                            nc.scalar.activation(dY[c], mx[:, c, :].rearrange("p (h t) -> p h t", h=4),
                                                 ACT.Copy).then_inc(inv_ys, 1)
                    for n, (dst, b, scale) in enumerate(((vn[0], 0, 1.0), (nwT, 2, -1.0), (dS, 1, 1.0), (vn[1], 3, 1.0))):
                        act.wait_ge(fin_ps, l * 12 + 6 * hg + n + 1)
                        nc.scalar.activation(dst, mx[:, b, :].rearrange("p (h t) -> p h t", h=4), ACT.Copy,
                                             scale=scale).then_inc(fin_sb, 1)
                    for c in range(2):
                        act.wait_ge(fin_ps, l * 12 + 6 * hg + 5 + c)
                        for h in range(4):
                            n = 432 + 8 * hg + 4 * c + h
                            ins = nc.scalar.activation(t_in[:, h, :], mx[:, c, P * h:P * (h + 1)], ACT.Square,
                                                       accum_out=st[:, n:n + 1])
                        chain.link(ins)
                        n = 8 * hg + 4 * c
                        rsqrt(st[:, 448 + n:452 + n], st[:, 432 + n:436 + n], st[:, 416 + 4 * c:420 + 4 * c], 1.0 / P, dn_rs)
                for k in range(KD):
                    evac(hT[:, k, 0:256], 256)
                stage("dn_out")
                sums(4)
                for k in range(KD):
                    evac(hT[:, k, 0:256], 256)
                gates((1,))
                stage("w_o")
                sums(4)
                use_norm[0], l_ff[0] = l * 2 + 5, l
                feed_forward(l + 2, 256, LAT, l * 16 + 36, 24, f_xs2, "norm_ffn", conv=True)
                gates((1,))
                sums(4)
                assert job.n == per.jobs
                chain.leave("ScalarE")

        @block.vector
        def _(dve):
            V = nc.vector
            chain = Chain(dve, dve_chain)
            link = chain.link
            uses = Cursor()
            loop = [None]

            def job_done(name, n):
                if loop[0] is None:
                    dve.wait_ge(acc_done, pre.job[name] + n)
                else:
                    dve.wait_ge(acc_done, loop[0] * per.jobs + (pre.jobs + per.job[name] + n))

            def rep(v, axis, shape):
                return v.unsqueeze(axis).to_broadcast(shape)

            def mod_cols(layer, first, n, bias):
                link(V.tensor_tensor(mb[:, :, first:first + n], modc[:, layer, :, first:first + n],
                                     rep(vcols[:, bias + first:bias + first + n], 1, [P, 2, n]), ALU.add))

            def norm(use, tiles, xs, scale, gain):
                V.scalar_tensor_tensor(ab[:, :, :], mb[:, :, scale:scale + KD], 1.0, rep(gain, 1, [P, 2, KD]),
                                       ALU.add, ALU.mult).then_inc(norm_ab, 1)
                dve.wait_ge(norm_rs, use + 1)
                for j, i in enumerate(tiles):
                    ins = V.tensor_scalar(xs[:, j, :], x[:, i, :], st[:, 4 + j:5 + j], None, ALU.mult)
                ins.then_inc(norm_xs, 1)

            def gates(name, conds, first):
                s = 0
                for c in conds:
                    for h in range(2):
                        if s >= 2:
                            dve.wait_ge(acc_full, pre.job[name] + s - 1)
                        cols = mb[:, c, first + 4 * h:first + 4 * h + 4]
                        V.tensor_tensor(dg[:, s % 2, :].rearrange("p (k m) -> p k m", k=4),
                                        rep(ident, 1, [P, 4, P]), rep(cols, 2, [P, 4, P]), ALU.mult).then_inc(dg_ready, 1)
                        s += 1

            def residual(name, tiles, gate_job, n_gates):
                job_done(gate_job, n_gates)
                for n in range(2 * len(tiles)):
                    h, i = n // len(tiles), tiles[n % len(tiles)]
                    u = uses.next()
                    job_done(name, n + 1)
                    cols = slice(512 * h, 512 * h + 512)
                    link(V.tensor_tensor(ybuf[:, u % 2, :], ybuf[:, u % 2, :], gate[:, i // 2, cols], ALU.mult))
                    V.tensor_tensor(x[:, i, cols], x[:, i, cols], ybuf[:, u % 2, :], ALU.add).then_inc(y_used, 1)

            def attention(base, n, blocks, mask, sink, S, out_):
                for u in range(n + 2):
                    if u < n:
                        w, c = P * blocks(u), u % 8
                        dve.wait_ge(att_s, base + u + 1)
                        since(dve, att_t, base, u - 1)
                        link(V.scalar_tensor_tensor(S[u % 2][:, 0:w], mx[:, u % 2, 0:w], HD ** -0.5, mask(u),
                                                    ALU.mult, ALU.add))
                        link(V.reduce_max(st[:, 40 + c:41 + c], S[u % 2][:, 0:w], AXX))
                        V.tensor_scalar(st[:, 8 + c:9 + c], st[:, 40 + c:41 + c], sink(u), -1.0,
                                        ALU.max, ALU.mult).then_inc(att_m, 1)
                    if u >= 2:
                        o = u - 2
                        c = o % 8
                        dve.wait_ge(att_p, base + o + 1)
                        link(V.tensor_tensor(st[:, 32 + c:33 + c], st[:, 16 + c:17 + c], st[:, 24 + c:25 + c], ALU.add))
                        link(V.reciprocal(st[:, 32 + c:33 + c], st[:, 32 + c:33 + c]))
                        dve.wait_ge(att_o, base + o + 1)
                        V.tensor_scalar(out_(o), mx[:, 3, HD * c:HD * c + HD], st[:, 32 + c:33 + c], None,
                                        ALU.mult).then_inc(att_d, 1)

            def rotate(dst1, dst2, v1, v2, t1, t2, both, cos, sin):
                V.tensor_tensor(t1[0], both, cos, ALU.mult)
                link(V.tensor_tensor(t2[0], both, sin, ALU.mult))
                V.tensor_tensor(dst1, t1[1], t2[2], ALU.subtract)
                return V.tensor_tensor(dst2, t1[2], t2[1], ALU.add)

            V.memset(eps[:, :], EPS)
            link(V.memset(conv_in[:, :, :], 0.0))
            dve.wait_ge(vcol_ps, 1)
            V.tensor_copy(vcols[:, :], mx[:, 0, 0:256]).then_inc(vcol_sb, 1)
            dve.wait_ge(vcol_sb, 1)
            TAU = 2.0 * np.pi
            parts = []
            left = TAU
            for bits in (8, 12):
                step = 2.0 ** (2 - bits - 6 * (bits == 12))
                parts.append(float(np.floor(left / step) * step))
                left -= parts[-1]
            parts.append(float(np.float32(left)))
            dve.wait_ge(pos_in, 16)
            posf, ang, turn = st[:, 500:502], st[:, 464:496].rearrange("p (t g f) -> p t g f", t=2, g=2), st[:, 48:64]
            link(V.tensor_copy(posf, pos_i[:, :]))
            dve.wait_ge(const_in, 32)
            V.tensor_copy(bconst[:, :], masks)
            a_sin, a_cos = ang[:, :, 1, :], ang[:, :, 0, :]
            t3 = turn.rearrange("p (t f) -> p t f", t=2)
            link(V.tensor_tensor(a_sin, rep(posf, 2, [P, 2, 8]), rep(const("inv"), 1, [P, 2, 8]), ALU.mult))
            link(V.tensor_scalar(t3, a_sin, float(np.float32(1.0 / TAU)), 12582912.0, ALU.mult, ALU.add))
            link(V.tensor_scalar(t3, t3, 12582912.0, None, ALU.subtract))
            for part in parts:
                link(V.scalar_tensor_tensor(a_sin, t3, -part, a_sin, ALU.mult, ALU.add))
            link(V.tensor_scalar(a_cos, a_sin, float(np.pi / 2), None, ALU.add))
            link(V.tensor_scalar(t3, a_cos, float(np.pi), -TAU, ALU.is_gt, ALU.mult))
            link(V.tensor_tensor(a_cos, a_cos, t3, ALU.add))
            V.tensor_scalar(ang[:, :, :, :], ang[:, :, :, :], 3.1415925, -3.1415925, ALU.min, ALU.max).then_inc(ang_ready, 1)
            m = st[:, 344:348]
            link(V.tensor_tensor(m, vcols[:, 248:252], vcols[:, 252:256], ALU.max))
            V.tensor_tensor(st[:, 328:336].rearrange("p (l h) -> p l h", l=2),
                            vcols[:, 248:256].rearrange("p (l h) -> p l h", l=2), rep(m, 1, [P, 2, 4]),
                            ALU.subtract).then_inc(lb_x, 1)
            dve.wait_ge(lb_e, 1)
            link(V.tensor_tensor(st[:, 348:352], st[:, 336:340], st[:, 340:344], ALU.add))
            link(V.reciprocal(st[:, 348:352], st[:, 348:352]))
            link(V.tensor_tensor(st[:, 348:352], st[:, 336:340], st[:, 348:352], ALU.mult))
            link(V.tensor_scalar(st[:, 344:348], st[:, 348:352], -0.5, 0.5, ALU.mult, ALU.add))
            link(V.tensor_tensor(st[:, 348:352], st[:, 348:352], st[:, 344:348], ALU.add))
            f_a, f_b = st[:, 344:348], st[:, 348:352]

            job_done("modB3", 1)
            mod_cols(0, 0, 16, 0)
            dve.wait_ge(x_in, 32)
            norm(0, BOTH, cat, 8, vcols[:, 96:104])
            dve.wait_ge(even_in, 64)
            for i in BOTH:
                job_done("even_k", i + 1)
                link(V.tensor_tensor(qk_t1, qk_raw[:, i, :], qk_raw[:, i, :], ALU.mult))
                ins = V.tensor_reduce(st[:, 80 + 10 * i:90 + 10 * i], qk_t1.rearrange("p (h d) -> p h d", h=10),
                                      axis=AXX, op=ALU.add)
                if i < 3:
                    link(ins)
                else:
                    ins.then_inc(qk_ss, 1)
            dve.wait_ge(qk_rs, 1)
            for i in BOTH:
                raw = qk_raw[:, i, :].rearrange("p (h d) -> p h d", h=10)
                t0 = qk_t0.rearrange("p (h d) -> p h d", h=10)
                link(V.tensor_tensor(t0, raw, rep(st[:, 120 + 10 * i:130 + 10 * i], 2, [P, 10, HD]), ALU.mult))
                if i >= 2:
                    dve.wait_ge(acc_full, pre.job["even_qkT"] + 2 * (i - 1))
                qp = qk_p[:, i % 2, 0:512].rearrange("p (j v d) -> p v j d", j=4, v=2)
                kp = qk_p[:, i % 2, 512:640].rearrange("p (v d) -> p v d", v=2)
                q0 = t0[:, 0:8, :].rearrange("p (v j) d -> p v j d", v=2)
                if i in CTX:
                    for v in range(2):
                        V.tensor_tensor(qp[:, v], q0[:, v], rep(erow[:, 0:HD], 1, [P, 4, HD]), ALU.mult)
                    V.tensor_tensor(kp, t0[:, 8:10, :], rep(erow[:, HD:2 * HD], 1, [P, 2, HD]),
                                    ALU.mult).then_inc(qk_ready, 1)
                    dve.wait_ge(qk_ready, i + 1)
                    continue
                V.tensor_tensor(t0[:, 0:8, :], t0[:, 0:8, :], rep(erow[:, 0:HD], 1, [P, 8, HD]), ALU.mult)
                link(V.tensor_tensor(t0[:, 8:10, :], t0[:, 8:10, :], rep(erow[:, HD:2 * HD], 1, [P, 2, HD]), ALU.mult))
                halves = qk_t0.rearrange("p (n d) -> p n d", d=32)
                t1h, t2h = qk_t1.rearrange("p (n d) -> p n d", d=32), qk_raw[:, i, :].rearrange("p (n d) -> p n d", d=32)
                rope = const("rope").rearrange("p (t f) -> p t f", t=2)[:, i - 2, :]
                V.tensor_tensor(t1h, halves, rep(rope[:, 0:32], 1, [P, 20, 32]), ALU.mult)
                link(V.tensor_tensor(t2h, halves, rep(rope[:, 32:64], 1, [P, 20, 32]), ALU.mult))
                c4 = qk_t1.rearrange("p (h g d) -> p h g d", g=2, d=32)
                s4 = qk_raw[:, i, :].rearrange("p (h g d) -> p h g d", g=2, d=32)
                for v in range(2):
                    hs = slice(4 * v, 4 * v + 4)
                    V.tensor_tensor(qp[:, v, :, 0:32], c4[:, hs, 0, :], s4[:, hs, 1, :], ALU.subtract)
                    V.tensor_tensor(qp[:, v, :, 32:64], c4[:, hs, 1, :], s4[:, hs, 0, :], ALU.add)
                V.tensor_tensor(kp[:, :, 0:32], c4[:, 8:10, 0, :], s4[:, 8:10, 1, :], ALU.subtract)
                V.tensor_tensor(kp[:, :, 32:64], c4[:, 8:10, 1, :], s4[:, 8:10, 0, :], ALU.add).then_inc(qk_ready, 1)
                dve.wait_ge(qk_ready, i + 1)
            win = const("win").rearrange("p (t k) -> p t k", t=2)
            attention(0, 32, lambda u: 2 if u < 16 else 4,
                      lambda u: win[:, 0, 0:256] if u < 16 else win[:, (u - 16) // 8, :],
                      lambda u: erow[:, 256 + u % 8:257 + u % 8], [eS[:, j, :] for j in range(2)],
                      lambda u: cat[:, u // 8, HD * (u % 8):HD * (u % 8) + HD])
            dve.wait_ge(att_d, 32)
            for d in range(2):
                V.memset(h_sc[d], 0.0)
                V.memset(h_S[d], 0.0)
            link(V.memset(st[:, 352:368], 0.0))
            scan = const("scan").rearrange("p (d t) -> p d t", d=2)
            for w in range(2 * HG):
                h, d = w // 2, w % 2
                f, kk = hf[d][:, h, :], h_kk[d]
                job_done("even_bf", HG * d + h + 1)
                if h:
                    dve.wait_ge(acc_full, pre.job[f"hg_o{h - 1}"] + 1)
                V.tensor_scalar(f, f, f_a[:, h:h + 1], f_b[:, h:h + 1], ALU.mult, ALU.add).then_inc(hg_f, 1)
                dve.wait_ge(hg_f, w + 1)
                V.tensor_scalar(kk, f, -1.0, 1.0, ALU.mult, ALU.add)
                dve.wait_ge(hg_lf, w + 1)
                lf, e = e_set[d][1], e_set[d]
                if d == 0:
                    link(V.tensor_tensor_scan(h_cum, scan[:, 0, :], lf, 0.0, ALU.mult, ALU.add))
                else:
                    link(V.tensor_tensor_scan(h_cum[:, ::-1], scan[:, 1, ::-1], lf[:, ::-1], 0.0, ALU.mult, ALU.add))
                cum = h_cum.rearrange("p (n t) -> p n t", t=64)
                ref, last = (32, 63) if d == 0 else (31, 0)
                V.tensor_tensor(e[0].rearrange("p (n t) -> p n t", t=64), cum,
                                cum[:, :, ref:ref + 1].to_broadcast([P, 8, 64]), ALU.subtract)
                V.tensor_tensor(e[3].rearrange("p (n t) -> p n t", t=64),
                                cum[:, :, last:last + 1].to_broadcast([P, 8, 64]), cum, ALU.subtract).then_inc(hg_cum, 1)
                dve.wait_ge(hg_e, w + 1)
                decay = st[:, 352 + 8 * d:360 + 8 * d]
                V.tensor_copy(decay, e[2].rearrange("p (n t) -> p n t", t=64)[:, :, last])
                V.tensor_tensor(e[0], e[0], hq[:, h, :], ALU.mult)
                def halves(v):
                    return v.rearrange("p (n g t) -> p n g t", g=2, t=32)

                V.memset(halves(h_kz)[:, :, 1 - d, :], 0.0)
                V.tensor_tensor(halves(h_kz)[:, :, d, :], halves(e[1])[:, :, d, :], halves(kk)[:, :, d, :], ALU.mult)
                link(V.tensor_tensor(e[3], e[3], kk, ALU.mult))
                V.tensor_tensor(e[1], e[1], kk, ALU.mult)
                V.tensor_tensor(e[2], e[2], hq[:, h, :], ALU.mult).then_inc(hg_prod, 1)
                dve.wait_ge(hg_s, w + 1)
                V.copy_predicated(h_sc[d], rep(bconst[:, P * d:P * (d + 1)], 1, [P, 4, P]),
                                  mx[:, 1, :].rearrange("p (t k) -> p t k", t=4)).then_inc(hg_ss, 1)
                dve.wait_ge(hg_u, w + 1)
                order = list(range(8)) if d == 0 else [3, 2, 1, 0, 7, 6, 5, 4]
                for n in range(7):
                    c, nxt = order[n], order[n + 1]
                    u_ps = mx[:, 2 + c % 2, P * (c // 2):P * (c // 2 + 1)]
                    if n == 0:
                        ins = V.tensor_copy(h_S[d][:, nxt, :], u_ps)
                    else:
                        ins = V.scalar_tensor_tensor(h_S[d][:, nxt, :], h_S[d][:, c, :], decay[:, c:c + 1], u_ps,
                                                     ALU.mult, ALU.add)
                    if n < 6:
                        link(ins)
                ins.then_inc(hg_st, 1)
            bl = cat[:, :, 512:1024]
            job_done("hg_o3", 1)
            link(V.tensor_tensor(o_sq, bl, bl, ALU.mult))
            V.tensor_reduce(st[:, 368:384], o_sq.rearrange("p t (h e) -> p (t h) e", h=4), axis=AXX, op=ALU.add).then_inc(hg_osq, 1)
            dve.wait_ge(hg_ors, 1)
            for i in BOTH:
                o3 = bl[:, i, :].rearrange("p (h e) -> p h e", h=4)
                link(V.tensor_tensor(o3, o3, rep(st[:, 384 + 4 * i:388 + 4 * i], 2, [P, 4, P]), ALU.mult))
                link(V.tensor_tensor(o3, o3, rep(erow[:, 128:256], 1, [P, 4, P]), ALU.mult))
                ins = V.tensor_tensor(bl[:, i, :], bl[:, i, :], hg_[:, i, :], ALU.mult)
            ins.then_inc(cat_ready, 1)
            job_done("modB11", 1)
            mod_cols(0, 16, 32, 0)
            gates("gate0", (1, 0), 16)
            residual("even_out", BOTH, "gate0", 4)

            def feed_forward(use, n_tok, ffT, conv=None):
                for t in range(11):
                    for j in range(2):
                        b = 2 * t + j
                        if conv is not None:
                            job_done("up", 4 * t + j + 1)
                            since(dve, ff_silu, conv * KF, b - 1)
                            tap = [pcols[:, P + KF * k + b:P + KF * k + b + 1] for k in range(4)]
                            link(V.tensor_scalar(c_buf[:, j, :], conv_in[:, j, 1:257], tap[0], tap[3], ALU.mult, ALU.add))
                            link(V.scalar_tensor_tensor(c_buf[:, j, :], conv_in[:, j, 2:258], tap[1], c_buf[:, j, :],
                                                        ALU.mult, ALU.add))
                            V.scalar_tensor_tensor(c_buf[:, j, :], conv_in[:, j, 3:259], tap[2], c_buf[:, j, :],
                                                   ALU.mult, ALU.add).then_inc(ff_conv, 1)
                    for j in range(2):
                        b = 2 * t + j
                        if conv is not None:
                            dve.wait_ge(ff_silu, conv * KF + b + 1)
                            job_done("up", 4 * t + j + 3)
                        else:
                            job_done(f"ffn{use}", 4 * t + j + 3)
                        V.tensor_tensor(ffT[:, b, :], g_buf[:, j, 0:n_tok], u_buf[:, j, 0:n_tok],
                                        ALU.mult).then_inc(ff_mul, 1)

            dve.wait_ge(y_used, 8)
            norm(1, BOTH, f_xs4, 32, vcols[:, 104:112])
            feed_forward(0, 512, ffT4)
            gates("gate1", (1, 0), 40)
            residual("down0", BOTH, "gate1", 4)
            job_done("modB23", 1)
            mod_cols(1, 0, 48, 0 + 48)
            dve.wait_ge(y_used, 16)
            norm(2, BOTH, r_xs, 8, vcols[:, 112:120])
            rr = const("ret_rope")
            cos, sin = rep(rr[:, 0:256], 1, [P, 2, 256]), rep(rr[:, 256:512], 1, [P, 2, 256])
            rt_c, rt_s = r_t[:, 0], r_t[:, 1]
            for h in range(RET):
                for last, v in enumerate((rq[:, 2 * h:2 * h + 2, :], rk[:, 2 * h:2 * h + 2, 256:512])):
                    job_done("ret_k", 2 * h + 2)
                    V.tensor_tensor(rt_c, v, cos, ALU.mult)
                    link(V.tensor_tensor(rt_s, v, sin, ALU.mult))
                    V.tensor_tensor(v[:, 0, :], rt_c[:, 0, :], rt_s[:, 1, :], ALU.subtract)
                    ins = V.tensor_tensor(v[:, 1, :], rt_c[:, 1, :], rt_s[:, 0, :], ALU.add)
                    if not last:
                        link(ins)
                ins.then_inc(ret_rope, 1)
                dve.wait_ge(ret_rope, h + 1)
            job_done("ret_g", 8)
            for h in range(RET):
                dve.wait_ge(dtab_in[h % 2], 16 * (h // 2 + 1))
                if h >= 2:
                    dve.wait_ge(ret_o, 2 * (h - 1))
                for s2 in range(2):
                    dve.wait_ge(ret_s, 2 * h + s2 + 1)
                    V.tensor_tensor(r_P[:, h % 2, 2 * s2:2 * s2 + 2, :], mx[:, s2, :].rearrange("p (s t) -> p s t", s=2),
                                    r_D[:, h % 2, 2 * s2:2 * s2 + 2, :], ALU.mult).then_inc(ret_p, 1)
                for t in range(2):
                    n = 2 * h + t
                    dve.wait_ge(ret_rs, n + 1)
                    g = rg[:, t, 512 * h:512 * (h + 1)]
                    V.scalar_tensor_tensor(g, mx[:, 2 + t, :], st[:, 408 + n:409 + n], g,
                                           ALU.mult, ALU.mult).then_inc(ret_n, 1)
            gates("gate2", (0,), 16)
            residual("ret_out", LAT, "gate2", 2)
            dve.wait_ge(y_used, 20)
            norm(3, LAT, f_xs2, 32, vcols[:, 120:128])
            feed_forward(1, 256, ffT2)
            gates("gate3", (0,), 40)
            residual("down1", LAT, "gate3", 2)
            job_done("modB47", 1)

            with dve.Fori(0, DEPTH2) as l:
                loop[0] = l
                chain.enter(l, DVE_LINKS)
                uses.enter(0)
                link(V.tensor_tensor(mb[:, 0, :], modc[:, bass.ds(l + 2, 1), 0, :].rearrange("p o n -> p (o n)"),
                                     vcols[:, bass.ds(l * 48 + 128, 48)], ALU.add))
                job_done("param", 2)
                dve.wait_ge(y_used, l * 16 + 24)
                norm(l * 2 + 4, LAT, d_xs, 8, pcols[:, 96:104])
                dve.wait_ge(lbc_in, l * 96 + 96)
                for i in range(2):
                    job_done("swa_k", i + 1)
                    link(V.tensor_tensor(s_t1, sqk[:, i, :], sqk[:, i, :], ALU.mult))
                    ins = V.tensor_reduce(st[:, 80 + 18 * i:98 + 18 * i], s_t1.rearrange("p (h d) -> p h d", h=18),
                                          axis=AXX, op=ALU.add)
                    if i == 0:
                        link(ins)
                    else:
                        ins.then_inc(qk_ss, 1)
                for b in range(24):
                    job_done("dn_in", b + 1)
                    tap = [pcols[:, 24 * k + b:24 * k + b + 1] for k in range(4)]
                    o, src = dnf[:, b, :], conv_in[:, b % 2, :]
                    link(V.tensor_scalar(o, src[:, 0:256], tap[0], None, ALU.mult))
                    link(V.scalar_tensor_tensor(o, src[:, 1:257], tap[1], o, ALU.mult, ALU.add))
                    link(V.scalar_tensor_tensor(o, src[:, 2:258], tap[2], o, ALU.mult, ALU.add))
                    V.scalar_tensor_tensor(o, src[:, 3:259], tap[3], o, ALU.mult, ALU.add).then_inc(dc_conv, 1)
                dve.wait_ge(rope_ready, 1)
                dve.wait_ge(qk_rs, l + 2)
                for i in range(2):
                    raw = sqk[:, i, :].rearrange("p (h d) -> p h d", h=18)
                    link(V.tensor_tensor(raw, raw, rep(st[:, 120 + 18 * i:138 + 18 * i], 2, [P, 18, HD]), ALU.mult))
                    V.tensor_tensor(raw[:, 0:16, :], raw[:, 0:16, :], rep(brow[:, 16:80], 1, [P, 16, HD]), ALU.mult)
                    link(V.tensor_tensor(raw[:, 16:18, :], raw[:, 16:18, :], rep(brow[:, 80:144], 1, [P, 2, HD]), ALU.mult))
                    r1 = raw[:, :, 0:16].rearrange("p h (g f) -> p h g f", g=2)
                    c1 = s_t0[:, 0:288].rearrange("p (h g f) -> p h g f", h=18, g=2)
                    c2 = s_t1[:, 0:288].rearrange("p (h g f) -> p h g f", h=18, g=2)
                    for g in range(2):
                        V.tensor_tensor(c1[:, :, g, :], r1[:, :, g, :], rep(srope[:, i, 0:8], 1, [P, 18, 8]), ALU.mult)
                        ins = V.tensor_tensor(c2[:, :, g, :], r1[:, :, g, :], rep(srope[:, i, 8:16], 1, [P, 18, 8]), ALU.mult)
                    link(ins)
                    V.tensor_tensor(r1[:, :, 0, :], c1[:, :, 0, :], c2[:, :, 1, :], ALU.subtract)
                    link(V.tensor_tensor(r1[:, :, 1, :], c1[:, :, 1, :], c2[:, :, 0, :], ALU.add))
                    sp_ = s_p[:, i, 0:1024].rearrange("p (j v d) -> p v j d", j=8, v=2)
                    for v in range(2):
                        V.tensor_copy(sp_[:, v], raw[:, 8 * v:8 * v + 8, :])
                    V.tensor_copy(s_p[:, i, 1024:1152], sqk[:, i, 1024:1152]).then_inc(qk_ready, 1)
                swa = const("swa")
                attention(l * 32 + 32, 32, lambda u: 1 if u < 16 else 2,
                          lambda u: swa[:, 0:128] if u < 16 else swa[:, 128:384],
                          lambda u: brow[:, 144 + u % 16:145 + u % 16], [sS[:, j, :] for j in range(2)],
                          lambda u: oswa[:, u // 16, HD * (u % 16):HD * (u % 16) + HD])

                def half_gates(s, name):
                    job_done(name, 4)
                    link(V.tensor_scalar(s, s, 0.5, 0.5, ALU.mult, ALU.add))

                half_gates(sgb, "gate_b")
                for n in range(4):
                    h, t = n // 2, n % 2
                    u = uses.next()
                    job_done("swa_out", n + 1)
                    cols = slice(512 * h, 512 * h + 512)
                    V.tensor_tensor(yb[:, t, cols], ybuf[:, u % 2, :], sgb[:, t, cols], ALU.mult).then_inc(y_used, 1)
                for s in range(9):
                    if s < 8:
                        f = dnf[:, 2 * s:2 * s + 2, :]
                        dve.wait_ge(dc_silu, l * 24 + 2 * s + 2)
                        since(dve, l2_ps, l * 8, s - 1)
                        V.tensor_tensor(l2_sq[:, s % 2, :].rearrange("p (b t) -> p b t", b=2), f, f,
                                        ALU.mult).then_inc(l2_sqd, 1)
                    if s >= 1:
                        o = s - 1
                        f = dnf[:, 2 * o:2 * o + 2, :]
                        dve.wait_ge(l2_rsd, l * 8 + o + 1)
                        V.scalar_tensor_tensor(f, f, P ** -0.5 if o < 4 else 1.0,
                                               l2_rs[:, o % 2, :].rearrange("p (b t) -> p b t", b=2),
                                               ALU.mult, ALU.mult).then_inc(l2_done, 1)
                job_done("dn_ab", 2)
                two = [P, 2, 8]

                def s3(lo):
                    return st[:, lo:lo + 16].rearrange("p (t h) -> p t h", t=2)

                link(V.tensor_tensor(s3(248), dab[:, :, 0:8], rep(brow[:, 0:8], 1, two), ALU.add))
                link(V.tensor_scalar(s3(312), s3(248), -1.0, None, ALU.mult))
                V.tensor_tensor(s3(264), s3(248), s3(312), ALU.max).then_inc(gb_x, 1)
                dve.wait_ge(gb_e, l + 1)
                link(V.scalar_tensor_tensor(s3(248), s3(248), 0.0, s3(280), ALU.max, ALU.add))
                V.tensor_scalar(s3(216), s3(216), 1.0, None, ALU.add)
                link(V.scalar_tensor_tensor(s3(248), s3(248), -1.0, rep(st[:, 296:304], 1, two), ALU.mult, ALU.mult))
                V.tensor_copy(st[:, 64:80], st[:, 248:264]).then_inc(gc_in, 1)
                link(V.reciprocal(st[:, 216:232], st[:, 216:232]))
                dve.wait_ge(gc_in, l + 1)
                link(V.tensor_scalar(st[:, 232:248], st[:, 216:232], -1.0, None, ALU.mult))
                dve.wait_ge(gc_ps, l + 1)
                link(V.tensor_copy(st[:, 160:184], mx[:, 2, 0:24]))
                V.tensor_tensor(st[:, 208:216], st[:, 176:184], st[:, 160:168], ALU.subtract).then_inc(gc_sb, 1)
                dve.wait_ge(gc_e, l + 1)
                link(V.tensor_tensor(st[:, 304:312], st[:, 224:232], st[:, 192:200], ALU.mult))
                four = [P, 4, P]
                for hg in range(2):
                    for c in range(2):
                        g = 2 * hg + c
                        at = 8 * c + 4 * hg
                        gcol, beta = st[:, 160 + at:164 + at], st[:, 216 + at:220 + at]
                        V.tensor_tensor(t_in, rep(tri, 1, four), rep(st[:, 64 + at:68 + at], 2, four),
                                        ALU.mult).then_inc(tg_in, 1)
                        dve.wait_ge(tg_ps, l * 4 + g + 1)
                        later = mx[:, 3, :].rearrange("p (h t) -> p h t", h=4)
                        V.tensor_tensor(t_g, later, rep(const("incl"), 1, four), ALU.add)
                        for h in range(4):
                            ins = V.scalar_tensor_tensor(t_st[:, h, :], mx[:, 3, P * h:P * (h + 1)], -1.0, const("strict"),
                                                         ALU.mult, ALU.add)
                        link(ins)
                        V.tensor_tensor(t_g, t_g, rep(gcol, 2, four), ALU.subtract)
                        V.tensor_tensor(t_st, t_st, rep(gcol, 2, four), ALU.add).then_inc(dec_in, 1)
                        V.tensor_copy(dT[c], rep(ident, 1, four))
                        V.tensor_copy(dTT[c], rep(ident, 1, four))
                        dve.wait_ge(dec_e, l * 4 + g + 1)
                        dve.wait_ge(kq_ps, l * 4 + g + 1)
                        V.tensor_tensor(dQ[c], mx[:, 1, :].rearrange("p (h t) -> p h t", h=4), t_g, ALU.mult)
                        if c == 1:
                            V.tensor_tensor(qdec, qdec, dnf[:, 4 * hg:4 * hg + 4, P:2 * P], ALU.mult)
                        link(V.tensor_tensor(t_st, mx[:, 0, :].rearrange("p (h t) -> p h t", h=4), t_st, ALU.mult))
                        V.tensor_tensor(dL[c], t_st, rep(st[:, 232 + at:236 + at], 2, four), ALU.mult).then_inc(l_ready, 1)
                        by_tok = mx[:, 2, :].rearrange("p (h t) -> p h t", h=4)
                        dve.wait_ge(kv_ps, l * 8 + 2 * g + 1)
                        V.tensor_tensor(vb[c], by_tok, rep(beta, 2, four), ALU.mult).then_inc(kv_sb, 1)
                        dve.wait_ge(kv_ps, l * 8 + 2 * g + 2)
                        if c == 0:
                            V.tensor_tensor(kdec, by_tok, rep(st[:, 200 + 4 * hg:204 + 4 * hg], 2, four),
                                            ALU.mult).then_inc(kv_sb, 1)
                        else:
                            V.tensor_tensor(kbe, by_tok, rep(st[:, 304 + 4 * hg:308 + 4 * hg], 2, four),
                                            ALU.mult).then_inc(kv_sb, 1)
                    for level in range(7):
                        n = (hg * 7 + level) * 2
                        fill = bconst[:, 256 + 256 * level:512 + 256 * level]
                        for c in range(2):
                            at = 480 + 2 * level + c
                            dve.wait_ge(inv_t, l * 28 + n + c + 1)
                            V.memset(st[:, at:at + 1], 0.0)
                            V.copy_predicated(dTT[c], rep(fill[:, P:2 * P], 1, four),
                                              mx[:, 2, :].rearrange("p (h t) -> p h t", h=4))
                            V.copy_predicated(dT[c], rep(fill[:, 0:P], 1, four),
                                              mx[:, 3, :].rearrange("p (h t) -> p h t", h=4)).then_inc(inv_d, 1)
                    job_done("dn_z", 4)
                    for c in range(2):
                        n = 448 + 8 * hg + 4 * c
                        dve.wait_ge(dn_rs, l * 4 + 2 * hg + c + 1)
                        since(dve, dn_o, l * 4, 2 * hg + c)
                        link(V.tensor_tensor(o_t, mx[:, c, :].rearrange("p (h e) -> p h e", h=4), rep(st[:, n:n + 4], 2, four),
                                             ALU.mult))
                        link(V.tensor_tensor(o_t, o_t, rep(brow[:, 160:288], 1, four), ALU.mult))
                        z = dz[:, c, 512 * hg:512 * hg + 512].rearrange("p (h e) -> p h e", h=4)
                        V.tensor_tensor(z, z, o_t, ALU.mult).then_inc(dn_o, 1)
                half_gates(sga, "gate_a")
                for n in range(4):
                    h, t = n // 2, n % 2
                    u = uses.next()
                    job_done("dn_out", n + 1)
                    cols = slice(512 * h, 512 * h + 512)
                    link(V.tensor_tensor(ybuf[:, u % 2, :], ybuf[:, u % 2, :], sga[:, t, cols], ALU.mult))
                    V.tensor_tensor(yb[:, t, cols], yb[:, t, cols], ybuf[:, u % 2, :], ALU.add).then_inc(y_used, 1)
                gates("gate_mix", (0,), 16)
                residual("w_o", LAT, "gate_mix", 2)
                dve.wait_ge(y_used, l * 16 + 36)
                norm(l * 2 + 5, LAT, f_xs2, 32, pcols[:, 104:112])
                feed_forward(l + 2, 256, ffT2, conv=l)
                gates("gate_ffn", (0,), 40)
                residual("down", LAT, "gate_ffn", 2)
                chain.leave("VectorE")


_INS = [
    "x", "c", "ctx", "c_ctx", "mod_w", "mod_b", "norm_g", "ffn_w_in", "ffn_w_out", "even_w_in", "even_w_out",
    "attn_qk_norm_g", "attn_sink", "hgrn_out_norm_g", "hgrn_lb", "odd_w_in", "odd_w_out", "c_2", "positions_2",
    "w_ada_2", "b_ada_2", "norm_mix_2", "w_in_2", "dn_conv_2", "dn_a_log_2", "dn_dt_bias_2", "dn_norm_2",
    "w_dn_out_2", "swa_q_norm_2", "swa_k_norm_2", "swa_sinks_2", "w_swa_out_2", "w_o_2", "norm_ffn_2", "w_up_2",
    "ffn_conv_2", "ffn_conv_b_2", "w_down_2",
]


def kernel(**inputs):
    import concourse.bacc as bacc
    from concourse.bass_utils import run_bass_kernel_spmd

    nc = bacc.Bacc("TRN2", target_bir_lowering=False, num_devices=1)
    arrays = {name: np.ascontiguousarray(inputs[name]) for name in _INS}
    arrays["const_f"], arrays["const_b"], arrays["const_ret"] = shape_constants()
    aps = {n: nc.dram_tensor("in_" + n, v.shape, mybir.dt.from_np(v.dtype), kind="ExternalInput").ap() for n, v in arrays.items()}
    out = nc.dram_tensor("out", arrays["x"].shape, F32, kind="ExternalOutput").ap()
    first_then_second_block(nc, aps, out)
    return run_bass_kernel_spmd(nc, [{"in_" + n: v for n, v in arrays.items()}], core_ids=[0]).results[0]["out"]
```

```python
from contextlib import ExitStack

import numpy as np

import concourse.bass as bass
from concourse import mybir

F32 = mybir.dt.float32
I32 = mybir.dt.int32
U8 = mybir.dt.uint8
ALU = mybir.AluOpType
ACT = mybir.ActivationFunctionType
AXX = mybir.AxisListType.X

P = 128
D = 1024
KD = D // P
NT = 4
CTX, LAT, BOTH = (0, 1), (2, 3), (0, 1, 2, 3)
EPS = 1e-6
MOD_CHUNKS = 12
FF = 2816
KF = FF // P
FF_SPLIT = (8, 8, 6)
EVEN_HEADS, HD = 8, 64
HG = 4
RET = 4
DN = 8
SWA = 16
RING = 2
WT = KD * 512
EXP_LN = "natural_log_exp_and_others"
SILU_TANH = "silu_and_others"
NEG = -1e30


def shape_constants():
    f = np.float32
    t = np.arange(256)
    p, q = np.arange(P)[:, None], np.arange(P)[None, :]
    same64 = (p // 64) == (q // 64)
    inv = (10000.0 ** (-np.arange(16, dtype=f) / 16)).astype(f)
    ang = np.concatenate([(t // 64).astype(f)[:, None] * inv, (t % 64).astype(f)[:, None] * inv], axis=-1)
    rope = np.concatenate([np.cos(ang), np.sin(ang)], axis=-1).reshape(2, P, 64).transpose(1, 0, 2)
    theta = (1.0 / (10000.0 ** np.linspace(0.0, 1.0, 128, dtype=f))).astype(f)
    rang = theta[:, None] * t.astype(f)[None, :]
    ret_rope = np.concatenate([np.cos(rang), np.sin(rang)], axis=1)
    win = np.zeros((P, 2, 512), f)
    swa = np.concatenate([np.where(q > p, 0.0, NEG), np.where(q <= p, 0.0, NEG)], axis=1)
    for i in range(2):
        qt = (i * P + np.arange(P))[:, None]
        win[:, i, 256:] = np.where(np.abs(t[None, :] - qt) <= 128, 0.0, NEG)
    u = np.arange(64)
    scan = np.stack([u != 0, u != 63]).astype(f)
    f_const = np.concatenate(
        [
            np.eye(P), np.ones((P, P)), (p <= q), np.where(p <= q, 0.0, NEG), np.where(q < p, 0.0, NEG),
            rope.reshape(P, 128), ret_rope, win.reshape(P, 1024), swa,
            np.broadcast_to(scan.reshape(1, 128), (P, 128)),
            np.broadcast_to((500000.0 ** (-np.arange(8, dtype=f) / 8)).astype(f)[None, :], (P, 8)),
        ],
        axis=1,
    ).astype(f)
    masks = [same64 & (p <= q), same64 & (p >= q)]
    for level in range(7):
        b = 1 << level
        fill = (p // (2 * b) == q // (2 * b)) & (p // b % 2 == 1) & (q // b % 2 == 0)
        masks += [fill, fill.T]
    b_const = np.concatenate(masks, axis=1).astype(f)
    gamma = np.log(1.0 - 2.0 ** (-5.0 - np.arange(RET)))
    s, tt = np.arange(512)[:, None], t[None, :]
    ret = []
    for h in range(RET):
        a, b = gamma[h], gamma[RET - 1 - h]
        context = np.exp(a * (tt + 256.0 - s)) + np.exp(b * (256.0 - tt + s))
        d = tt - (s - 256.0)
        latent = np.where(d >= 0, np.exp(a * np.maximum(d, 0)), 0) + np.where(d <= 0, np.exp(b * np.maximum(-d, 0)), 0)
        ret.append(np.where(s < 256, context, latent) / 16.0)
    ret = np.stack(ret).reshape(RET, 4, P, 256).transpose(0, 2, 1, 3)
    return f_const, np.ascontiguousarray(b_const), np.ascontiguousarray(ret.astype(f))


F_COLS = {}
_at = 0
for _name, _n in (("ident", P), ("ones", P), ("tri", P), ("incl", P), ("strict", P), ("rope", 128),
                  ("ret_rope", 512), ("win", 1024), ("swa", 256), ("scan", 128), ("inv", 8)):
    F_COLS[_name] = (_at, _at + _n)
    _at += _n
F_WIDTH = _at


class Plan:

    def __init__(self):
        self.jobs, self.tiles, self.parts = 0, 0, 0
        self.job, self.tile, self.part = {}, {}, {}
        self.own = {}
        self.chunks = {}
        self.done = []

    def upto(self, stage, n):
        return self.own[stage][n - 1] + 1 if stage in self.own else self.job[stage] + n

    def start(self, stage):
        self.job[stage], self.tile[stage], self.part[stage] = self.jobs, self.tiles, self.parts

    def free_jobs(self, stage, n):
        self.start(stage)
        self.jobs += n

    def weights(self, stage, jobs_per_tile):
        self.start(stage)
        for n in jobs_per_tile:
            self.jobs += n
            self.tiles += 1
            self.done.append(("job", self.jobs))

    def down(self, stage, halves, groups, tok):
        self.start(stage)
        for _ in range(halves):
            for g in range(groups):
                self.tiles += 1
                if g < groups - 1:
                    self.parts += 1
                    self.done.append(("part", self.parts))
                else:
                    self.jobs += tok
                    self.done.append(("job", self.jobs))


MOD_START = [("A", 0), ("A", 1), ("B", 0), ("A", 2), ("B", 1), ("A", 3), ("B", 2), ("B", 3)]
MOD_FIRST, MOD_LAST = 4, 4 * MOD_CHUNKS
MOD_AFTER_JOB = {"even": (11, 18, 20, 22, 24, 26, 28, 30), "ffn0": tuple(range(1, 44, 2)),
                 "odd": tuple(range(8, 36, 2))}


def mod_conds(n):
    return 2 if n < 2 * MOD_CHUNKS else 1


def mod_steps(n):
    return sum(KD * mod_conds(c) for c in range(MOD_FIRST, n))


def make_plans():
    a = Plan()
    for kind, n in MOD_START:
        if kind == "A":
            a.weights(f"modA{n}", [1])
        else:
            a.free_jobs(f"modB{n}", 1)
    chunk = iter(range(MOD_FIRST, MOD_LAST))

    def mod(tile):
        n = next(chunk)
        a.chunks.setdefault(tile, []).append(n)
        a.free_jobs(f"mod{n}", 1)

    def tiles(where, stages):
        job = 0
        for name, jobs in stages:
            a.start(name)
            a.own[name] = []
            for n in jobs:
                for left in range(n, 0, -1):
                    a.own[name].append(a.jobs)
                    a.jobs += 1
                    if left == 1:
                        a.tiles += 1
                        a.done.append(("job", a.jobs))
                    if job in MOD_AFTER_JOB.get(where, ()):
                        mod(a.tiles - (left == 1))
                    job += 1

    a.free_jobs("norm0", KD)
    tiles("even", (("even_q", [4]), ("even_k", [4]), ("even_v", [4]), ("even_bq", [HG]), ("even_bf", [HG, HG]),
                   ("even_bi", [4]), ("even_bg", [4])))
    a.free_jobs("even_qkT", 2 * NT)
    a.free_jobs("att_catT", KD // 2)
    for h in range(HG):
        a.free_jobs(f"hg_o{h}", 1)
    a.free_jobs("hg_catT", KD // 2)
    a.free_jobs("gate0", 4)
    a.weights("even_out", [4, 4])
    a.free_jobs("norm1", KD)
    tiles("ffn0", (("ffn0", [4] * 11),))
    a.free_jobs("gate1", 4)
    a.down("down0", 2, 3, 4)
    a.free_jobs("norm2", KD)
    tiles("odd", (("ret_q", [4, 4]), ("ret_k", [4, 4]), ("ret_v", [4] * 4), ("ret_g", [2] * 4)))
    a.free_jobs("ret_oT", KD)
    a.free_jobs("gate2", 2)
    a.down("ret_out", 2, 2, 2)
    a.free_jobs("norm3", KD)
    a.weights("ffn1", [4] * 11)
    a.free_jobs("gate3", 2)
    a.down("down1", 2, 3, 2)
    assert next(chunk, None) is None

    b = Plan()
    b.free_jobs("param", 2)
    b.free_jobs("norm", KD)
    b.weights("swa_q", [2, 2])
    b.weights("swa_k", [2])
    b.weights("swa_v", [2])
    b.weights("dn_in", [4] * 6)
    b.weights("dn_ab", [2])
    b.free_jobs("swa_qkT", 6)
    b.weights("dn_z", [2, 2])
    b.free_jobs("swa_oT", KD)
    b.weights("swa_out", [2, 2])
    b.weights("gate_b", [2, 2])
    b.weights("gate_a", [2, 2])
    b.free_jobs("dn_oT", KD)
    b.weights("dn_out", [2, 2])
    b.free_jobs("mergeT", KD)
    b.free_jobs("gate_mix", 2)
    b.weights("w_o", [2, 2])
    b.free_jobs("norm_ffn", KD)
    b.weights("up", [4] * 11)
    b.free_jobs("gate_ffn", 2)
    b.down("down", 2, 3, 2)
    return a, b


def need(eng, sem, value):
    if isinstance(value, int) and value <= 0:
        return
    eng.wait_ge(sem, value)


def since(eng, sem, before, n):
    if n > 0:
        eng.wait_ge(sem, before + n)


class Chain:

    def __init__(self, eng, sem):
        self.eng, self.sem, self.n, self.base = eng, sem, 0, 0

    def link(self, ins):
        self.n += 1
        ins.then_inc(self.sem, 1)
        self.eng.wait_ge(self.sem, self.base + self.n)

    def enter(self, layer, per_layer):
        self.base, self.n, self.per = self.n + layer * per_layer, 0, per_layer

    def leave(self, name):
        assert self.n == self.per, f"{name}: {self.n} links in a layer"


class Cursor:

    def __init__(self):
        self.n, self.base = 0, 0

    def next(self):
        self.n += 1
        return self.n - 1

    def enter(self, base):
        self.n, self.base = 0, base


DVE_LINKS, ACT_LINKS = 294, 22
Y_USES = 12


def first_then_second_block(nc, a, out):
    pre, per = make_plans()
    DEPTH2 = a["w_in_2"].shape[0]

    with ExitStack() as ctx:
        def sb(name, shape, dt=F32):
            return ctx.enter_context(nc.sbuf_tensor(name, shape, dt))

        def sem(name):
            return ctx.enter_context(nc.semaphore(name))

        x = sb("x", [P, NT, D])
        hT = sb("hT", [P, KD, NT * P])
        ring = sb("ring", [P, RING, WT])
        gate = sb("gate", [P, 2, D])
        ybuf = sb("ybuf", [P, 2, 512])
        fconst = sb("fconst", [P, F_WIDTH])
        bconst = sb("bconst", [P, 2048], U8)
        vcols = sb("vcols", [P, 256])
        modc = sb("modc", [P, 4, 2, 48])
        mb = sb("mb", [P, 2, 48])
        ab = sb("ab", [P, 2, KD])
        mod_w = sb("mod_w", [P, 2, 2, 512])
        shared = sb("shared", [P, 1024])
        mod_acc = shared[:, :].rearrange("p (c n) -> p c n", c=2)
        conv_in = shared[:, 0:520].rearrange("p (j n) -> p j n", j=2)
        brow, pcols = shared[:, 520:808], shared[:, 808:1024]
        cond = sb("cond", [P, 2, KD, 2])
        st = sb("st", [P, 512])
        erow = sb("erow", [P, 264])
        dg = sb("dg", [P, 2, 512])
        eps = sb("eps", [P, 1])
        ARENA = 24576
        arena = sb("arena", [P, ARENA])

        def view(at, *shape):
            n = int(np.prod(shape))
            assert at + n <= ARENA, (at, shape)
            v = arena[:, at:at + n]
            if len(shape) == 1:
                return v
            names = "abcd"[:len(shape)]
            return v.rearrange(f"p ({' '.join(names)}) -> p {' '.join(names)}", **dict(zip(names, shape)))

        def const(name):
            lo, hi = F_COLS[name]
            return fconst[:, lo:hi]

        ident, ones, tri = const("ident"), const("ones"), const("tri")

        def over(v, shape):
            return v.to_broadcast(shape)

        acc = ctx.enter_context(nc.psum_tensor("acc", [P, 4, 512], F32))
        mx = ctx.enter_context(nc.psum_tensor("mx", [P, 4, 512], F32))

        hv, hg_, hq = view(0, 4, 512), view(2048, 4, 512), view(4096, 4, 512)
        rows = view(2048, 2, 512)[0:2]
        masks = view(0, 2048)
        hf = [view(6144, 4, 512), view(8192, 4, 512)]
        cat = view(10240, 4, 1024)
        A0 = 14336
        qk_raw, v_raw = view(A0, 4, 640), view(A0 + 2560, 4, 128)
        qk_t0, qk_t1 = view(A0 + 3072, 640), view(A0 + 3712, 640)
        qk_p = [view(A0 + 4352, 640), view(A0 + 4992, 640), gate[:, 0, 0:640], gate[:, 1, 0:640]]
        ekT, eqT = view(A0 + 5632, 512), view(A0 + 6144, 4, 512)
        eS, ePT = view(A0 + 8192, 2, 512), view(A0 + 9216, 2, 512)
        e_set = [[view(A0 + 2048 * d + 512 * j, 512) for j in range(4)] for d in range(2)]
        e_q = [[e_set[d][2] for d in range(2)], [gate[:, d, 0:512] for d in range(2)]]
        h_kk = [view(A0 + 4096 + 512 * d, 512) for d in range(2)]
        h_kd = view(A0 + 5632, 2, 4, 128)
        h_sc = [view(A0 + 6656 + 512 * d, 4, 128) for d in range(2)]
        h_S = [view(A0 + 7680 + 1024 * d, 8, 128) for d in range(2)]
        h_cum = [view(A0 + 5120, 512), mod_acc[:, 0, :]]
        h_kz = [view(A0 + 9728, 512), mod_acc[:, 1, :]]
        o_sq = gate[:, 0, 512:1024]
        ffT4, ffT2 = view(0, KF, 512), view(0, KF, 256)
        f_xs4, f_xs2 = view(11264, 4, 1024), view(5632, 2, 1024)
        g_buf, u_buf, c_buf = view(16384, 2, 512), view(17408, 3, 512), view(18944, 2, 256)
        rv, rg, rk, rq = view(0, 4, 2048), view(8192, 2, 2048), view(12288, 8, 512), view(16384, 8, 256)
        r_t = view(18432, 2, 2, 256)
        r_P, r_D, r_junk = view(19456, 2, 4, 256), view(21504, 2, 4, 256), view(23552, 512)
        r_xs = view(0, 4, 1024)
        d_xs, dnf = view(0, 2, 1024), view(0, 24, 256)
        sqk, s_v = view(6144, 2, 1152), view(8448, 2, 128)
        s_t0, s_t1, s_p = view(8704, 1152), view(9856, 1152), view(11008, 2, 1152)
        sqT, skT = view(13312, 8, 256), view(15360, 256)
        sS, sPT, oswa = view(15616, 2, 256), view(16128, 2, 256), view(16640, 2, 1024)
        sgb, yb = view(18688, 2, 1024), view(20736, 2, 1024)
        dz, sga = view(6144, 2, 1024), x[:, 0:2, :]
        B0 = 8192
        dL, dT, dTT, dQ, dY = ([view(B0 + 1024 * j + 512 * c, 4, 128) for c in range(2)] for j in range(5))
        t_in, t_st = view(B0 + 5120, 4, 128), view(B0 + 5632, 4, 128)
        t_g, kdec, kbe = view(B0 + 6144, 4, 128), view(B0 + 6656, 4, 128), view(B0 + 7168, 4, 128)
        dS, nwT, qdec, o_t = (view(B0 + 7680 + 512 * j, 4, 128) for j in range(4))
        vb = [view(17920, 4, 128), view(22784, 4, 128)]
        vn = [view(23296 + 512 * c, 4, 128) for c in range(2)]
        l2_sq, l2_rs = view(B0, 2, 512), view(B0 + 1024, 2, 512)
        srope = sb("srope", [P, 2, 16])
        prow = sb("prow", [P, 2, P])
        dab = st[:, 328:360].rearrange("p (t n) -> p t n", t=2)
        pos_i = sb("pos_i", [P, 2], I32)

        ident_in = sem("ident_in")
        const_in, rows_in, x_in, even_in = sem("const_in"), sem("rows_in"), sem("x_in"), sem("even_in")
        lrow_in, lbc_in, pos_in = sem("layer_rows_in"), sem("layer_bcast_in"), sem("positions_in")
        dtab_in = [sem("dtab0_in"), sem("dtab1_in")]
        mod_in, mod_sum = [sem("mod0_in"), sem("mod1_in")], sem("mod_sum")
        out_stored = sem("out_stored")
        w_in = [sem(f"weights{s}_in") for s in range(RING)]
        w_part = sem("weights_partly_used")
        acc_full, acc_done = sem("acc_full"), sem("acc_done")
        vcol_ps, vcol_sb, cond_e, cond_ready = sem("vcol_ps"), sem("vcol_sb"), sem("cond_e"), sem("cond_ready")
        dve_chain, act_chain = sem("dve_chain"), sem("act_chain")
        setup_done = sem("setup_done")
        ang_ready, rope_ready = sem("ang_ready"), sem("rope_ready")
        norm_rs, norm_xs, norm_ab = sem("norm_rs"), sem("norm_xs"), sem("norm_ab")
        dg_ready, y_used = sem("dg_ready"), sem("y_used")
        qk_ss, qk_rs, qk_ready = sem("qk_ss"), sem("qk_rs"), sem("qk_ready")
        att_s, att_m, att_p, att_t, att_pt, att_o, att_d = (sem(f"att_{n}") for n in (
            "scores", "shifted", "probs", "transposed", "pt_copied", "out_ps", "out_done"))
        lb_x, lb_e = sem("lb_x"), sem("lb_e")
        hg_f, hg_lf, hg_cum, hg_e, hg_prod = (sem(f"hg_{n}") for n in ("f", "logf", "cum", "exps", "products"))
        hg_kt, hg_kts, hg_s, hg_ss, hg_u, hg_st = (sem(f"hg_{n}") for n in (
            "kd_ps", "kd_sb", "scores_ps", "scores_sb", "updates", "states"))
        hg_osq, hg_ors, cat_ready = sem("hg_out_ss"), sem("hg_out_rs"), sem("cat_ready")
        ff_conv, ff_silu, ff_mul = sem("ff_conv"), sem("ff_silu"), sem("ff_mul")
        ret_rope, ret_s, ret_p, ret_o, ret_rs, ret_n = (sem(f"ret_{n}") for n in (
            "roped", "scores", "weighted", "out_ps", "rstd", "normed"))
        lcol_ps, lcol_sb = sem("layer_cols_ps"), sem("layer_cols_sb")
        dc_conv, dc_silu = sem("dn_conv"), sem("dn_silu")
        l2_sqd, l2_ps, l2_rsd, l2_done = sem("l2_sq"), sem("l2_ps"), sem("l2_rs"), sem("l2_done")
        gb_x, gb_e, gc_in, gc_ps, gc_sb, gc_e = (sem(f"dn_{n}") for n in (
            "gate_x", "gate_e", "g", "cum_ps", "cum_sb", "cum_e"))
        tg_in, tg_ps, dec_in, dec_e = sem("dn_tri_g"), sem("dn_cum_rows"), sem("dn_decay_in"), sem("dn_decay")
        kq_ps, l_ready, kv_ps, kv_sb = sem("dn_kk_qk"), sem("dn_triangle"), sem("dn_kv_ps"), sem("dn_kv_sb")
        inv_y, inv_ys, inv_t, inv_d = (sem(f"inv_{n}") for n in ("y_ps", "y_sb", "t_ps", "t_sb"))
        dz_ready, mix_ready = sem("dn_z_ready"), sem("mix_gates_ready")
        fin_ps, fin_sb, dn_rs, dn_o = sem("dn_fin_ps"), sem("dn_fin_sb"), sem("dn_out_rs"), sem("dn_out_done")

        def wcols(w, lo, hi):
            return w.rearrange("(k p) n -> p k n", p=P)[:, :, lo:hi]

        block = ctx.enter_context(nc.Block())

        @block.sync
        def _(sp):
            tile, piece = Cursor(), Cursor()
            PIECES = KD // 2

            def load_chunk(n):
                layer, c = n // MOD_CHUNKS, n % MOD_CHUNKS
                w = a["mod_w"][layer] if layer < 2 else a["w_ada_2"][layer - 2]
                for g in range(PIECES):
                    i = piece.next()
                    if i >= 2:
                        m, read = MOD_FIRST + (i - 2) // PIECES, (i - 2) % PIECES + 1
                        sp.wait_ge(mod_sum, mod_steps(m) + 2 * mod_conds(m) * read)
                    sp.dma_start(mod_w[:, i % 2], wcols(w, 512 * c, 512 * c + 512)[:, 2 * g:2 * g + 2, :]).then_inc(
                        mod_in[i % 2], 16)

            def load(*parts, in_loop=None):
                t = tile.next()
                if in_loop is None:
                    for n in pre.chunks.get(t - 1, ())[:1]:
                        load_chunk(n)
                    slot = t % RING
                    if t >= RING:
                        kind, n = pre.done[t - RING]
                        sp.wait_ge(acc_full if kind == "job" else w_part, n)
                else:
                    slot = (pre.tiles + t) % RING
                    kind, n = per.done[t - RING] if t >= RING else last[t]
                    if kind == "job":
                        sp.wait_ge(acc_full, in_loop * per.jobs + (pre.jobs + n))
                    else:
                        sp.wait_ge(w_part, in_loop * per.parts + (pre.parts + n))
                width = at = sum(q.shape[2] for q in parts)
                for p in reversed(parts):
                    k, n = p.shape[1], p.shape[2]
                    at -= n
                    dst = ring[:, slot, 0:k * width].rearrange("p (k n) -> p k n", k=k)[:, :, at:at + n]
                    sp.dma_start(dst, p).then_inc(w_in[slot], 16 if len(parts) == 2 else 32)
                if in_loop is None:
                    for n in pre.chunks.get(t - 1, ())[1:]:
                        load_chunk(n)

            for c in range(MOD_FIRST):
                load(wcols(a["mod_w"][0], 512 * c, 512 * c + 512))
            ew = a["even_w_in"][0]
            for lo, hi in ((0, 512), (512, 640), (640, 768), (768, 1280), (1280, 1792), (1792, 2304),
                           (2304, 2816), (2816, 3328)):
                load(wcols(ew, lo, hi))
            for h in range(2):
                load(wcols(a["even_w_out"][0], 512 * h, 512 * h + 512))

            def feed_forward(w_up, w_down, in_loop=None):
                for b in range(11):
                    load(wcols(w_up, 256 * b, 256 * b + 256), wcols(w_up, FF + 256 * b, FF + 256 * b + 256),
                         in_loop=in_loop)
                for h in range(2):
                    at = 0
                    for n in FF_SPLIT:
                        load(wcols(w_down[P * at:P * (at + n), :], 512 * h, 512 * h + 512), in_loop=in_loop)
                        at += n

            feed_forward(a["ffn_w_in"][0], a["ffn_w_out"][0])
            for c in range(12):
                load(wcols(a["odd_w_in"][0], 512 * c, 512 * c + 512))
            for h in range(2):
                for g in range(2):
                    load(wcols(a["odd_w_out"][0][D * g:D * (g + 1), :], 512 * h, 512 * h + 512))
            feed_forward(a["ffn_w_in"][1], a["ffn_w_out"][1])
            assert tile.n == pre.tiles

            last = [(kind, n - {"job": p.jobs, "part": p.parts}[kind]) for p in (pre,) for kind, n in p.done[-RING:]]
            assert last == [(kind, n - {"job": per.jobs, "part": per.parts}[kind]) for kind, n in per.done[-RING:]]
            with sp.Fori(0, DEPTH2) as l:
                def of(name):
                    w = a[name]
                    rest = "abc"[:len(w.shape) - 1]
                    return w[bass.ds(l, 1)].rearrange(f"o {' '.join(rest)} -> (o {rest[0]}) {' '.join(rest[1:])}")

                tile.enter(0)
                for dst, src in (
                    (prow[0:96, 0, :], of("dn_conv_2").rearrange("k (b p) -> (k b) p", p=P)),
                    (prow[96:104, 0, :], a["norm_mix_2"][bass.ds(l, 1)].rearrange("o (b p) -> (o b) p", p=P)),
                    (prow[104:112, 0, :], a["norm_ffn_2"][bass.ds(l, 1)].rearrange("o (b p) -> (o b) p", p=P)),
                    (prow[0:66, 1, :], of("ffn_conv_2").rearrange("k (b p) -> (k b) p", p=P)),
                    (prow[66:88, 1, :], a["ffn_conv_b_2"][bass.ds(l, 1)].rearrange("o (b p) -> (o b) p", p=P)),
                ):
                    sp.dma_start(dst, src).then_inc(lrow_in, 16)
                at = 0
                for name in ("dn_dt_bias_2", "dn_a_log_2", "swa_q_norm_2", "swa_k_norm_2", "swa_sinks_2", "dn_norm_2"):
                    n = a[name].shape[1]
                    sp.dma_start(brow[:, at:at + n], a[name][bass.ds(l, 1)].to_broadcast([P, n])).then_inc(lbc_in, 16)
                    at += n
                w = of("w_in_2")
                for lo, n in ((4112, 512), (4624, 512), (5136, 128), (5264, 128), (0, 512), (512, 512), (1024, 512),
                              (1536, 512), (2048, 512), (2560, 512), (4096, 16), (3072, 512), (3584, 512)):
                    if lo:
                        load(wcols(w, lo, lo + n), in_loop=l)
                    else:
                        load(wcols(w, 0, n // 2), wcols(w, n // 2, n), in_loop=l)
                for h in range(2):
                    load(wcols(of("w_swa_out_2"), 512 * h, 512 * h + 512), in_loop=l)
                for lo in (6416, 6928, 5392, 5904):
                    load(wcols(w, lo, lo + 512), in_loop=l)
                for name in ("w_dn_out_2", "w_o_2"):
                    for h in range(2):
                        load(wcols(of(name), 512 * h, 512 * h + 512), in_loop=l)
                feed_forward(of("w_up_2"), of("w_down_2"), in_loop=l)
                assert tile.n == per.tiles

            sp.wait_ge(y_used, 24 + Y_USES * DEPTH2)
            sp.dma_start(out[0].rearrange("(t p) d -> p t d", p=P), x[:, 2:4, :]).then_inc(out_stored, 16)
            sp.wait_ge(out_stored, 16)

        @block.tensor
        def _(pe):
            job, tile, chunk, own, filling = Cursor(), Cursor(), Cursor(), Cursor(), Cursor()
            chunk.n = MOD_FIRST
            loop = [None]

            def weights(width, k=KD):
                t = tile.next()
                if loop[0] is None:
                    slot = t % RING
                    pe.wait_ge(w_in[slot], 32 * (t // RING + 1))
                else:
                    slot = (pre.tiles + t) % RING
                    pe.wait_ge(w_in[slot], loop[0] * (32 * per.tiles // RING) + 32 * ((pre.tiles + t) // RING + 1))
                return ring[:, slot, 0:k * width].rearrange("p (k n) -> p k n", k=k)

            def bank():
                n = job.next()
                if loop[0] is None:
                    need(pe, acc_done, n - 3)
                else:
                    pe.wait_ge(acc_done, job.base + (n - 3 if n >= 4 else 0))
                return acc[:, n % 4, :]

            def done(n):
                need(pe, acc_done, job.base + n)

            def stage(name):
                p = pre if loop[0] is None else per
                assert (job.n, tile.n) == (p.job[name], p.tile[name]), (name, job.n, tile.n, p.job[name], p.tile[name])

            def by_token(tiles, width, src=hT, where=None):
                w = weights(width)
                for i in tiles:
                    b = bank()
                    for k in range(KD):
                        ins = nc.tensor.matmul(b[:, 0:width], src[:, k, P * i:P * (i + 1)], w[:, k, :],
                                               start=k == 0, stop=k == KD - 1)
                    ins.then_inc(acc_full, 1)
                    mod_after(where)

            def by_feature(blocks, lo, hi, where=None):
                w = weights(P * blocks)
                for f in range(blocks):
                    b = bank()
                    for k in range(KD):
                        ins = nc.tensor.matmul(b[:, 0:hi - lo], w[:, k, P * f:P * (f + 1)], hT[:, k, lo:hi],
                                               start=k == 0, stop=k == KD - 1)
                    ins.then_inc(acc_full, 1)
                    mod_after(where)

            def fill(n, src, tiles):
                for _ in range(n):
                    s = filling.next()
                    k, i = s % KD, tiles[s // KD % 2]
                    if s % 16 == 0:
                        filling.w = weights(512)
                    if k == 0:
                        filling.b = bank()
                    ins = nc.tensor.matmul(filling.b, src[:, k, P * i:P * (i + 1)], filling.w[:, k, :],
                                           start=k == 0, stop=k == KD - 1)
                    if k == KD - 1:
                        ins.then_inc(acc_full, 1)

            def down(src, groups, tiles, ready):
                for h in range(2):
                    banks = [bank() for _ in tiles]
                    at = 0
                    for g, n in enumerate(groups):
                        ready(at + n)
                        w = weights(512, n)
                        for b, i in zip(banks, tiles):
                            for k in range(n):
                                ins = nc.tensor.matmul(b, src[:, at + k, P * i:P * (i + 1)], w[:, k, :],
                                                       start=at + k == 0, stop=at + k == sum(groups) - 1)
                            if g == len(groups) - 1:
                                ins.then_inc(acc_full, 1)
                        if g < len(groups) - 1:
                            ins.then_inc(w_part, 1)
                        at += n

            def transposed(src, tiles, blocks=1, first=0, last=KD):
                for k in range(first * blocks, last * blocks, blocks):
                    b = bank()
                    for q in range(blocks):
                        for j, i in enumerate(tiles):
                            at = P * (q * len(tiles) + j)
                            ins = nc.tensor.transpose(b[:, at:at + P], src[:, i, P * (k + q):P * (k + q + 1)], ident)
                    ins.then_inc(acc_full, 1)

            def mod_start():
                for kind, n in MOD_START:
                    stage(f"mod{kind}{n}")
                    if kind == "A":
                        w = weights(512)
                        b = bank()
                        for k in range(KD):
                            ins = nc.tensor.matmul(b[0:2, :], cond[:, n // 24, k, :], w[:, k, :],
                                                   start=k == 0, stop=k == KD - 1)
                    else:
                        b = bank()
                        done(pre.job[f"modA{n}"] + 1)
                        for q in range(4):
                            ins = nc.tensor.matmul(b[:, 2 * q:2 * q + 2], rows[:, n % 2, P * q:P * (q + 1)],
                                                   ident[0:2, 0:2], start=True, stop=True)
                    ins.then_inc(acc_full, 1)

            def mod():
                n = chunk.next()
                assert job.n == pre.job[f"mod{n}"]
                b = bank()
                pe.wait_ge(mod_sum, mod_steps(n + 1))
                for c in range(mod_conds(n)):
                    for q in range(4):
                        ins = nc.tensor.matmul(b[:, 4 * c + q:4 * c + q + 1], mod_acc[:, c, P * q:P * (q + 1)],
                                               ones[:, 0:1], start=True, stop=True)
                ins.then_inc(acc_full, 1)

            def mod_after(where):
                if where and own.next() in MOD_AFTER_JOB[where]:
                    mod()

            def norm(use, tiles, name):
                stage(name)
                pe.wait_ge(norm_xs, use + 1)
                xs = {0: cat, 1: f_xs4, 2: r_xs, 3: f_xs2}[use] if isinstance(use, int) else None
                return xs

            def gates(jobs, base):
                for s in range(jobs):
                    b = bank()
                    pe.wait_ge(dg_ready, base + s + 1)
                    nc.tensor.matmul(b, ones, dg[:, s % 2, :], start=True, stop=True).then_inc(acc_full, 1)

            def attention(base, units, fill):
                n = len(units)
                for u in range(n + 2):
                    if u < n:
                        q, k, blocks, v = units[u]
                        since(pe, att_m, base, u - 1)
                        nc.tensor.matmul(mx[:, u % 2, 0:P * blocks], q, k, start=True, stop=True).then_inc(att_s, 1)
                    if 1 <= u <= n:
                        blocks = units[u - 1][2]
                        pe.wait_ge(att_p, base + u)
                        since(pe, att_pt, base, u - 1)
                        for j in range(blocks):
                            ins = nc.tensor.transpose(mx[:, 2, P * j:P * (j + 1)], att_S[(u - 1) % 2][:, P * j:P * (j + 1)],
                                                      ident)
                        ins.then_inc(att_t, 1)
                    if u >= 2:
                        o, (_, _, blocks, v) = u - 2, units[u - 2]
                        pe.wait_ge(att_pt, base + o + 1)
                        since(pe, att_d, base, o)
                        for j in range(blocks):
                            ins = nc.tensor.matmul(mx[:, 3, HD * (o % 8):HD * (o % 8 + 1)],
                                                   att_PT[o % 2][:, P * j:P * (j + 1)], v[j],
                                                   start=j == 0, stop=j == blocks - 1)
                        ins.then_inc(att_o, 1)
                    fill(u)

            pe.wait_ge(ident_in, 16)
            pe.wait_ge(rows_in, 16 * 7)
            for j in range(2):
                ins = nc.tensor.transpose(mx[:, 0, P * j:P * (j + 1)], dg[:, j, 0:P], ident)
            ins.then_inc(vcol_ps, 1)
            pe.wait_ge(cond_ready, 1)
            mod_start()
            transposed(norm(0, BOTH, "norm0"), BOTH)
            stage("even_q")
            done(pre.job["norm0"] + KD)
            for width in (512, P, P):
                by_token(BOTH, width, where="even")
            for _ in range(3):
                by_feature(HG, 0, 512, where="even")
            for _ in range(2):
                by_token(BOTH, 512, where="even")
            stage("even_qkT")
            for i in BOTH:
                pe.wait_ge(qk_ready, i + 1)
                b = bank()
                for j in range(4):
                    ins = nc.tensor.transpose(b[:, P * j:P * (j + 1)], qk_p[i][:, P * j:P * (j + 1)], ident)
                ins.then_inc(acc_full, 1)
                b = bank()
                nc.tensor.transpose(b[:, 0:P], qk_p[i][:, 512:640], ident).then_inc(acc_full, 1)
            done(pre.job["even_qkT"] + 2 * NT)
            units = []
            att_S, att_PT = [eS[:, j, :] for j in range(2)], [ePT[:, j, :] for j in range(2)]
            for i in BOTH:
                for kv in range(2):
                    for j in range(4):
                        half = slice(HD * kv, HD * kv + HD)
                        blocks = 2 if i in CTX else 4
                        units.append((eqT[half, j, P * i:P * (i + 1)], ekT[half, 0:P * blocks], blocks,
                                      [v_raw[:, t, HD * kv:HD * kv + HD] for t in range(blocks)]))
            attention(0, units, lambda u: None)
            stage("att_catT")
            pe.wait_ge(att_d, 32)
            transposed(cat, BOTH, last=KD // 2)
            for h in range(HG):
                def keys_by_token(d):
                    pe.wait_ge(hg_prod, 2 * h + d + 1)
                    need(pe, hg_kts, 2 * h + d)
                    kd = e_set[d][3]
                    for t in range(NT):
                        ins = nc.tensor.transpose(mx[:, 0, P * t:P * (t + 1)], kd[:, P * t:P * (t + 1)], ident)
                    ins.then_inc(hg_kt, 1)

                def scores(d):
                    need(pe, hg_ss, 2 * h + d)
                    for t in range(NT):
                        s = slice(P * t, P * (t + 1))
                        for early in (True, False):
                            at = 32 * (early == (d == 1))
                            q = e_set[d][0][:, s].rearrange("p (n t) -> p n t", t=64)[:, :, at:at + 32]
                            o = mx[:, 1, s].rearrange("p (n t) -> p n t", t=64)[:, :, at:at + 32]
                            ins = nc.tensor.matmul(o, (h_kz[d] if early else e_set[d][1])[:, s], q, start=True, stop=True)
                    ins.then_inc(hg_s, 1)

                def updates(d):
                    w = 2 * h + d
                    pe.wait_ge(hg_kts, w + 1)
                    need(pe, hg_st, w)
                    for c in range(8):
                        half = slice(64 * (c % 2), 64 * (c % 2) + 64)
                        ins = nc.tensor.matmul(mx[:, 2 + c % 2, P * (c // 2):P * (c // 2 + 1)], h_kd[half, d, c // 2, :],
                                               hv[half, c // 2, P * h:P * (h + 1)], start=True, stop=True)
                    ins.then_inc(hg_u, 1)

                keys_by_token(0)
                scores(0)
                updates(0)
                keys_by_token(1)
                scores(1)
                updates(1)
                stage(f"hg_o{h}")
                b = bank()
                pe.wait_ge(hg_ss, 2 * h + 2)
                pe.wait_ge(hg_st, 2 * h + 2)
                for t in range(NT):
                    v = hv[:, t, P * h:P * (h + 1)]
                    nc.tensor.matmul(b[:, P * t:P * (t + 1)], h_sc[0][:, t, :], v, start=True, stop=False)
                    nc.tensor.matmul(b[:, P * t:P * (t + 1)], h_sc[1][:, t, :], v, start=False, stop=False)
                    for c in (2 * t, 2 * t + 1):
                        half = slice(64 * (c % 2), 64 * (c % 2) + 64)
                        for dd, first in ((0, c == 0), (1, c == 3)):
                            if not first:
                                ins = nc.tensor.matmul(b[half, P * t:P * (t + 1)], e_q[h % 2][dd][:, 64 * c:64 * c + 64],
                                                       h_S[dd][:, c, :], start=False, stop=dd == (c != 3))
                ins.then_inc(acc_full, 1)
            pe.wait_ge(cat_ready, 1)
            stage("hg_catT")
            transposed(cat, BOTH, first=KD // 2)
            gates(4, 0)
            stage("even_out")
            done(pre.job["hg_catT"] + KD // 2)
            by_token(BOTH, 512)
            by_token(BOTH, 512)

            def feed_forward(name, use, ffT, lo, hi, tiles, gate_base):
                stage(name)
                own.n = 0
                for _ in range(11):
                    by_feature(4, lo, hi, where="ffn0" if name == "ffn0" else None)
                gates(4 if len(tiles) == 4 else 2, gate_base)
                down(ffT, FF_SPLIT, tiles, lambda n: pe.wait_ge(ff_mul, use * KF + n))

            transposed(norm(1, BOTH, "norm1"), BOTH)
            done(pre.job["norm1"] + KD)
            feed_forward("ffn0", 0, ffT4, 0, 512, BOTH, 4)
            transposed(norm(2, BOTH, "norm2"), BOTH)
            done(pre.job["norm2"] + KD)
            own.n = 0
            for lo in (256, 256, 0, 0):
                by_feature(4, lo, 512, where="odd")
            for tok in (BOTH,) * 4 + (LAT,) * 4:
                by_token(tok, 512, where="odd")
            done(pre.upto("ret_v", 16))
            for h in range(RET):
                pe.wait_ge(ret_rope, h + 1)
                for s2 in range(2):
                    need(pe, ret_p, 2 * h - 1 + s2)
                    for s in (2 * s2, 2 * s2 + 1):
                        for k in range(2):
                            ins = nc.tensor.matmul(mx[:, s2, 256 * (s % 2):256 * (s % 2) + 256],
                                                   rk[:, 2 * h + k, P * s:P * (s + 1)], rq[:, 2 * h + k, :],
                                                   start=k == 0, stop=k == 1)
                    ins.then_inc(ret_s, 1)
                pe.wait_ge(ret_p, 2 * h + 2)
                for t in range(2):
                    need(pe, ret_n, 2 * h - 1 + t)
                    for s in range(4):
                        ins = nc.tensor.matmul(mx[:, 2 + t, :], r_P[:, h % 2, s, P * t:P * (t + 1)],
                                               rv[:, s, 512 * h:512 * (h + 1)], start=s == 0, stop=s == 3)
                    ins.then_inc(ret_o, 1)
            pe.wait_ge(ret_n, 2 * RET)
            stage("ret_oT")
            transposed(rg, (0, 1), 2)
            gates(2, 8)
            stage("ret_out")
            roT = hT[:, :, :].rearrange("p a b -> p (a b)").rearrange("p (k t) -> p k t", k=16)
            done(pre.job["ret_oT"] + KD)
            down(roT, (8, 8), (0, 1), lambda n: None)
            transposed(norm(3, LAT, "norm3"), (0, 1))
            done(pre.job["norm3"] + KD)
            feed_forward("ffn1", 1, ffT2, 256, 512, (0, 1), 10)
            assert job.n == pre.jobs and tile.n == pre.tiles

            with pe.Fori(0, DEPTH2) as l:
                loop[0] = l
                job.enter(l * per.jobs + pre.jobs)
                tile.enter(0)
                oT = hT[:, :, 0:256]
                stage("param")
                pe.wait_ge(lrow_in, l * 80 + 80)
                for j, n in enumerate((112, 88)):
                    b = bank()
                    nc.tensor.transpose(b[:, 0:n], prow[0:n, j, :], ident[0:n, 0:n]).then_inc(acc_full, 1)
                stage("norm")
                pe.wait_ge(norm_xs, l * 2 + 5)
                transposed(d_xs, (0, 1))
                done(per.job["norm"] + KD)
                for _ in range(2):
                    by_token(LAT, 512)
                for _ in range(2):
                    by_token(LAT, P)
                for _ in range(6):
                    by_feature(4, 256, 512)
                by_token(LAT, 16)
                stage("swa_qkT")
                for i in range(2):
                    pe.wait_ge(qk_ready, l * 2 + (NT + i + 1))
                    for j2 in range(2):
                        b = bank()
                        for j in range(4):
                            at = 512 * j2 + P * j
                            ins = nc.tensor.transpose(b[:, P * j:P * (j + 1)], s_p[:, i, at:at + P], ident)
                        ins.then_inc(acc_full, 1)
                    b = bank()
                    nc.tensor.transpose(b[:, 0:P], s_p[:, i, 1024:1152], ident).then_inc(acc_full, 1)
                done(per.job["swa_qkT"] + 6)
                att_S, att_PT = [sS[:, j, :] for j in range(2)], [sPT[:, j, :] for j in range(2)]
                units = []
                for i in range(2):
                    for kv in range(2):
                        for j in range(8):
                            half = slice(HD * kv, HD * kv + HD)
                            units.append((sqT[half, j, P * i:P * (i + 1)], skT[half, 0:P * (i + 1)], i + 1,
                                          [s_v[:, t, HD * kv:HD * kv + HD] for t in range(i + 1)]))
                stage("dn_z")
                attention(l * 32 + 32, units, lambda u: fill(1, hT, LAT) if u < 32 else None)
                stage("swa_oT")
                pe.wait_ge(att_d, l * 32 + 64)
                transposed(oswa, (0, 1))
                done(per.job["swa_oT"] + KD)
                stage("swa_out")
                fill(8, oT, (0, 1))
                for s in range(8):
                    pe.wait_ge(l2_sqd, l * 8 + s + 1)
                    since(pe, l2_rsd, l * 8, s - 1)
                    nc.tensor.matmul(mx[:, s % 2, :], ones, l2_sq[:, s % 2, :], start=True, stop=True).then_inc(l2_ps, 1)
                    fill(2, oT, (0, 1))
                pe.wait_ge(gc_in, l + 1)
                dg_ = st[:, 64:80].rearrange("p (c h) -> p c h", c=2)
                for c in range(2):
                    nc.tensor.matmul(mx[:, 2, 8 * c:8 * c + 8], tri, dg_[:, c, :], start=True, stop=True)
                nc.tensor.matmul(mx[:, 2, 16:24], ones, dg_[:, 0, :], start=True, stop=True).then_inc(gc_ps, 1)
                fill(8, oT, (0, 1))
                stage("gate_b")
                pe.wait_ge(l2_done, l * 8 + 8)
                for hg in range(2):
                    if hg:
                        pe.wait_ge(dn_o, l * 4 + 2)
                    for c in range(2):
                        g = 2 * hg + c
                        tok = slice(P * c, P * (c + 1))
                        pe.wait_ge(tg_in, l * 4 + g + 1)
                        nc.tensor.matmul(mx[:, 3, :], ones, t_in.rearrange("p a b -> p (a b)"),
                                         start=True, stop=True).then_inc(tg_ps, 1)
                        fill(2, hT, LAT)
                        since(pe, l_ready, l * 4, g)
                        for h in range(4):
                            kT, qT = dnf[:, 8 + 4 * hg + h, tok], dnf[:, 4 * hg + h, tok]
                            nc.tensor.matmul(mx[:, 0, P * h:P * (h + 1)], kT, kT, start=True, stop=True)
                            ins = nc.tensor.matmul(mx[:, 1, P * h:P * (h + 1)], kT, qT, start=True, stop=True)
                        ins.then_inc(kq_ps, 1)
                        for j, f in enumerate((16, 8)):
                            since(pe, kv_sb, l * 8, 2 * g + j)
                            for h in range(4):
                                ins = nc.tensor.transpose(mx[:, 2, P * h:P * (h + 1)], dnf[:, f + 4 * hg + h, tok], ident)
                            ins.then_inc(kv_ps, 1)
                            fill(1, hT, LAT)
                        if c == 1:
                            pe.wait_ge(l_ready, l * 4 + g + 1)
                    for level in range(7):
                        n = (hg * 7 + level) * 2
                        for c in range(2):
                            if level:
                                pe.wait_ge(inv_d, l * 28 + n - 1 + c)
                            for h in range(4):
                                ins = nc.tensor.matmul(mx[:, c, P * h:P * (h + 1)], dL[c][:, h, :], dTT[c][:, h, :],
                                                       start=True, stop=True)
                            ins.then_inc(inv_y, 1)
                        fill(1, hT, LAT)
                        for c in range(2):
                            pe.wait_ge(inv_ys, l * 28 + n + c + 1)
                            if level == 0 and c == 0:
                                pe.wait_ge(kv_sb, l * 8 + 4 * hg + 4)
                            for h in range(4):
                                if level < 6:
                                    nc.tensor.matmul(mx[:, 2 + c, P * h:P * (h + 1)], dY[c][:, h, :], dT[c][:, h, :],
                                                     start=True, stop=True)
                                ins = nc.tensor.matmul(mx[:, c, P * h:P * (h + 1)], dT[c][:, h, :], dY[c][:, h, :],
                                                       start=True, stop=True)
                            ins.then_inc(inv_t, 1)
                        fill(2, hT, LAT)
                    fill(3, hT, LAT)
                    pe.wait_ge(inv_d, l * 28 + 14 * hg + 14)
                    heads = [(h, slice(P * h, P * (h + 1))) for h in range(4)]
                    for h, s in heads:
                        ins = nc.tensor.matmul(mx[:, 0, s], dTT[0][:, h, :], vb[0][:, h, :], start=True, stop=True)
                    ins.then_inc(fin_ps, 1)
                    for h, s in heads:
                        ins = nc.tensor.matmul(mx[:, 2, s], kbe[:, h, :], dTT[1][:, h, :], start=True, stop=True)
                    ins.then_inc(fin_ps, 1)
                    pe.wait_ge(fin_sb, l * 8 + 4 * hg + 1)
                    for h, s in heads:
                        ins = nc.tensor.matmul(mx[:, 1, s], kdec[:, h, :], vn[0][:, h, :], start=True, stop=True)
                    ins.then_inc(fin_ps, 1)
                    pe.wait_ge(fin_sb, l * 8 + 4 * hg + 3)
                    for h, s in heads:
                        nc.tensor.matmul(mx[:, 3, s], dTT[1][:, h, :], vb[1][:, h, :], start=True, stop=False)
                        ins = nc.tensor.matmul(mx[:, 3, s], nwT[:, h, :], dS[:, h, :], start=False, stop=True)
                    ins.then_inc(fin_ps, 1)
                    for h, s in heads:
                        ins = nc.tensor.matmul(mx[:, 0, s], dQ[0][:, h, :], vn[0][:, h, :], start=True, stop=True)
                    ins.then_inc(fin_ps, 1)
                    pe.wait_ge(fin_sb, l * 8 + 4 * hg + 4)
                    for h, s in heads:
                        nc.tensor.matmul(mx[:, 1, s], qdec[:, h, :], dS[:, h, :], start=True, stop=False)
                        ins = nc.tensor.matmul(mx[:, 1, s], dQ[1][:, h, :], vn[1][:, h, :], start=False, stop=True)
                    ins.then_inc(fin_ps, 1)
                stage("dn_oT")
                pe.wait_ge(dn_o, l * 4 + 4)
                transposed(dz, (0, 1))
                done(per.job["dn_oT"] + KD)
                for _ in range(2):
                    by_token((0, 1), 512, oT)
                stage("mergeT")
                pe.wait_ge(y_used, l * Y_USES + 28)
                transposed(yb, (0, 1))
                gates(2, l * 4 + 12)
                done(per.job["mergeT"] + KD)
                for _ in range(2):
                    by_token((0, 1), 512, oT)
                stage("norm_ffn")
                pe.wait_ge(norm_xs, l * 2 + 6)
                transposed(f_xs2, (0, 1))
                done(per.job["norm_ffn"] + KD)
                feed_forward("up", l + 2, ffT2, 256, 512, (0, 1), l * 4 + 14)
                assert job.n == per.jobs and tile.n == per.tiles

        @block.scalar
        def _(act):
            job, uses, chunk, own = Cursor(), Cursor(), Cursor(), Cursor()
            chunk.n = MOD_FIRST
            chain = Chain(act, act_chain)
            loop = [None]

            act.dma_start(ident, a["const_f"][:, 0:P]).then_inc(ident_in, 16)
            for dst, src in (
                (dg[0:96, 0, 0:P], a["mod_b"].rearrange("l (b p) -> (l b) p", p=P)),
                (dg[96:128, 0, 0:P], a["norm_g"].rearrange("l h (k p) -> (l h k) p", p=P)),
                (dg[0:96, 1, 0:P], a["b_ada_2"].rearrange("l (b p) -> (l b) p", p=P)),
                (dg[96:104, 1, 0:P], a["c"].rearrange("o (k p) -> (o k) p", p=P)),
                (dg[104:112, 1, 0:P], a["c_ctx"].rearrange("(k p) -> k p", p=P)),
                (dg[112:120, 1, 0:P], a["c_2"].rearrange("o (k p) -> (o k) p", p=P)),
                (dg[120:128, 1, 0:P], a["hgrn_lb"].rearrange("l (k p) -> (l k) p", p=P)),
            ):
                act.dma_start(dst, src).then_inc(rows_in, 16)
            for j, name in enumerate(("ctx", "x")):
                act.dma_start(x[:, 2 * j:2 * j + 2, :], a[name][0].rearrange("(t p) d -> p t d", p=P)).then_inc(x_in, 16)
            for dst, src in ((fconst[:, P:], a["const_f"][:, P:]), (masks, a["const_b"])):
                act.dma_start(dst, src).then_inc(const_in, 16)
            for lo, src in ((0, a["attn_qk_norm_g"][0, 0:1, :]), (64, a["attn_qk_norm_g"][0, 1:2, :]),
                            (128, a["hgrn_out_norm_g"]), (256, a["attn_sink"])):
                n = src.shape[1]
                act.dma_start(erow[:, lo:lo + n], src.to_broadcast([P, n])).then_inc(even_in, 16)
            act.dma_start(pos_i[:, :], a["positions_2"][0].rearrange("(t p) -> p t", p=P),
                          allow_slow_non_contiguous=True).then_inc(pos_in, 16)

            def evac(dst, width, func=ACT.Copy, rows_=P, shape=None, first=0, signal=True, **kw):
                if first == 0:
                    job.now = job.next()
                    act.wait_ge(acc_full, job.base + job.now + 1)
                src = acc[0:rows_, job.now % 4, first:first + width]
                if shape:
                    src = src.rearrange(shape[0], **shape[1])
                ins = nc.scalar.activation(dst, src, func, **kw)
                if signal:
                    ins.then_inc(acc_done, 1)

            def stage(name):
                p = pre if loop[0] is None else per
                assert job.n == p.job[name], name

            def mod_start():
                for kind, n in MOD_START:
                    stage(f"mod{kind}{n}")
                    if kind == "A":
                        evac(rows[:, n % 2, :], 512, rows_=2)
                    else:
                        c = 4 * (n % MOD_CHUNKS)
                        evac(modc[:, n // MOD_CHUNKS, :, c:c + 4], 8, shape=("p (b c) -> p c b", dict(c=2)))

            def mod():
                n = chunk.next()
                stage(f"mod{n}")
                c, conds = 4 * (n % MOD_CHUNKS), mod_conds(n)
                evac(modc[:, n // MOD_CHUNKS, 0:conds, c:c + 4], 4 * conds, shape=("p (c b) -> p c b", dict(c=conds)))

            def mod_after(where):
                if own.next() in MOD_AFTER_JOB[where]:
                    mod()

            def exp_ln():
                nc.scalar.preload_act_table_set(EXP_LN)

            def silu_tanh():
                nc.scalar.preload_act_table_set(SILU_TANH)

            def rsqrt(dst, src, tmp, scale, signal):
                chain.link(nc.scalar.activation(tmp, src, ACT.Ln, bias=eps[:, 0:1], scale=scale))
                nc.scalar.activation(dst, tmp, ACT.Exp, scale=-0.5).then_inc(signal, 1)

            def norm(tiles, xs, name, sums_before=None):
                exp_ln()
                if sums_before is not None:
                    act.wait_ge(y_used, sums_before)
                for j, i in enumerate(tiles):
                    ins = nc.scalar.activation(xs[:, j, :], x[:, i, :], ACT.Square, accum_out=st[:, j:j + 1])
                n = len(tiles)
                chain.link(ins)
                rsqrt(st[:, 4:4 + n], st[:, 0:n], st[:, 416:416 + n], 1.0 / D, norm_rs)
                stage(name)

            def modulated(shift, n, use):
                act.wait_ge(norm_ab, use + 1)
                for k in range(KD):
                    if n == 4:
                        evac(hT[:, k, 0:256], 256, ACT.Identity, signal=False,
                             scale=ab[:, 1, k:k + 1], bias=mb[:, 1, shift + k:shift + k + 1])
                        evac(hT[:, k, 256:512], 256, ACT.Identity, first=256,
                             scale=ab[:, 0, k:k + 1], bias=mb[:, 0, shift + k:shift + k + 1])
                    else:
                        evac(hT[:, k, 256:512], 256, ACT.Identity,
                             scale=ab[:, 0, k:k + 1], bias=mb[:, 0, shift + k:shift + k + 1])

            def gates(conds):
                for g in conds:
                    for h in range(2):
                        evac(gate[:, g, 512 * h:512 * h + 512], 512)

            def sums(n, base=0):
                for _ in range(n):
                    u = uses.next()
                    need(act, y_used, uses.base + u - 1 if loop[0] is not None else u - 1)
                    evac(ybuf[:, u % 2, :], 512)

            def attention(base, n, blocks, sink, S, PT, fill):
                for u in range(n + 1):
                    if u < n:
                        act.wait_ge(att_m, base + u + 1)
                        c = u % 8
                        nc.scalar.activation(S[u % 2][:, 0:P * blocks(u)], S[u % 2][:, 0:P * blocks(u)], ACT.Exp,
                                             bias=st[:, 8 + c:9 + c], accum_out=st[:, 16 + c:17 + c])
                        nc.scalar.activation(st[:, 24 + c:25 + c], sink(u), ACT.Exp,
                                             bias=st[:, 8 + c:9 + c]).then_inc(att_p, 1)
                    if u >= 1:
                        act.wait_ge(att_t, base + u)
                        since(act, att_o, base, u - 2)
                        w = P * blocks(u - 1)
                        nc.scalar.activation(PT[(u - 1) % 2][:, 0:w], mx[:, 2, 0:w], ACT.Copy).then_inc(att_pt, 1)
                    fill(u)

            silu_tanh()
            act.wait_ge(vcol_sb, 1)
            for blk, j, lo in ((0, 0, 224), (0, 1, 232), (1, 0, 240), (1, 1, 240)):
                ins = nc.scalar.activation(cond[:, blk, :, j], vcols[:, lo:lo + KD], ACT.Silu)
            ins.then_inc(cond_ready, 1)
            act.wait_ge(ang_ready, 1)
            nc.scalar.activation(srope[:, :, :], st[:, 464:496].rearrange("p (t f) -> p t f", t=2),
                                 ACT.Sin).then_inc(rope_ready, 1)
            exp_ln()
            act.wait_ge(lb_x, 1)
            nc.scalar.activation(st[:, 336:344], st[:, 328:336], ACT.Exp).then_inc(lb_e, 1)
            act.wait_ge(x_in, 32)
            norm(BOTH, cat, "modA0")
            mod_start()
            stage("norm0")
            modulated(0, 4, 0)
            silu_tanh()
            for i in BOTH:
                evac(qk_raw[:, i, 0:512], 512)
                mod_after("even")
            for i in BOTH:
                evac(qk_raw[:, i, 512:640], P)
                mod_after("even")
            for i in BOTH:
                evac(v_raw[:, i, :], P)
                mod_after("even")
            exp_ln()
            act.wait_ge(qk_ss, 1)
            rsqrt(st[:, 120:160], st[:, 80:120], st[:, 120:160], 1.0 / HD, qk_rs)
            silu_tanh()
            for h in range(HG):
                evac(hq[:, h, :], 512, ACT.Silu)
                mod_after("even")
            for d in range(2):
                for h in range(HG):
                    evac(hf[d][:, h, :], 512, ACT.Tanh, scale=0.5)
                    mod_after("even")
            for i in BOTH:
                evac(hv[:, i, :], 512)
                mod_after("even")
            for i in BOTH:
                evac(hg_[:, i, :], 512, ACT.Silu)
                mod_after("even")
            exp_ln()
            for i in BOTH:
                evac(eqT[:, :, P * i:P * (i + 1)], 512, shape=("p (j t) -> p j t", dict(j=4)))
                evac(ekT[:, P * i:P * (i + 1)], P)
            act.wait_ge(even_in, 64)
            attention(0, 32, lambda u: 2 if u < 16 else 4, lambda u: erow[:, 256 + u % 8:257 + u % 8],
                      [eS[:, j, :] for j in range(2)], [ePT[:, j, :] for j in range(2)],
                      lambda u: None)
            stage("att_catT")
            for k in range(KD // 2):
                evac(hT[:, k, :], 512)

            def log_gates(h, d):
                act.wait_ge(hg_f, 2 * h + d + 1)
                need(act, hg_s, 2 * h + d - 1)
                nc.scalar.activation(e_set[d][1], hf[d][:, h, :], ACT.Ln).then_inc(hg_lf, 1)

            def factors(h, d):
                e = e_set[d]
                act.wait_ge(hg_cum, 2 * h + d + 1)
                nc.scalar.activation(e[1], e[0], ACT.Exp, scale=-1.0)
                nc.scalar.activation(e_q[h % 2][d], h_cum[d], ACT.Exp)
                chain.link(nc.scalar.activation(e[3], e[3], ACT.Exp))
                nc.scalar.activation(e[0], e[0], ACT.Exp).then_inc(hg_e, 1)

            for d in range(2):
                log_gates(0, d)
            for d in range(2):
                factors(0, d)
            for h in range(HG):
                for d in range(2):
                    w = 2 * h + d
                    act.wait_ge(hg_kt, w + 1)
                    need(act, hg_u, w - 1)
                    nc.scalar.activation(h_kd[:, d, :, :], mx[:, 0, :].rearrange("p (t k) -> p t k", t=4),
                                         ACT.Copy).then_inc(hg_kts, 1)
                    if h + 1 < HG:
                        log_gates(h + 1, d)
                if h + 1 < HG:
                    for d in range(2):
                        factors(h + 1, d)
                stage(f"hg_o{h}")
                evac(cat[:, :, 512 + P * h:512 + P * (h + 1)], 512, shape=("p (t e) -> p t e", dict(t=4)))
                act.wait_ge(hg_osq, h + 1)
                rsqrt(st[:, 384 + 4 * h:388 + 4 * h], st[:, 368 + 4 * h:372 + 4 * h], st[:, 384 + 4 * h:388 + 4 * h],
                      1.0 / P, hg_ors)
            stage("hg_catT")
            for k in range(KD // 2, KD):
                evac(hT[:, k, :], 512)
            gates((0, 1))
            stage("even_out")
            sums(8)

            def feed_forward(use, n, tiles, gated, shift, xs, norm_job, conv=False):
                norm(tiles, xs, norm_job, gated)
                modulated(shift, len(tiles), use_norm[0])
                silu_tanh()
                own.n = 0
                for t in range(11):
                    for j in range(2):
                        b = 2 * t + j
                        if conv:
                            since(act, ff_conv, l_ff[0] * KF, b - 1)
                            evac(conv_in[:, j, 3:259], n)
                        else:
                            need(act, ff_mul, use * KF + b - 1)
                            evac(g_buf[:, j, 0:n], n, ACT.Silu)
                            if use == 0:
                                mod_after("ffn0")
                    for j in range(2):
                        b = 2 * t + j
                        if conv:
                            since(act, ff_mul, use * KF, b - 1)
                        evac(u_buf[:, j, 0:n], n)
                        if not conv and use == 0:
                            mod_after("ffn0")
                    if conv:
                        for j in range(2):
                            act.wait_ge(ff_conv, l_ff[0] * KF + 2 * t + j + 1)
                            nc.scalar.activation(g_buf[:, j, 0:n], c_buf[:, j, :], ACT.Silu).then_inc(ff_silu, 1)

            use_norm, l_ff = [1], [0]
            feed_forward(0, 512, BOTH, 8, 24, f_xs4, "norm1")
            gates((0, 1))
            sums(8)
            norm(BOTH, r_xs, "norm2", 16)
            modulated(0, 4, 2)
            silu_tanh()
            def table(h):
                act.dma_start(r_D[:, h % 2], a["const_ret"][h]).then_inc(dtab_in[h % 2], 16)

            table(0)
            table(1)
            own.n = 0
            for f in range(8):
                evac(rq[:, f, :], 256)
                mod_after("odd")
            for f in range(8):
                evac(rk[:, f, :], 512)
                mod_after("odd")
            for c in range(4):
                for i in BOTH:
                    evac(rv[:, i, 512 * c:512 * (c + 1)], 512)
                    mod_after("odd")
            for c in range(4):
                for t in range(2):
                    evac(rg[:, t, 512 * c:512 * (c + 1)], 512, ACT.Silu)
                    mod_after("odd")
            exp_ln()
            for h in range(RET):
                for t in range(2):
                    n = 2 * h + t
                    act.wait_ge(ret_o, n + 1)
                    chain.link(nc.scalar.activation(r_junk, mx[:, 2 + t, :], ACT.Square,
                                                    accum_out=st[:, 400 + n:401 + n]))
                    rsqrt(st[:, 408 + n:409 + n], st[:, 400 + n:401 + n], st[:, 416 + n:417 + n], 1.0 / 512, ret_rs)
                if h + 2 < RET:
                    act.wait_ge(ret_p, 2 * h + 2)
                    table(h + 2)
            stage("ret_oT")
            roT = hT[:, :, :].rearrange("p a b -> p (a b)").rearrange("p (k t) -> p k t", k=16)
            for k in range(KD):
                evac(roT[:, 2 * k:2 * k + 2, :], 512, shape=("p (q t) -> p q t", dict(q=2)))
            gates((1,))
            stage("ret_out")
            sums(4)
            use_norm[0] = 3
            feed_forward(1, 256, LAT, 20, 24, f_xs2, "norm3")
            gates((1,))
            sums(4)
            assert job.n == pre.jobs

            with act.Fori(0, DEPTH2) as l:
                loop[0] = l
                job.enter(l * per.jobs + pre.jobs)
                uses.enter(l * Y_USES + 24)
                chain.enter(l, ACT_LINKS)
                for j, n in enumerate((112, 88)):
                    evac(pcols[:, P * j:P * j + n], n)
                norm(LAT, d_xs, "norm", l * Y_USES + 24)
                modulated(0, 2, l * 2 + 4)
                silu_tanh()
                for c in range(2):
                    for t in range(2):
                        evac(sqk[:, t, 512 * c:512 * (c + 1)], 512)
                for t in range(2):
                    evac(sqk[:, t, 1024:1152], P)
                for t in range(2):
                    evac(s_v[:, t, :], P)
                exp_ln()
                act.wait_ge(qk_ss, l + 2)
                rsqrt(st[:, 120:156], st[:, 80:116], st[:, 120:156], 1.0 / HD, qk_rs)
                silu_tanh()
                for b in range(25):
                    if b < 24:
                        since(act, dc_conv, l * 24, b - 1)
                        evac(conv_in[:, b % 2, 3:259], 256)
                    if b:
                        act.wait_ge(dc_conv, l * 24 + b)
                        nc.scalar.activation(dnf[:, b - 1, :], dnf[:, b - 1, :], ACT.Silu).then_inc(dc_silu, 1)
                for t in range(2):
                    evac(dab[:, t, :], 16)
                exp_ln()
                for i in range(2):
                    for j2 in range(2):
                        evac(sqT[:, 4 * j2:4 * j2 + 4, P * i:P * (i + 1)], 512, shape=("p (j t) -> p j t", dict(j=4)))
                    evac(skT[:, P * i:P * (i + 1)], P)

                def filled(dst, n):
                    evac(dst[:, n % 2, 512 * (n // 2):512 * (n // 2) + 512], 512)

                stage("dn_z")
                attention(l * 32 + 32, 32, lambda u: 1 if u < 16 else 2, lambda u: brow[:, 144 + u % 16:145 + u % 16],
                          [sS[:, j, :] for j in range(2)], [sPT[:, j, :] for j in range(2)],
                          lambda u: filled(dz, u // 8 - 1) if u % 8 == 0 and u else None)
                stage("swa_oT")
                for k in range(KD):
                    evac(hT[:, k, 0:256], 256)
                silu_tanh()
                act.wait_ge(acc_done, l * per.jobs + pre.jobs + per.job["dn_z"] + 4)
                for t in range(2):
                    ins = nc.scalar.activation(dz[:, t, :], dz[:, t, :], ACT.Silu)
                ins.then_inc(dz_ready, 1)
                exp_ln()
                for s in range(8):
                    act.wait_ge(l2_ps, l * 8 + s + 1)
                    since(act, l2_done, l * 8, s - 1)
                    chain.link(nc.scalar.activation(l2_rs[:, s % 2, :], mx[:, s % 2, :], ACT.Ln, bias=eps[:, 0:1]))
                    nc.scalar.activation(l2_rs[:, s % 2, :], l2_rs[:, s % 2, :], ACT.Exp, scale=-0.5).then_inc(l2_rsd, 1)
                    if s % 4 == 1:
                        filled(yb, s // 4)
                filled(yb, 2)
                act.wait_ge(gb_x, l + 1)
                chain.link(nc.scalar.activation(st[:, 280:296], st[:, 264:280], ACT.Exp, scale=-1.0))
                nc.scalar.activation(st[:, 280:296], st[:, 280:296], ACT.Ln, bias=1.0)
                nc.scalar.activation(st[:, 296:304], brow[:, 8:16], ACT.Exp)
                nc.scalar.activation(st[:, 216:232].rearrange("p (t h) -> p t h", t=2), dab[:, :, 8:16], ACT.Exp,
                                     scale=-1.0).then_inc(gb_e, 1)
                act.wait_ge(gc_sb, l + 1)
                nc.scalar.activation(st[:, 184:200], st[:, 160:176], ACT.Exp)
                nc.scalar.activation(st[:, 200:208], st[:, 208:216], ACT.Exp).then_inc(gc_e, 1)
                filled(yb, 3)
                stage("gate_b")
                steps, emptied = 0, 0

                def gate_steps(n):
                    nonlocal steps, emptied
                    if steps // KD > emptied:
                        filled(sgb if emptied < 4 else sga, emptied % 4)
                        emptied += 1
                    steps += n

                for hg in range(2):
                    for c in range(2):
                        g = 2 * hg + c
                        act.wait_ge(dec_in, l * 4 + g + 1)
                        if c == 1:
                            nc.scalar.activation(qdec, mx[:, 3, :].rearrange("p (h t) -> p h t", h=4), ACT.Exp)
                        nc.scalar.activation(t_g, t_g, ACT.Exp)
                        nc.scalar.activation(t_st, t_st, ACT.Exp).then_inc(dec_e, 1)
                        gate_steps(4)
                    for level in range(7):
                        n = (hg * 7 + level) * 2
                        for c in range(2):
                            act.wait_ge(inv_y, l * 28 + n + c + 1)
                            if level:
                                act.wait_ge(inv_t, l * 28 + n - 1 + c)
                            nc.scalar.activation(dY[c], mx[:, c, :].rearrange("p (h t) -> p h t", h=4),
                                                 ACT.Copy).then_inc(inv_ys, 1)
                        gate_steps(3)
                    gate_steps(3)
                    for n, (dst, b, scale) in enumerate(((vn[0], 0, 1.0), (nwT, 2, -1.0), (dS, 1, 1.0), (vn[1], 3, 1.0))):
                        act.wait_ge(fin_ps, l * 12 + 6 * hg + n + 1)
                        nc.scalar.activation(dst, mx[:, b, :].rearrange("p (h t) -> p h t", h=4), ACT.Copy,
                                             scale=scale).then_inc(fin_sb, 1)
                    for c in range(2):
                        act.wait_ge(fin_ps, l * 12 + 6 * hg + 5 + c)
                        for h in range(4):
                            n = 432 + 8 * hg + 4 * c + h
                            ins = nc.scalar.activation(t_in[:, h, :], mx[:, c, P * h:P * (h + 1)], ACT.Square,
                                                       accum_out=st[:, n:n + 1])
                        chain.link(ins)
                        n = 8 * hg + 4 * c
                        rsqrt(st[:, 448 + n:452 + n], st[:, 432 + n:436 + n], st[:, 416 + 4 * c:420 + 4 * c], 1.0 / P, dn_rs)
                gate_steps(0)
                assert emptied == 8
                for k in range(KD):
                    evac(hT[:, k, 0:256], 256)
                silu_tanh()
                act.wait_ge(acc_done, l * per.jobs + pre.jobs + per.job["dn_oT"])
                for s in (sgb, sga):
                    for t in range(2):
                        ins = nc.scalar.activation(s[:, t, :], s[:, t, :], ACT.Tanh, scale=0.5)
                ins.then_inc(mix_ready, 1)
                stage("dn_out")
                sums(4)
                for k in range(KD):
                    evac(hT[:, k, 0:256], 256)
                gates((1,))
                stage("w_o")
                sums(4)
                use_norm[0], l_ff[0] = l * 2 + 5, l
                feed_forward(l + 2, 256, LAT, l * Y_USES + 32, 24, f_xs2, "norm_ffn", conv=True)
                gates((1,))
                sums(4)
                assert job.n == per.jobs
                chain.leave("ScalarE")

        @block.vector
        def _(dve):
            V = nc.vector
            chain = Chain(dve, dve_chain)
            link = chain.link
            uses, chunk = Cursor(), Cursor()
            chunk.n = MOD_FIRST
            loop = [None]

            def job_done(name, n):
                if loop[0] is None:
                    dve.wait_ge(acc_done, pre.upto(name, n))
                else:
                    dve.wait_ge(acc_done, loop[0] * per.jobs + (pre.jobs + per.job[name] + n))

            def rep(v, axis, shape):
                return v.unsqueeze(axis).to_broadcast(shape)

            def mod_cols(layer, first, n, bias):
                link(V.tensor_tensor(mb[:, :, first:first + n], modc[:, layer, :, first:first + n],
                                     rep(vcols[:, bias + first:bias + first + n], 1, [P, 2, n]), ALU.add))

            def mod_chunk():
                n = chunk.next()
                step, conds = mod_steps(n), mod_conds(n)
                for k in range(KD):
                    i = (n - MOD_FIRST) * (KD // 2) + k // 2
                    w = mod_w[:, i % 2, k % 2, :]
                    if k % 2 == 0:
                        dve.wait_ge(mod_in[i % 2], 16 * (i // 2 + 1))
                    if k == 0 and n > MOD_FIRST:
                        dve.wait_ge(acc_full, pre.job[f"mod{n - 1}"] + 1)
                    for c in range(conds):
                        col = cond[:, n // 24, k, c:c + 1]
                        if k == 0:
                            ins = V.tensor_scalar(mod_acc[:, c, :], w, col, None, ALU.mult)
                        else:
                            dve.wait_ge(mod_sum, step + 1 - conds)
                            ins = V.scalar_tensor_tensor(mod_acc[:, c, :], w, col, mod_acc[:, c, :], ALU.mult, ALU.add)
                        ins.then_inc(mod_sum, 1)
                        step += 1

            def norm(use, tiles, xs, scale, gain):
                V.scalar_tensor_tensor(ab[:, :, :], mb[:, :, scale:scale + KD], 1.0, rep(gain, 1, [P, 2, KD]),
                                       ALU.add, ALU.mult).then_inc(norm_ab, 1)
                dve.wait_ge(norm_rs, use + 1)
                for j, i in enumerate(tiles):
                    ins = V.tensor_scalar(xs[:, j, :], x[:, i, :], st[:, 4 + j:5 + j], None, ALU.mult)
                ins.then_inc(norm_xs, 1)

            def gates(name, conds, first):
                s = 0
                for c in conds:
                    for h in range(2):
                        if s >= 2:
                            dve.wait_ge(acc_full, pre.job[name] + s - 1)
                        cols = mb[:, c, first + 4 * h:first + 4 * h + 4]
                        V.tensor_tensor(dg[:, s % 2, :].rearrange("p (k m) -> p k m", k=4),
                                        rep(ident, 1, [P, 4, P]), rep(cols, 2, [P, 4, P]), ALU.mult).then_inc(dg_ready, 1)
                        s += 1

            def residual(name, tiles, gate_job, n_gates):
                job_done(gate_job, n_gates)
                for n in range(2 * len(tiles)):
                    h, i = n // len(tiles), tiles[n % len(tiles)]
                    u = uses.next()
                    job_done(name, n + 1)
                    cols = slice(512 * h, 512 * h + 512)
                    link(V.tensor_tensor(ybuf[:, u % 2, :], ybuf[:, u % 2, :], gate[:, i // 2, cols], ALU.mult))
                    V.tensor_tensor(x[:, i, cols], x[:, i, cols], ybuf[:, u % 2, :], ALU.add).then_inc(y_used, 1)

            def attention(base, n, blocks, mask, sink, S, out_):
                for u in range(n + 2):
                    if u < n:
                        w, c = P * blocks(u), u % 8
                        dve.wait_ge(att_s, base + u + 1)
                        since(dve, att_t, base, u - 1)
                        link(V.scalar_tensor_tensor(S[u % 2][:, 0:w], mx[:, u % 2, 0:w], HD ** -0.5, mask(u),
                                                    ALU.mult, ALU.add))
                        link(V.reduce_max(st[:, 40 + c:41 + c], S[u % 2][:, 0:w], AXX))
                        V.tensor_scalar(st[:, 8 + c:9 + c], st[:, 40 + c:41 + c], sink(u), -1.0,
                                        ALU.max, ALU.mult).then_inc(att_m, 1)
                    if u >= 2:
                        o = u - 2
                        c = o % 8
                        dve.wait_ge(att_p, base + o + 1)
                        link(V.tensor_tensor(st[:, 32 + c:33 + c], st[:, 16 + c:17 + c], st[:, 24 + c:25 + c], ALU.add))
                        link(V.reciprocal(st[:, 32 + c:33 + c], st[:, 32 + c:33 + c]))
                        dve.wait_ge(att_o, base + o + 1)
                        V.tensor_scalar(out_(o), mx[:, 3, HD * c:HD * c + HD], st[:, 32 + c:33 + c], None,
                                        ALU.mult).then_inc(att_d, 1)

            def rotate(dst1, dst2, v1, v2, t1, t2, both, cos, sin):
                V.tensor_tensor(t1[0], both, cos, ALU.mult)
                link(V.tensor_tensor(t2[0], both, sin, ALU.mult))
                V.tensor_tensor(dst1, t1[1], t2[2], ALU.subtract)
                return V.tensor_tensor(dst2, t1[2], t2[1], ALU.add)

            V.memset(eps[:, :], EPS)
            dve.wait_ge(vcol_ps, 1)
            V.tensor_copy(vcols[:, :], mx[:, 0, 0:256]).then_inc(vcol_sb, 1)
            dve.wait_ge(vcol_sb, 1)
            TAU = 2.0 * np.pi
            parts = []
            left = TAU
            for bits in (8, 12):
                step = 2.0 ** (2 - bits - 6 * (bits == 12))
                parts.append(float(np.floor(left / step) * step))
                left -= parts[-1]
            parts.append(float(np.float32(left)))
            dve.wait_ge(pos_in, 16)
            posf, ang, turn = st[:, 500:502], st[:, 464:496].rearrange("p (t g f) -> p t g f", t=2, g=2), st[:, 48:64]
            link(V.tensor_copy(posf, pos_i[:, :]))
            dve.wait_ge(ident_in, 16)
            dve.wait_ge(const_in, 32)
            V.tensor_copy(bconst[:, :], masks)
            a_sin, a_cos = ang[:, :, 1, :], ang[:, :, 0, :]
            t3 = turn.rearrange("p (t f) -> p t f", t=2)
            link(V.tensor_tensor(a_sin, rep(posf, 2, [P, 2, 8]), rep(const("inv"), 1, [P, 2, 8]), ALU.mult))
            link(V.tensor_scalar(t3, a_sin, float(np.float32(1.0 / TAU)), 12582912.0, ALU.mult, ALU.add))
            link(V.tensor_scalar(t3, t3, 12582912.0, None, ALU.subtract))
            for part in parts:
                link(V.scalar_tensor_tensor(a_sin, t3, -part, a_sin, ALU.mult, ALU.add))
            link(V.tensor_scalar(a_cos, a_sin, float(np.pi / 2), None, ALU.add))
            link(V.tensor_scalar(t3, a_cos, float(np.pi), -TAU, ALU.is_gt, ALU.mult))
            link(V.tensor_tensor(a_cos, a_cos, t3, ALU.add))
            V.tensor_scalar(ang[:, :, :, :], ang[:, :, :, :], 3.1415925, -3.1415925, ALU.min, ALU.max).then_inc(ang_ready, 1)
            m = st[:, 344:348]
            link(V.tensor_tensor(m, vcols[:, 248:252], vcols[:, 252:256], ALU.max))
            V.tensor_tensor(st[:, 328:336].rearrange("p (l h) -> p l h", l=2),
                            vcols[:, 248:256].rearrange("p (l h) -> p l h", l=2), rep(m, 1, [P, 2, 4]),
                            ALU.subtract).then_inc(lb_x, 1)
            dve.wait_ge(lb_e, 1)
            link(V.tensor_tensor(st[:, 348:352], st[:, 336:340], st[:, 340:344], ALU.add))
            link(V.reciprocal(st[:, 348:352], st[:, 348:352]))
            link(V.tensor_tensor(st[:, 348:352], st[:, 336:340], st[:, 348:352], ALU.mult))
            link(V.tensor_scalar(st[:, 344:348], st[:, 348:352], -0.5, 0.5, ALU.mult, ALU.add))
            link(V.tensor_tensor(st[:, 348:352], st[:, 348:352], st[:, 344:348], ALU.add))
            f_a, f_b = st[:, 344:348], st[:, 348:352]

            job_done("modB3", 1)
            mod_cols(0, 0, 16, 0)
            dve.wait_ge(x_in, 32)
            norm(0, BOTH, cat, 8, vcols[:, 96:104])
            mod_chunk()
            dve.wait_ge(even_in, 64)
            for i in BOTH:
                job_done("even_k", i + 1)
                link(V.tensor_tensor(qk_t1, qk_raw[:, i, :], qk_raw[:, i, :], ALU.mult))
                ins = V.tensor_reduce(st[:, 80 + 10 * i:90 + 10 * i], qk_t1.rearrange("p (h d) -> p h d", h=10),
                                      axis=AXX, op=ALU.add)
                if i < 3:
                    link(ins)
                else:
                    ins.then_inc(qk_ss, 1)
            dve.wait_ge(qk_rs, 1)
            for i in BOTH:
                raw = qk_raw[:, i, :].rearrange("p (h d) -> p h d", h=10)
                t0 = qk_t0.rearrange("p (h d) -> p h d", h=10)
                link(V.tensor_tensor(t0, raw, rep(st[:, 120 + 10 * i:130 + 10 * i], 2, [P, 10, HD]), ALU.mult))
                qp = qk_p[i][:, 0:512].rearrange("p (j v d) -> p v j d", j=4, v=2)
                kp = qk_p[i][:, 512:640].rearrange("p (v d) -> p v d", v=2)
                q0 = t0[:, 0:8, :].rearrange("p (v j) d -> p v j d", v=2)
                if i in CTX:
                    for v in range(2):
                        V.tensor_tensor(qp[:, v], q0[:, v], rep(erow[:, 0:HD], 1, [P, 4, HD]), ALU.mult)
                    V.tensor_tensor(kp, t0[:, 8:10, :], rep(erow[:, HD:2 * HD], 1, [P, 2, HD]),
                                    ALU.mult).then_inc(qk_ready, 1)
                    dve.wait_ge(qk_ready, i + 1)
                    continue
                V.tensor_tensor(t0[:, 0:8, :], t0[:, 0:8, :], rep(erow[:, 0:HD], 1, [P, 8, HD]), ALU.mult)
                link(V.tensor_tensor(t0[:, 8:10, :], t0[:, 8:10, :], rep(erow[:, HD:2 * HD], 1, [P, 2, HD]), ALU.mult))
                halves = qk_t0.rearrange("p (n d) -> p n d", d=32)
                t1h, t2h = qk_t1.rearrange("p (n d) -> p n d", d=32), qk_raw[:, i, :].rearrange("p (n d) -> p n d", d=32)
                rope = const("rope").rearrange("p (t f) -> p t f", t=2)[:, i - 2, :]
                V.tensor_tensor(t1h, halves, rep(rope[:, 0:32], 1, [P, 20, 32]), ALU.mult)
                link(V.tensor_tensor(t2h, halves, rep(rope[:, 32:64], 1, [P, 20, 32]), ALU.mult))
                c4 = qk_t1.rearrange("p (h g d) -> p h g d", g=2, d=32)
                s4 = qk_raw[:, i, :].rearrange("p (h g d) -> p h g d", g=2, d=32)
                for v in range(2):
                    hs = slice(4 * v, 4 * v + 4)
                    V.tensor_tensor(qp[:, v, :, 0:32], c4[:, hs, 0, :], s4[:, hs, 1, :], ALU.subtract)
                    V.tensor_tensor(qp[:, v, :, 32:64], c4[:, hs, 1, :], s4[:, hs, 0, :], ALU.add)
                V.tensor_tensor(kp[:, :, 0:32], c4[:, 8:10, 0, :], s4[:, 8:10, 1, :], ALU.subtract)
                V.tensor_tensor(kp[:, :, 32:64], c4[:, 8:10, 1, :], s4[:, 8:10, 0, :], ALU.add).then_inc(qk_ready, 1)
                dve.wait_ge(qk_ready, i + 1)
            for _ in MOD_AFTER_JOB["even"][1:]:
                mod_chunk()
            win = const("win").rearrange("p (t k) -> p t k", t=2)
            attention(0, 32, lambda u: 2 if u < 16 else 4,
                      lambda u: win[:, 0, 0:256] if u < 16 else win[:, (u - 16) // 8, :],
                      lambda u: erow[:, 256 + u % 8:257 + u % 8], [eS[:, j, :] for j in range(2)],
                      lambda u: cat[:, u // 8, HD * (u % 8):HD * (u % 8) + HD])
            dve.wait_ge(att_d, 32)
            for d in range(2):
                V.memset(h_sc[d], 0.0)
                V.memset(h_S[d], 0.0)
            V.memset(st[:, 352:368], 0.0)
            for d in range(2):
                ins = V.tensor_copy(dg[:, d, :].rearrange("p (n t) -> p n t", t=64),
                                    rep(const("scan")[:, 64 * d:64 * d + 64], 1, [P, 8, 64]))
            link(ins)
            def halves(v):
                return v.rearrange("p (n g t) -> p n g t", g=2, t=32)

            def forget_gates(h):
                for d in range(2):
                    f = hf[d][:, h, :]
                    job_done("even_bf", HG * d + h + 1)
                    V.tensor_scalar(f, f, f_a[:, h:h + 1], f_b[:, h:h + 1], ALU.mult, ALU.add).then_inc(hg_f, 1)

            def running_sums(h, d):
                w, e, cum_ = 2 * h + d, e_set[d], h_cum[d]
                dve.wait_ge(hg_f, w + 1)
                if h:
                    dve.wait_ge(hg_prod, w - 1)
                V.tensor_scalar(h_kk[d], hf[d][:, h, :], -1.0, 1.0, ALU.mult, ALU.add)
                dve.wait_ge(hg_lf, w + 1)
                if d == 0:
                    link(V.tensor_tensor_scan(cum_, dg[:, 0, :], e[1], 0.0, ALU.mult, ALU.add))
                else:
                    link(V.tensor_tensor_scan(cum_[:, ::-1], dg[:, 1, ::-1], e[1][:, ::-1], 0.0, ALU.mult, ALU.add))
                cum = cum_.rearrange("p (n t) -> p n t", t=64)
                ref, last = (32, 63) if d == 0 else (31, 0)
                V.tensor_tensor(e[0].rearrange("p (n t) -> p n t", t=64), cum,
                                cum[:, :, ref:ref + 1].to_broadcast([P, 8, 64]), ALU.subtract)
                V.tensor_tensor(e[3].rearrange("p (n t) -> p n t", t=64),
                                cum[:, :, last:last + 1].to_broadcast([P, 8, 64]), cum, ALU.subtract).then_inc(hg_cum, 1)

            def scaled(h, d):
                w, e, kk, q = 2 * h + d, e_set[d], h_kk[d], e_q[h % 2][d]
                dve.wait_ge(hg_e, w + 1)
                V.tensor_copy(st[:, 352 + 8 * d:360 + 8 * d], q.rearrange("p (n t) -> p n t", t=64)[:, :, (63, 0)[d]])
                V.tensor_tensor(e[3], e[3], kk, ALU.mult)
                V.tensor_tensor(e[0], e[0], hq[:, h, :], ALU.mult)
                V.memset(halves(h_kz[d])[:, :, 1 - d, :], 0.0)
                link(V.tensor_tensor(halves(h_kz[d])[:, :, d, :], halves(e[1])[:, :, d, :], halves(kk)[:, :, d, :],
                                     ALU.mult))
                V.tensor_tensor(e[1], e[1], kk, ALU.mult)
                V.tensor_tensor(q, q, hq[:, h, :], ALU.mult).then_inc(hg_prod, 1)

            def masked_scores(h, d):
                if h:
                    dve.wait_ge(acc_full, pre.job[f"hg_o{h - 1}"] + 1)
                dve.wait_ge(hg_s, 2 * h + d + 1)
                V.copy_predicated(h_sc[d], rep(bconst[:, P * d:P * (d + 1)], 1, [P, 4, P]),
                                  mx[:, 1, :].rearrange("p (t k) -> p t k", t=4)).then_inc(hg_ss, 1)

            def states(h, d):
                w, decay = 2 * h + d, st[:, 352 + 8 * d:360 + 8 * d]
                dve.wait_ge(hg_u, w + 1)
                order = list(range(8)) if d == 0 else [3, 2, 1, 0, 7, 6, 5, 4]
                for n in range(7):
                    c, nxt = order[n], order[n + 1]
                    u_ps = mx[:, 2 + c % 2, P * (c // 2):P * (c // 2 + 1)]
                    if n == 0:
                        ins = V.tensor_copy(h_S[d][:, nxt, :], u_ps)
                    else:
                        ins = V.scalar_tensor_tensor(h_S[d][:, nxt, :], h_S[d][:, c, :], decay[:, c:c + 1], u_ps,
                                                     ALU.mult, ALU.add)
                    if n < 6:
                        link(ins)
                ins.then_inc(hg_st, 1)
                dve.wait_ge(hg_st, w + 1)

            def squares(h):
                o = cat[:, :, 512 + P * h:512 + P * (h + 1)]
                job_done(f"hg_o{h}", 1)
                o_sq_ = o_sq.rearrange("p (t e) -> p t e", t=4)
                link(V.tensor_tensor(o_sq_, o, o, ALU.mult))
                V.tensor_reduce(st[:, 368 + 4 * h:372 + 4 * h], o_sq_, axis=AXX, op=ALU.add).then_inc(hg_osq, 1)

            def normed(h):
                o = cat[:, :, 512 + P * h:512 + P * (h + 1)]
                dve.wait_ge(hg_ors, h + 1)
                link(V.tensor_tensor(o, o, rep(st[:, 384 + 4 * h:388 + 4 * h], 2, [P, 4, P]), ALU.mult))
                link(V.tensor_tensor(o, o, rep(erow[:, 128:256], 1, [P, 4, P]), ALU.mult))
                return V.tensor_tensor(o, o, hg_[:, :, P * h:P * (h + 1)], ALU.mult)

            forget_gates(0)
            for d in range(2):
                running_sums(0, d)
            for h in range(HG):
                for d in range(2):
                    scaled(h, d)
                if h:
                    squares(h - 1)
                if h + 1 < HG:
                    forget_gates(h + 1)
                for d in range(2):
                    masked_scores(h, d)
                    if h + 1 < HG:
                        running_sums(h + 1, d)
                    states(h, d)
                    if h and d == 0:
                        normed(h - 1)
            squares(HG - 1)
            normed(HG - 1).then_inc(cat_ready, 1)
            job_done("mod11", 1)
            mod_cols(0, 16, 32, 0)
            gates("gate0", (1, 0), 16)
            residual("even_out", BOTH, "gate0", 4)

            def feed_forward(use, n_tok, ffT, conv=None):
                for t in range(11):
                    if conv is None and use == 0:
                        mod_chunk()
                        mod_chunk()
                    for j in range(2):
                        b = 2 * t + j
                        if conv is not None:
                            job_done("up", 4 * t + j + 1)
                            since(dve, ff_silu, conv * KF, b - 1)
                            tap = [pcols[:, P + KF * k + b:P + KF * k + b + 1] for k in range(4)]
                            link(V.tensor_scalar(c_buf[:, j, :], conv_in[:, j, 1:257], tap[0], tap[3], ALU.mult, ALU.add))
                            link(V.scalar_tensor_tensor(c_buf[:, j, :], conv_in[:, j, 2:258], tap[1], c_buf[:, j, :],
                                                        ALU.mult, ALU.add))
                            V.scalar_tensor_tensor(c_buf[:, j, :], conv_in[:, j, 3:259], tap[2], c_buf[:, j, :],
                                                   ALU.mult, ALU.add).then_inc(ff_conv, 1)
                    for j in range(2):
                        b = 2 * t + j
                        if conv is not None:
                            dve.wait_ge(ff_silu, conv * KF + b + 1)
                            job_done("up", 4 * t + j + 3)
                        else:
                            job_done(f"ffn{use}", 4 * t + j + 3)
                        V.tensor_tensor(ffT[:, b, :], g_buf[:, j, 0:n_tok], u_buf[:, j, 0:n_tok],
                                        ALU.mult).then_inc(ff_mul, 1)

            dve.wait_ge(y_used, 8)
            norm(1, BOTH, f_xs4, 32, vcols[:, 104:112])
            feed_forward(0, 512, ffT4)
            gates("gate1", (1, 0), 40)
            residual("down0", BOTH, "gate1", 4)
            job_done("mod23", 1)
            mod_cols(1, 0, 48, 48)
            dve.wait_ge(y_used, 16)
            norm(2, BOTH, r_xs, 8, vcols[:, 112:120])
            rr = const("ret_rope")
            cos, sin = rep(rr[:, 0:256], 1, [P, 2, 256]), rep(rr[:, 256:512], 1, [P, 2, 256])
            rt_c, rt_s = r_t[:, 0], r_t[:, 1]
            for _ in MOD_AFTER_JOB["odd"][:8]:
                mod_chunk()
            for h in range(RET):
                for last, v in enumerate((rq[:, 2 * h:2 * h + 2, :], rk[:, 2 * h:2 * h + 2, 256:512])):
                    job_done("ret_k", 2 * h + 2)
                    V.tensor_tensor(rt_c, v, cos, ALU.mult)
                    link(V.tensor_tensor(rt_s, v, sin, ALU.mult))
                    V.tensor_tensor(v[:, 0, :], rt_c[:, 0, :], rt_s[:, 1, :], ALU.subtract)
                    ins = V.tensor_tensor(v[:, 1, :], rt_c[:, 1, :], rt_s[:, 0, :], ALU.add)
                    if not last:
                        link(ins)
                ins.then_inc(ret_rope, 1)
                dve.wait_ge(ret_rope, h + 1)
            for _ in MOD_AFTER_JOB["odd"][8:]:
                mod_chunk()
            job_done("ret_g", 8)
            for h in range(RET):
                dve.wait_ge(dtab_in[h % 2], 16 * (h // 2 + 1))
                if h >= 2:
                    dve.wait_ge(ret_o, 2 * (h - 1))
                for s2 in range(2):
                    dve.wait_ge(ret_s, 2 * h + s2 + 1)
                    V.tensor_tensor(r_P[:, h % 2, 2 * s2:2 * s2 + 2, :], mx[:, s2, :].rearrange("p (s t) -> p s t", s=2),
                                    r_D[:, h % 2, 2 * s2:2 * s2 + 2, :], ALU.mult).then_inc(ret_p, 1)
                for t in range(2):
                    n = 2 * h + t
                    dve.wait_ge(ret_rs, n + 1)
                    g = rg[:, t, 512 * h:512 * (h + 1)]
                    V.scalar_tensor_tensor(g, mx[:, 2 + t, :], st[:, 408 + n:409 + n], g,
                                           ALU.mult, ALU.mult).then_inc(ret_n, 1)
            gates("gate2", (0,), 16)
            residual("ret_out", LAT, "gate2", 2)
            dve.wait_ge(y_used, 20)
            norm(3, LAT, f_xs2, 32, vcols[:, 120:128])
            feed_forward(1, 256, ffT2)
            gates("gate3", (0,), 40)
            residual("down1", LAT, "gate3", 2)
            job_done("mod47", 1)
            link(V.memset(conv_in[:, :, 0:3], 0.0))

            with dve.Fori(0, DEPTH2) as l:
                loop[0] = l
                chain.enter(l, DVE_LINKS)
                uses.enter(0)
                link(V.tensor_tensor(mb[:, 0, :], modc[:, bass.ds(l + 2, 1), 0, :].rearrange("p o n -> p (o n)"),
                                     vcols[:, bass.ds(l * 48 + 128, 48)], ALU.add))
                job_done("param", 2)
                dve.wait_ge(y_used, l * Y_USES + 24)
                norm(l * 2 + 4, LAT, d_xs, 8, pcols[:, 96:104])
                dve.wait_ge(lbc_in, l * 96 + 96)
                for i in range(2):
                    job_done("swa_k", i + 1)
                    link(V.tensor_tensor(s_t1, sqk[:, i, :], sqk[:, i, :], ALU.mult))
                    ins = V.tensor_reduce(st[:, 80 + 18 * i:98 + 18 * i], s_t1.rearrange("p (h d) -> p h d", h=18),
                                          axis=AXX, op=ALU.add)
                    if i == 0:
                        link(ins)
                    else:
                        ins.then_inc(qk_ss, 1)
                def query_keys(i):
                    dve.wait_ge(rope_ready, 1)
                    dve.wait_ge(qk_rs, l + 2)
                    raw = sqk[:, i, :].rearrange("p (h d) -> p h d", h=18)
                    link(V.tensor_tensor(raw, raw, rep(st[:, 120 + 18 * i:138 + 18 * i], 2, [P, 18, HD]), ALU.mult))
                    V.tensor_tensor(raw[:, 0:16, :], raw[:, 0:16, :], rep(brow[:, 16:80], 1, [P, 16, HD]), ALU.mult)
                    link(V.tensor_tensor(raw[:, 16:18, :], raw[:, 16:18, :], rep(brow[:, 80:144], 1, [P, 2, HD]), ALU.mult))
                    r1 = raw[:, :, 0:16].rearrange("p h (g f) -> p h g f", g=2)
                    c1 = s_t0[:, 0:288].rearrange("p (h g f) -> p h g f", h=18, g=2)
                    c2 = s_t1[:, 0:288].rearrange("p (h g f) -> p h g f", h=18, g=2)
                    for g in range(2):
                        V.tensor_tensor(c1[:, :, g, :], r1[:, :, g, :], rep(srope[:, i, 0:8], 1, [P, 18, 8]), ALU.mult)
                        ins = V.tensor_tensor(c2[:, :, g, :], r1[:, :, g, :], rep(srope[:, i, 8:16], 1, [P, 18, 8]), ALU.mult)
                    link(ins)
                    V.tensor_tensor(r1[:, :, 0, :], c1[:, :, 0, :], c2[:, :, 1, :], ALU.subtract)
                    link(V.tensor_tensor(r1[:, :, 1, :], c1[:, :, 1, :], c2[:, :, 0, :], ALU.add))
                    sp_ = s_p[:, i, 0:1024].rearrange("p (j v d) -> p v j d", j=8, v=2)
                    for v in range(2):
                        V.tensor_copy(sp_[:, v], raw[:, 8 * v:8 * v + 8, :])
                    V.tensor_copy(s_p[:, i, 1024:1152], sqk[:, i, 1024:1152]).then_inc(qk_ready, 1)

                for b in range(24):
                    job_done("dn_in", b + 1)
                    tap = [pcols[:, 24 * k + b:24 * k + b + 1] for k in range(4)]
                    o, src = dnf[:, b, :], conv_in[:, b % 2, :]
                    link(V.tensor_scalar(o, src[:, 0:256], tap[0], None, ALU.mult))
                    link(V.scalar_tensor_tensor(o, src[:, 1:257], tap[1], o, ALU.mult, ALU.add))
                    link(V.scalar_tensor_tensor(o, src[:, 2:258], tap[2], o, ALU.mult, ALU.add))
                    V.scalar_tensor_tensor(o, src[:, 3:259], tap[3], o, ALU.mult, ALU.add).then_inc(dc_conv, 1)
                    if b in (3, 9):
                        query_keys((b - 3) // 6)
                swa = const("swa")
                attention(l * 32 + 32, 32, lambda u: 1 if u < 16 else 2,
                          lambda u: swa[:, 128:256] if u < 16 else swa,
                          lambda u: brow[:, 144 + u % 16:145 + u % 16], [sS[:, j, :] for j in range(2)],
                          lambda u: oswa[:, u // 16, HD * (u % 16):HD * (u % 16) + HD])

                for s in range(9):
                    if s < 8:
                        f = dnf[:, 2 * s:2 * s + 2, :]
                        dve.wait_ge(dc_silu, l * 24 + 2 * s + 2)
                        since(dve, l2_ps, l * 8, s - 1)
                        V.tensor_tensor(l2_sq[:, s % 2, :].rearrange("p (b t) -> p b t", b=2), f, f,
                                        ALU.mult).then_inc(l2_sqd, 1)
                    if s >= 1:
                        o = s - 1
                        f = dnf[:, 2 * o:2 * o + 2, :]
                        dve.wait_ge(l2_rsd, l * 8 + o + 1)
                        V.scalar_tensor_tensor(f, f, P ** -0.5 if o < 4 else 1.0,
                                               l2_rs[:, o % 2, :].rearrange("p (b t) -> p b t", b=2),
                                               ALU.mult, ALU.mult).then_inc(l2_done, 1)
                job_done("dn_ab", 2)
                two = [P, 2, 8]

                def s3(lo):
                    return st[:, lo:lo + 16].rearrange("p (t h) -> p t h", t=2)

                link(V.tensor_tensor(s3(248), dab[:, :, 0:8], rep(brow[:, 0:8], 1, two), ALU.add))
                link(V.tensor_scalar(s3(312), s3(248), -1.0, None, ALU.mult))
                V.tensor_tensor(s3(264), s3(248), s3(312), ALU.max).then_inc(gb_x, 1)
                dve.wait_ge(gb_e, l + 1)
                link(V.scalar_tensor_tensor(s3(248), s3(248), 0.0, s3(280), ALU.max, ALU.add))
                V.tensor_scalar(s3(216), s3(216), 1.0, None, ALU.add)
                link(V.scalar_tensor_tensor(s3(248), s3(248), -1.0, rep(st[:, 296:304], 1, two), ALU.mult, ALU.mult))
                V.tensor_copy(st[:, 64:80], st[:, 248:264]).then_inc(gc_in, 1)
                link(V.reciprocal(st[:, 216:232], st[:, 216:232]))
                dve.wait_ge(gc_in, l + 1)
                link(V.tensor_scalar(st[:, 232:248], st[:, 216:232], -1.0, None, ALU.mult))
                dve.wait_ge(gc_ps, l + 1)
                link(V.tensor_copy(st[:, 160:184], mx[:, 2, 0:24]))
                V.tensor_tensor(st[:, 208:216], st[:, 176:184], st[:, 160:168], ALU.subtract).then_inc(gc_sb, 1)
                dve.wait_ge(gc_e, l + 1)
                link(V.tensor_tensor(st[:, 304:312], st[:, 224:232], st[:, 192:200], ALU.mult))
                four = [P, 4, P]
                for hg in range(2):
                    for c in range(2):
                        g = 2 * hg + c
                        at = 8 * c + 4 * hg
                        gcol, beta = st[:, 160 + at:164 + at], st[:, 216 + at:220 + at]
                        V.tensor_tensor(t_in, rep(tri, 1, four), rep(st[:, 64 + at:68 + at], 2, four),
                                        ALU.mult).then_inc(tg_in, 1)
                        dve.wait_ge(tg_ps, l * 4 + g + 1)
                        later = mx[:, 3, :].rearrange("p (h t) -> p h t", h=4)
                        V.tensor_tensor(t_g, later, rep(const("incl"), 1, four), ALU.add)
                        for h in range(4):
                            ins = V.scalar_tensor_tensor(t_st[:, h, :], mx[:, 3, P * h:P * (h + 1)], -1.0, const("strict"),
                                                         ALU.mult, ALU.add)
                        link(ins)
                        V.tensor_tensor(t_g, t_g, rep(gcol, 2, four), ALU.subtract)
                        V.tensor_tensor(t_st, t_st, rep(gcol, 2, four), ALU.add).then_inc(dec_in, 1)
                        V.tensor_copy(dT[c], rep(ident, 1, four))
                        V.tensor_copy(dTT[c], rep(ident, 1, four))
                        dve.wait_ge(dec_e, l * 4 + g + 1)
                        dve.wait_ge(kq_ps, l * 4 + g + 1)
                        V.tensor_tensor(dQ[c], mx[:, 1, :].rearrange("p (h t) -> p h t", h=4), t_g, ALU.mult)
                        if c == 1:
                            V.tensor_tensor(qdec, qdec, dnf[:, 4 * hg:4 * hg + 4, P:2 * P], ALU.mult)
                        link(V.tensor_tensor(t_st, mx[:, 0, :].rearrange("p (h t) -> p h t", h=4), t_st, ALU.mult))
                        V.tensor_tensor(dL[c], t_st, rep(st[:, 232 + at:236 + at], 2, four), ALU.mult).then_inc(l_ready, 1)
                        by_tok = mx[:, 2, :].rearrange("p (h t) -> p h t", h=4)
                        dve.wait_ge(kv_ps, l * 8 + 2 * g + 1)
                        V.tensor_tensor(vb[c], by_tok, rep(beta, 2, four), ALU.mult).then_inc(kv_sb, 1)
                        dve.wait_ge(kv_ps, l * 8 + 2 * g + 2)
                        if c == 0:
                            V.tensor_tensor(kdec, by_tok, rep(st[:, 200 + 4 * hg:204 + 4 * hg], 2, four),
                                            ALU.mult).then_inc(kv_sb, 1)
                        else:
                            V.tensor_tensor(kbe, by_tok, rep(st[:, 304 + 4 * hg:308 + 4 * hg], 2, four),
                                            ALU.mult).then_inc(kv_sb, 1)
                    for level in range(7):
                        n = (hg * 7 + level) * 2
                        fill = bconst[:, 256 + 256 * level:512 + 256 * level]
                        for c in range(2):
                            at = 480 + 2 * level + c
                            dve.wait_ge(inv_t, l * 28 + n + c + 1)
                            V.memset(st[:, at:at + 1], 0.0)
                            if level < 6:
                                V.copy_predicated(dT[c], rep(fill[:, 0:P], 1, four),
                                                  mx[:, 2 + c, :].rearrange("p (h t) -> p h t", h=4))
                            V.copy_predicated(dTT[c], rep(fill[:, P:2 * P], 1, four),
                                              mx[:, c, :].rearrange("p (h t) -> p h t", h=4)).then_inc(inv_d, 1)
                    dve.wait_ge(dz_ready, l + 1)
                    for c in range(2):
                        n = 448 + 8 * hg + 4 * c
                        dve.wait_ge(dn_rs, l * 4 + 2 * hg + c + 1)
                        since(dve, dn_o, l * 4, 2 * hg + c)
                        link(V.tensor_tensor(o_t, mx[:, c, :].rearrange("p (h e) -> p h e", h=4), rep(st[:, n:n + 4], 2, four),
                                             ALU.mult))
                        link(V.tensor_tensor(o_t, o_t, rep(brow[:, 160:288], 1, four), ALU.mult))
                        z = dz[:, c, 512 * hg:512 * hg + 512].rearrange("p (h e) -> p h e", h=4)
                        V.tensor_tensor(z, z, o_t, ALU.mult).then_inc(dn_o, 1)
                dve.wait_ge(mix_ready, l + 1)
                for s in (sgb, sga):
                    ins = V.tensor_scalar(s, s, 0.5, 0.5, ALU.mult, ALU.add)
                link(ins)
                job_done("swa_out", 4)
                link(V.tensor_tensor(yb, yb, sgb, ALU.mult))
                for n in range(4):
                    h, t = n // 2, n % 2
                    u = uses.next()
                    job_done("dn_out", n + 1)
                    cols = slice(512 * h, 512 * h + 512)
                    link(V.tensor_tensor(ybuf[:, u % 2, :], ybuf[:, u % 2, :], sga[:, t, cols], ALU.mult))
                    V.tensor_tensor(yb[:, t, cols], yb[:, t, cols], ybuf[:, u % 2, :], ALU.add).then_inc(y_used, 1)
                gates("gate_mix", (0,), 16)
                residual("w_o", LAT, "gate_mix", 2)
                dve.wait_ge(y_used, l * Y_USES + 32)
                norm(l * 2 + 5, LAT, f_xs2, 32, pcols[:, 104:112])
                feed_forward(l + 2, 256, ffT2, conv=l)
                gates("gate_ffn", (0,), 40)
                residual("down", LAT, "gate_ffn", 2)
                chain.leave("VectorE")


_INS = [
    "x", "c", "ctx", "c_ctx", "mod_w", "mod_b", "norm_g", "ffn_w_in", "ffn_w_out", "even_w_in", "even_w_out",
    "attn_qk_norm_g", "attn_sink", "hgrn_out_norm_g", "hgrn_lb", "odd_w_in", "odd_w_out", "c_2", "positions_2",
    "w_ada_2", "b_ada_2", "norm_mix_2", "w_in_2", "dn_conv_2", "dn_a_log_2", "dn_dt_bias_2", "dn_norm_2",
    "w_dn_out_2", "swa_q_norm_2", "swa_k_norm_2", "swa_sinks_2", "w_swa_out_2", "w_o_2", "norm_ffn_2", "w_up_2",
    "ffn_conv_2", "ffn_conv_b_2", "w_down_2",
]


def kernel(**inputs):
    import concourse.bacc as bacc
    from concourse.bass_utils import run_bass_kernel_spmd

    nc = bacc.Bacc("TRN2", target_bir_lowering=False, num_devices=1)
    arrays = {name: np.ascontiguousarray(inputs[name]) for name in _INS}
    arrays["const_f"], arrays["const_b"], arrays["const_ret"] = shape_constants()
    aps = {n: nc.dram_tensor("in_" + n, v.shape, mybir.dt.from_np(v.dtype), kind="ExternalInput").ap() for n, v in arrays.items()}
    out = nc.dram_tensor("out", arrays["x"].shape, F32, kind="ExternalOutput").ap()
    first_then_second_block(nc, aps, out)
    return run_bass_kernel_spmd(nc, [{"in_" + n: v for n, v in arrays.items()}], core_ids=[0]).results[0]["out"]
```
